# Optimizing a Trainium2 kernel written in Bass

```python
import jax
import jax.numpy as jnp
from jax import lax
import numpy as np
import math
import jax, jax.numpy as jnp

D_MODEL = 1024
BATCH = 1
SEQ = 512
DEPTH = 1

NSA_HEADS = 8
NSA_KV_GROUPS = 2
NSA_HEAD_DIM = 64
CMP_LEN = 32
CMP_STRIDE = 16
CMP_HIDDEN = 128
SLC_LEN = 64
N_SELECT = 16
WINDOW = 512
Q_BLOCK = 128
FORCE_SCORE = 1e4
HGRN_HEADS = 4
HGRN_KEY_DIM = 128
HGRN_VAL_DIM = 128
HGRN_CHUNK = 64
D_FF = -(-8 * D_MODEL // (3 * 256)) * 256
RMS_EPS = 1e-6

NSA_WIDTH = NSA_HEADS * NSA_HEAD_DIM
NSA_KV_WIDTH = NSA_KV_GROUPS * NSA_HEAD_DIM
HGRN_KEY_WIDTH = HGRN_HEADS * HGRN_KEY_DIM
HGRN_VAL_WIDTH = HGRN_HEADS * HGRN_VAL_DIM
MIX_WIDTH = NSA_WIDTH + HGRN_VAL_WIDTH
IN_SIZES = (NSA_WIDTH,) + (NSA_KV_WIDTH,) * 6 + (3 * NSA_HEADS, HGRN_KEY_WIDTH, HGRN_KEY_WIDTH, HGRN_VAL_WIDTH, HGRN_VAL_WIDTH)
IN_WIDTH = sum(IN_SIZES)


def rms_norm(x, g):
    xf = x.astype(jnp.float32)
    y = xf * lax.rsqrt(jnp.mean(xf * xf, axis=-1, keepdims=True) + RMS_EPS)
    return (y * g.astype(jnp.float32)).astype(x.dtype)

def masked_softmax(s, mask):
    s = jnp.where(mask, s.astype(jnp.float32), -1e30)
    p = jax.nn.softmax(s, axis=-1)
    return jnp.where(mask, p, 0.0)

def compress(seq, pos, w1, w2):
    B, T, G, dh = seq.shape
    ratio = CMP_LEN // CMP_STRIDE
    nseg = T // CMP_STRIDE
    ncmp = nseg - ratio + 1
    seg = seq.reshape(B, nseg, CMP_STRIDE, G, dh)
    blocks = jnp.concatenate([seg[:, r:r + ncmp] for r in range(ratio)], axis=2)
    blocks = blocks + pos[None, None, :, None, :]
    flat = blocks.transpose(0, 1, 3, 2, 4).reshape(B, ncmp, G, CMP_LEN * dh)
    return jax.nn.gelu(flat @ w1) @ w2

def nsa_mixer(q, kc, vc, ks, vs, kw, vw, gates):
    B, T, H, dh = q.shape
    G = NSA_KV_GROUPS
    R = H // G
    ncmp = kc.shape[1]
    nslc = T // SLC_LEN
    n_sel = min(N_SELECT, nslc)
    scale = dh ** -0.5
    cmp_start = jnp.arange(ncmp) * CMP_STRIDE
    cmp_end = cmp_start + CMP_LEN - 1
    slc_start = jnp.arange(nslc) * SLC_LEN
    overlap = ((cmp_start[:, None] < slc_start[None, :] + SLC_LEN)
               & (cmp_start[:, None] + CMP_LEN > slc_start[None, :])).astype(jnp.float32)
    ks_blk = ks.reshape(B, nslc, SLC_LEN, G, dh).transpose(0, 3, 1, 2, 4)
    vs_blk = vs.reshape(B, nslc, SLC_LEN, G, dh).transpose(0, 3, 1, 2, 4)
    pad = ((0, 0), (WINDOW, 0), (0, 0), (0, 0))
    kw_pad = jnp.pad(kw, pad)
    vw_pad = jnp.pad(vw, pad)
    bi = jnp.arange(B)[:, None, None, None]
    gi = jnp.arange(G)[None, :, None, None]
    j = jnp.arange(nslc)

    def block(qb):
        s = qb * Q_BLOCK
        t = s + jnp.arange(Q_BLOCK)
        qblk = lax.dynamic_slice_in_dim(q, s, Q_BLOCK, 1).reshape(B, Q_BLOCK, G, R, dh)
        sc = jnp.einsum('bqgrd,bngd->bgrqn', qblk, kc) * scale
        p_cmp = masked_softmax(sc, cmp_end[None, :] <= t[:, None])
        o_cmp = jnp.einsum('bgrqn,bngd->bqgrd', p_cmp, vc.astype(jnp.float32))
        imp = jnp.einsum('bgrqn,nj->bgqj', p_cmp, overlap)
        jcur = t // SLC_LEN
        forced = (j[None, :] == 0) | (j[None, :] == jcur[:, None]) | (j[None, :] == jcur[:, None] - 1)
        future = j[None, :] > jcur[:, None]
        imp = jnp.where(forced, FORCE_SCORE, jnp.where(future, -1.0, imp))
        _, idx = lax.top_k(imp, n_sel)
        k_sel = ks_blk[bi, gi, idx].reshape(B, G, Q_BLOCK, n_sel * SLC_LEN, dh)
        v_sel = vs_blk[bi, gi, idx].reshape(B, G, Q_BLOCK, n_sel * SLC_LEN, dh)
        pos_sel = (idx[..., None] * SLC_LEN + jnp.arange(SLC_LEN)).reshape(B, G, Q_BLOCK, n_sel * SLC_LEN)
        ss = jnp.einsum('bqgrd,bgqkd->bgrqk', qblk, k_sel) * scale
        p_sel = masked_softmax(ss, (pos_sel <= t[None, None, :, None])[:, :, None])
        o_sel = jnp.einsum('bgrqk,bgqkd->bqgrd', p_sel, v_sel.astype(jnp.float32))
        k_win = lax.dynamic_slice_in_dim(kw_pad, s, WINDOW + Q_BLOCK, 1)
        v_win = lax.dynamic_slice_in_dim(vw_pad, s, WINDOW + Q_BLOCK, 1)
        pos_win = s - WINDOW + jnp.arange(WINDOW + Q_BLOCK)
        diff = t[:, None] - pos_win[None, :]
        win_mask = (diff >= 0) & (diff < WINDOW) & (pos_win[None, :] >= 0)
        sw = jnp.einsum('bqgrd,bkgd->bgrqk', qblk, k_win) * scale
        p_win = masked_softmax(sw, win_mask)
        o_win = jnp.einsum('bgrqk,bkgd->bqgrd', p_win, v_win.astype(jnp.float32))
        g = lax.dynamic_slice_in_dim(gates, s, Q_BLOCK, 1).reshape(B, Q_BLOCK, G, R, 3)
        o = g[..., 0:1] * o_cmp + g[..., 1:2] * o_sel + g[..., 2:3] * o_win
        return o.reshape(B, Q_BLOCK, H * dh)

    out = lax.map(block, jnp.arange(T // Q_BLOCK))
    return out.transpose(1, 0, 2, 3).reshape(B, T, H * dh)

def hgrn2_mixer(hq, hf, hi, hg, lb, o_gain):
    B, T, _ = hq.shape
    H, dk, dv, C = HGRN_HEADS, HGRN_KEY_DIM, HGRN_VAL_DIM, HGRN_CHUNK
    f32 = jnp.float32
    q = jax.nn.silu(hq.astype(f32)).reshape(B, T, H, dk)
    f = lb + (1.0 - lb) * jax.nn.sigmoid(hf.astype(f32))
    logf = jnp.log(f).reshape(B, T, H, dk)
    k = (1.0 - f).reshape(B, T, H, dk)
    v = hi.astype(f32).reshape(B, T, H, dv)
    nc = T // C

    def to_chunks(a):
        return a.reshape(B, nc, C, H, a.shape[-1]).transpose(1, 0, 3, 2, 4)

    causal = jnp.tril(jnp.ones((C, C), dtype=bool))

    def step(S, xs):
        qc, kc, vc, gc = xs
        b = jnp.cumsum(gc, axis=-2)
        b_last = b[:, :, -1:, :]
        o_inter = jnp.einsum('bhcd,bhde->bhce', qc * jnp.exp(b), S)
        decay = jnp.exp(jnp.where(causal[:, :, None], b[:, :, :, None, :] - b[:, :, None, :, :], -jnp.inf))
        attn = jnp.einsum('bhtd,bhsd,bhtsd->bhts', qc, kc, decay)
        o = o_inter + jnp.einsum('bhts,bhse->bhte', attn, vc)
        S = jnp.exp(b_last[:, :, 0, :])[..., None] * S + jnp.einsum('bhsd,bhse->bhde', kc * jnp.exp(b_last - b), vc)
        return S, o

    S0 = jnp.zeros((B, H, dk, dv), f32)
    _, o = lax.scan(step, S0, (to_chunks(q), to_chunks(k), to_chunks(v), to_chunks(logf)))
    o = o.transpose(1, 0, 3, 2, 4).reshape(B, T, H, dv)
    o = rms_norm(o, o_gain) * jax.nn.silu(hg.astype(f32)).reshape(B, T, H, dv)
    return o.reshape(B, T, H * dv)

def first_inputs(seed: int = 0) -> dict:
    key = jax.random.key(seed)
    k = jax.random.split(key, 17)
    f32 = jnp.float32
    dh = NSA_HEAD_DIM

    def nrm(kk, shape, scale):
        return jax.random.normal(kk, shape, f32) * scale

    return {
        'x': nrm(k[0], (BATCH, SEQ, D_MODEL), 1.0),
        'norm_mix': 1.0 + nrm(k[1], (DEPTH, D_MODEL), 0.02),
        'w_in': nrm(k[2], (DEPTH, D_MODEL, IN_WIDTH), D_MODEL ** -0.5),
        'q_norm': 1.0 + nrm(k[3], (DEPTH, dh), 0.02),
        'k_norm': 1.0 + nrm(k[4], (DEPTH, 3, dh), 0.02),
        'cmp_pos_k': nrm(k[5], (DEPTH, CMP_LEN, dh), 0.5),
        'cmp_pos_v': nrm(k[6], (DEPTH, CMP_LEN, dh), 0.5),
        'cmp_k_w1': nrm(k[7], (DEPTH, CMP_LEN * dh, CMP_HIDDEN), (CMP_LEN * dh) ** -0.5),
        'cmp_k_w2': nrm(k[8], (DEPTH, CMP_HIDDEN, dh), CMP_HIDDEN ** -0.5),
        'cmp_v_w1': nrm(k[9], (DEPTH, CMP_LEN * dh, CMP_HIDDEN), (CMP_LEN * dh) ** -0.5),
        'cmp_v_w2': nrm(k[10], (DEPTH, CMP_HIDDEN, dh), CMP_HIDDEN ** -0.5),
        'hgrn_lb_logits': nrm(k[11], (DEPTH + 1, HGRN_KEY_WIDTH), 0.5),
        'hgrn_o_norm': 1.0 + nrm(k[12], (DEPTH, HGRN_VAL_DIM), 0.02),
        'w_out': nrm(k[13], (DEPTH, MIX_WIDTH, D_MODEL), MIX_WIDTH ** -0.5),
        'norm_ffn': 1.0 + nrm(k[14], (DEPTH, D_MODEL), 0.02),
        'w_gate_up': nrm(k[15], (DEPTH, D_MODEL, 2 * D_FF), D_MODEL ** -0.5),
        'w_down': nrm(k[16], (DEPTH, D_FF, D_MODEL), D_FF ** -0.5),
    }

def first_block(x, norm_mix, w_in, q_norm, k_norm, cmp_pos_k, cmp_pos_v, cmp_k_w1, cmp_k_w2, cmp_v_w1, cmp_v_w2,
              hgrn_lb_logits, hgrn_o_norm, w_out, norm_ffn, w_gate_up, w_down):
    B, T, _ = x.shape
    H, G, dh = NSA_HEADS, NSA_KV_GROUPS, NSA_HEAD_DIM
    split_points = [int(v) for v in np.cumsum(IN_SIZES)[:-1]]
    lower_bounds = jnp.cumsum(jax.nn.softmax(hgrn_lb_logits.astype(jnp.float32), axis=0), axis=0)
    for l in range(DEPTH):
        h = rms_norm(x, norm_mix[l])
        proj = h @ w_in[l]
        (q, kc_raw, vc_raw, ks, vs, kw, vw, gate_logits, hq, hf, hi, hg) = jnp.split(proj, split_points, axis=-1)
        q = rms_norm(q.reshape(B, T, H, dh), q_norm[l])
        kc = rms_norm(compress(kc_raw.reshape(B, T, G, dh), cmp_pos_k[l], cmp_k_w1[l], cmp_k_w2[l]), k_norm[l, 0])
        vc = compress(vc_raw.reshape(B, T, G, dh), cmp_pos_v[l], cmp_v_w1[l], cmp_v_w2[l])
        ks = rms_norm(ks.reshape(B, T, G, dh), k_norm[l, 1])
        kw = rms_norm(kw.reshape(B, T, G, dh), k_norm[l, 2])
        gates = jax.nn.sigmoid(gate_logits.astype(jnp.float32)).reshape(B, T, H, 3)
        o_nsa = nsa_mixer(q, kc, vc, ks, vs.reshape(B, T, G, dh), kw, vw.reshape(B, T, G, dh), gates)
        o_hgrn = hgrn2_mixer(hq, hf, hi, hg, lower_bounds[l], hgrn_o_norm[l])
        mix = jnp.concatenate([o_nsa.astype(x.dtype), o_hgrn.astype(x.dtype)], axis=-1)
        x = x + mix @ w_out[l]
        h = rms_norm(x, norm_ffn[l])
        gate, up = jnp.split(h @ w_gate_up[l], 2, axis=-1)
        x = x + (jax.nn.silu(gate) * up) @ w_down[l]
    return x


DEPTH_2 = 2

CHUNK = 64
EPS = 1e-6
ROPE_THETA = 10000.0

SB_HEAD_DIM = 64
SB_WIDTH = D_MODEL // 2
SB_HEADS = SB_WIDTH // SB_HEAD_DIM
DF_HEAD_DIM = 64
DF_WIDTH = D_MODEL - SB_WIDTH
DF_HEADS = DF_WIDTH // (2 * DF_HEAD_DIM)
MIX_WIDTH_2 = SB_WIDTH + DF_WIDTH
PROJ_WIDTH = 3 * SB_WIDTH + 3 * DF_WIDTH
D_FF_2 = 4 * D_MODEL


def rmsnorm(x, g):
    xf = x.astype(jnp.float32)
    y = xf * lax.rsqrt(jnp.mean(xf * xf, axis=-1, keepdims=True) + EPS) * g.astype(jnp.float32)
    return y.astype(x.dtype)

def rope(x, pos):
    d = x.shape[-1]
    inv = 1.0 / (ROPE_THETA ** (jnp.arange(0, d, 2, dtype=jnp.float32) / d))
    ang = pos.astype(jnp.float32)[:, None] * inv[None, :]
    ang = jnp.concatenate([ang, ang], axis=-1)
    shape = (1, x.shape[1]) + (1,) * (x.ndim - 3) + (d,)
    cos = jnp.cos(ang).reshape(shape)
    sin = jnp.sin(ang).reshape(shape)
    xf = x.astype(jnp.float32)
    x1, x2 = xf[..., : d // 2], xf[..., d // 2:]
    rot = jnp.concatenate([-x2, x1], axis=-1)
    return (xf * cos + rot * sin).astype(x.dtype)

def stick_breaking_attention(q, k, v):
    B, S, H, d = q.shape
    nb = S // Q_BLOCK
    scale = d ** -0.5
    kh = k.transpose(0, 2, 1, 3)
    vh = v.transpose(0, 2, 1, 3)
    qb = q.transpose(0, 2, 1, 3).reshape(B, H, nb, Q_BLOCK, d).transpose(2, 0, 1, 3, 4)
    kpos = jnp.arange(S)
    qpos = kpos.reshape(nb, Q_BLOCK)

    def block(args):
        qblk, qp = args
        z = jnp.einsum('bhqd,bhkd->bhqk', qblk, kh).astype(jnp.float32) * scale
        strict = kpos[None, :] < qp[:, None]
        log_beta = jax.nn.log_sigmoid(z)
        log_keep = jnp.where(strict, jax.nn.log_sigmoid(-z), 0.0)
        between = lax.cumsum(log_keep, axis=log_keep.ndim - 1, reverse=True) - log_keep
        w = jnp.where(strict, jnp.exp(log_beta + between), 0.0)
        return jnp.einsum('bhqk,bhkd->bhqd', w.astype(vh.dtype), vh)

    out = lax.map(block, (qb, qpos))
    return out.transpose(1, 0, 3, 2, 4).reshape(B, S, H * d)

def differential_attention(q, k, v, lam):
    B, S, H, _, d = q.shape
    dv = v.shape[-1]
    nb = S // Q_BLOCK
    scale = d ** -0.5
    kh = k.transpose(0, 2, 3, 1, 4)
    vh = v.transpose(0, 2, 1, 3)
    qb = q.transpose(0, 2, 3, 1, 4).reshape(B, H, 2, nb, Q_BLOCK, d).transpose(3, 0, 1, 2, 4, 5)
    kchunk = jnp.arange(S) // CHUNK
    qpos = jnp.arange(S).reshape(nb, Q_BLOCK)
    neg = jnp.finfo(jnp.float32).min

    def block(args):
        qblk, qp = args
        s = jnp.einsum('bhmqd,bhmkd->bhmqk', qblk, kh).astype(jnp.float32) * scale
        allowed = kchunk[None, :] <= (qp // CHUNK)[:, None]
        p = jax.nn.softmax(jnp.where(allowed, s, neg), axis=-1)
        attn = p[:, :, 0] - lam * p[:, :, 1]
        return jnp.einsum('bhqk,bhkd->bhqd', attn.astype(vh.dtype), vh)

    out = lax.map(block, (qb, qpos))
    return out.transpose(1, 0, 3, 2, 4).reshape(B, S, H, dv)

def second_inputs(seed: int = 0) -> dict:
    key = jax.random.key(seed)
    ks = jax.random.split(key, 14)
    f32 = jnp.float32
    out_scale = (2.0 * DEPTH_2) ** -0.5
    x = jax.random.normal(ks[0], (BATCH, SEQ, D_MODEL), f32)
    w_in = jax.random.normal(ks[1], (DEPTH_2, D_MODEL, PROJ_WIDTH), f32) * D_MODEL ** -0.5
    w_o = jax.random.normal(ks[2], (DEPTH_2, MIX_WIDTH_2, D_MODEL), f32) * (MIX_WIDTH_2 ** -0.5) * out_scale
    attn_norm = 1.0 + 0.02 * jax.random.normal(ks[3], (DEPTH_2, D_MODEL), f32)
    subln_norm = 1.0 + 0.02 * jax.random.normal(ks[4], (DEPTH_2, 2 * DF_HEAD_DIM), f32)
    lam_q1 = 0.1 * jax.random.normal(ks[5], (DEPTH_2, DF_HEAD_DIM), f32)
    lam_k1 = 0.1 * jax.random.normal(ks[6], (DEPTH_2, DF_HEAD_DIM), f32)
    lam_q2 = 0.1 * jax.random.normal(ks[7], (DEPTH_2, DF_HEAD_DIM), f32)
    lam_k2 = 0.1 * jax.random.normal(ks[8], (DEPTH_2, DF_HEAD_DIM), f32)
    mlp_norm = 1.0 + 0.02 * jax.random.normal(ks[9], (DEPTH_2, D_MODEL), f32)
    w_ff1 = jax.random.normal(ks[10], (DEPTH_2, D_MODEL, D_FF_2), f32) * D_MODEL ** -0.5
    w_ff2 = jax.random.normal(ks[11], (DEPTH_2, D_FF_2, D_MODEL), f32) * (D_FF_2 ** -0.5) * out_scale
    final_norm = 1.0 + 0.02 * jax.random.normal(ks[12], (D_MODEL,), f32)
    return {"x": x, "w_in": w_in, "w_o": w_o, "attn_norm": attn_norm,
            "subln_norm": subln_norm, "lam_q1": lam_q1, "lam_k1": lam_k1,
            "lam_q2": lam_q2, "lam_k2": lam_k2, "mlp_norm": mlp_norm,
            "w_ff1": w_ff1, "w_ff2": w_ff2, "final_norm": final_norm}

def second_block(x, w_in, w_o, attn_norm, subln_norm, lam_q1, lam_k1, lam_q2, lam_k2,
              mlp_norm, w_ff1, w_ff2, final_norm):
    B, S, _ = x.shape
    pos = jnp.arange(S)
    splits = np.cumsum([SB_WIDTH, SB_WIDTH, SB_WIDTH, DF_WIDTH, DF_WIDTH]).tolist()
    for l in range(DEPTH_2):
        h = rmsnorm(x, attn_norm[l])
        proj = jnp.einsum('bsd,de->bse', h, w_in[l])
        sb_q, sb_k, sb_v, df_q, df_k, df_v = jnp.split(proj, splits, axis=-1)

        sb_out = stick_breaking_attention(
            sb_q.reshape(B, S, SB_HEADS, SB_HEAD_DIM),
            sb_k.reshape(B, S, SB_HEADS, SB_HEAD_DIM),
            sb_v.reshape(B, S, SB_HEADS, SB_HEAD_DIM))

        lambda_init = 0.8 - 0.6 * math.exp(-0.3 * l)
        lam = (jnp.exp(jnp.sum(lam_q1[l].astype(jnp.float32) * lam_k1[l].astype(jnp.float32)))
               - jnp.exp(jnp.sum(lam_q2[l].astype(jnp.float32) * lam_k2[l].astype(jnp.float32)))
               + lambda_init)
        dq = rope(df_q.reshape(B, S, DF_HEADS, 2, DF_HEAD_DIM), pos)
        dk = rope(df_k.reshape(B, S, DF_HEADS, 2, DF_HEAD_DIM), pos)
        dvv = df_v.reshape(B, S, DF_HEADS, 2 * DF_HEAD_DIM)
        df_heads = differential_attention(dq, dk, dvv, lam)
        df_out = (rmsnorm(df_heads, subln_norm[l]) * (1.0 - lambda_init)).reshape(B, S, DF_WIDTH)

        mixed = jnp.concatenate([sb_out, df_out.astype(sb_out.dtype)], axis=-1)
        x = x + jnp.einsum('bse,ed->bsd', mixed, w_o[l])

        h = rmsnorm(x, mlp_norm[l])
        u = jnp.square(jax.nn.relu(jnp.einsum('bsd,df->bsf', h, w_ff1[l])))
        x = x + jnp.einsum('bsf,fd->bsd', u, w_ff2[l])
    return rmsnorm(x, final_norm)


def setup_inputs(seed=0):
    out = dict(first_inputs(seed))
    for name, value in second_inputs(seed + 1).items():
        if name != "x":
            out[name + "_2"] = value
    return out


def reference(
    x, norm_mix, w_in, q_norm, k_norm, cmp_pos_k, cmp_pos_v, cmp_k_w1, cmp_k_w2, cmp_v_w1,
    cmp_v_w2, hgrn_lb_logits, hgrn_o_norm, w_out, norm_ffn, w_gate_up, w_down, w_in_2, w_o_2,
    attn_norm_2, subln_norm_2, lam_q1_2, lam_k1_2, lam_q2_2, lam_k2_2, mlp_norm_2, w_ff1_2,
    w_ff2_2, final_norm_2,
):
    x = first_block(
        x, norm_mix, w_in, q_norm, k_norm, cmp_pos_k, cmp_pos_v, cmp_k_w1, cmp_k_w2, cmp_v_w1,
        cmp_v_w2, hgrn_lb_logits, hgrn_o_norm, w_out, norm_ffn, w_gate_up, w_down,
    )
    return second_block(
        x, w_in_2, w_o_2, attn_norm_2, subln_norm_2, lam_q1_2, lam_k1_2, lam_q2_2, lam_k2_2,
        mlp_norm_2, w_ff1_2, w_ff2_2, final_norm_2,
    )


_drawn_inputs = setup_inputs


def setup_inputs(seed=0):
    import zlib

    import numpy as np

    out = dict(_drawn_inputs(seed))
    spreads = {}
    factors = {'norm_mix': 3.627,
     'q_norm': 8.0,
     'k_norm': 8.0,
     'hgrn_o_norm': 6.555,
     'norm_ffn': 3.841,
     'attn_norm_2': 5.419,
     'subln_norm_2': 64.0,
     'lam_q2_2': 29.674,
     'mlp_norm_2': 11.608,
     'final_norm_2': 8.019,
     'lam_q1_2': 4.921,
     'lam_k1_2': 5.487}
    for name, (base, spread) in spreads.items():
        noise = np.random.default_rng([zlib.crc32(name.encode()), seed]).standard_normal(out[name].shape)
        drawn = base * np.exp(spread * noise) if base else spread * noise
        out[name] = jnp.asarray(drawn.astype(out[name].dtype))
    for name, factor in factors.items():
        out[name] = (out[name] * factor).astype(out[name].dtype)
    return out
```

```python
import numpy as np
import concourse.bass as bass
from concourse import mybir
from concourse.alu_op_type import AluOpType as ALU
from contextlib import ExitStack

F32 = mybir.dt.float32
F32R = mybir.dt.float32r
BF16 = mybir.dt.bfloat16
U32 = mybir.dt.uint32
AF = mybir.ActivationFunctionType
AX = mybir.AxisListType

T = 512
D = 1024
KT = D // 128
NEG = -1e30
EPS = 1e-6
D_FF = 2816
D_FF2 = 4096


class Step:

    def __init__(self, sem=None, value=None):
        self.sem, self.value, self.signals = sem, value, False


class Slot:

    def __init__(self, sem):
        self.sem, self.count = sem, 0


class Lane:

    def __init__(self, sem):
        self.sem, self.items = sem, []

    def __call__(self, fn):
        step = Step()
        self.items.append((step, fn))
        return step

    def wait(self, *steps):
        for s in steps:
            if s is not None:
                s.signals = True
                self.items.append((s, None))

    def dma(self, slot, fn):
        slot.count += 16
        step = Step(slot.sem, slot.count)
        self.items.append((step, fn))
        return step

    def number(self):
        n = 0
        for step, fn in self.items:
            if fn is not None and step.sem is None and step.signals:
                n += 1
                step.sem, step.value = self.sem, n
                step.mine = True

    def play(self, eng):
        seen = {}
        for step, fn in self.items:
            if fn is None:
                if seen.get(step.sem.name, 0) < step.value:
                    eng.wait_ge(step.sem, step.value)
                    seen[step.sem.name] = step.value
                continue
            ins = fn(eng)
            if step.sem is not None:
                ins.then_inc(step.sem, 1 if step.sem is self.sem else 16)


def program(nc, A, out):
    ctx = ExitStack()
    with ctx:
        def semaphore(name):
            return ctx.enter_context(nc.semaphore(name))

        pe, act, dve, pool, sp = (Lane(semaphore(n)) for n in ("s_pe", "s_act", "s_dve", "s_pool", "s_sp"))
        lanes = (pe, act, dve, pool, sp)

        base = (nc.sbuf_base + 63) // 64 * 64
        room = nc.sbuf_usable_end - base

        def at(name, shape, dt, off):
            size = int(np.prod(shape[1:])) * mybir.dt.size(dt)
            assert off % 32 == 0 and off + size <= room, (name, off, size, room)
            return nc.alloc_sbuf_tensor_at(name, shape, dt, offset=base + off)

        NR, NS = 2, 4
        o_x = 0
        o_h = o_x + 16384
        o_raw = o_h + 32768
        o_ws = o_raw + NR * 8192
        o_u = o_ws + NS * 8192
        o_c = o_u + 32768
        XT = at("XT", [128, KT, T], F32, o_x)
        HH = at("HH", [128, KT, T], F32R, o_h)
        HL = at("HL", [128, KT, T], F32R, o_h + 16384)
        RAW = at("RAW", [128, NR, 2048], F32, o_raw)
        WH = at("WH", [128, NS, 1024], F32R, o_ws)
        WL = at("WL", [128, NS, 1024], F32R, o_ws + NS * 4096)
        UH = at("UH", [128, KT, T], F32R, o_u)
        UL = at("UL", [128, KT, T], F32R, o_u + 16384)
        P = ctx.enter_context(nc.psum_tensor("ps", [128, 8, 512], F32))

        off = [o_c]

        def const(name, shape, dt):
            t = at(name, shape, dt, off[0])
            off[0] += (int(np.prod(shape[1:])) * mybir.dt.size(dt) + 31) // 32 * 32
            return t

        IDN = const("IDN", [128, 128], F32)
        IDB = const("IDB", [128, 128], BF16)
        ONES = const("ONES", [128, 128], F32)
        BLK = const("BLK", [128, 128], F32)
        M01 = const("M01", [128, 128], F32)
        MASKB = const("MASKB", [128, 4, 128], BF16)
        VEC = const("VEC", [128, 128], F32)
        GT = const("GT", [128, 128], F32)
        CS_off = off[0]
        CS = const("CS", [128, 2, T], F32)
        RB = const("RB", [128, T], F32)
        SM = const("SM", [128, 64], F32)
        RT = SM[:, 0:4]
        STD = SM[:, 4:8]
        EPSC = SM[:, 8:9]
        LB = SM[:, 12:16]
        LB1 = SM[:, 16:20]
        QFOLD = SM[:, 20:23]
        LAM = SM[:, 24:26]
        MS = SM[:, 28:32]
        NW = SM[:, 60:64]
        o_a = (off[0] + 63) // 64 * 64

        def matmul(o, l, r, start, stop):
            return pe(lambda e: e.matmul(o, l, r, start=start, stop=stop))

        def transpose(o, i, ident):
            return pe(lambda e: e.transpose(o, i, ident))

        def tt(lane, o, a, b, op):
            return lane(lambda e: e.tensor_tensor(o, a, b, op))

        def ts(lane, o, a, s1, op0, s2=None, op1=None):
            if op1 is None:
                return lane(lambda e: e.tensor_scalar(o, a, s1, None, op0))
            return lane(lambda e: e.tensor_scalar(o, a, s1, s2, op0, op1))

        def stt(lane, o, a, s, b, op0, op1):
            return lane(lambda e: e.scalar_tensor_tensor(o, a, s, b, op0, op1))

        def copy(lane, o, a):
            if lane is act:
                return lane(lambda e: e.copy(o, a))
            return lane(lambda e: e.tensor_copy(o, a))

        def activ(o, a, func, scale=1.0, bias=None, accum=None):
            kw = {}
            if bias is not None:
                kw["bias"] = bias
            if accum is not None:
                kw["accum_out"] = accum
            return act(lambda e: e.activation(o, a, func, scale=scale, **kw))

        def recip(o, a):
            return dve(lambda e: e.reciprocal(o, a))

        def zero(lane, o):
            return lane(lambda e: e.memset(o, 0.0))

        def diff(lane, o, a, b):
            return tt(lane, o, a, b, ALU.subtract)

        bfree = [[] for _ in range(8)]

        class Unit:
            pass

        units = []

        def plan(src_cols, nk, raw=False, rows=None):
            u = Unit()
            u.src, u.nk, u.raw = src_cols, nk, raw
            u.width = sum(s.shape[-1] for s in src_cols) if not raw else 0
            u.i = len(units)
            units.append(u)
            return u

        wslots = [Slot(semaphore(f"s_w{i}")) for i in range(NR)]
        raw_free = [[] for _ in range(NR)]
        slot_free = [[] for _ in range(NS)]
        state = {"load": 0, "split": 0, "slot": 0}

        def pump():
            while state["load"] < len(units) and raw_free[state["load"] % NR] is not None:
                u = units[state["load"]]
                r = u.i % NR
                sp.wait(*raw_free[r])
                raw_free[r] = None
                c = 0
                for s in u.src:
                    if u.raw:
                        dst, src = s[0](RAW[:, r, :]), s[1]
                    else:
                        w = s.shape[-1]
                        dst = RAW[:, r, 0:u.nk * u.width].rearrange("p (k c) -> p k c", k=u.nk)[:, :, c:c + w]
                        src = s.rearrange("(k p) c -> p k c", p=128)
                        c += w
                    u.arrived = sp.dma(wslots[r], lambda e, dst=dst, src=src: e.dma_start(dst, src))
                state["load"] += 1

        def split_next():
            u = units[state["split"]]
            r = u.i % NR
            state["split"] += 1
            if u.raw:
                u.view = RAW[:, r, :]
                return
            rv = RAW[:, r, 0:u.nk * u.width].rearrange("p (k c) -> p k c", k=u.nk)
            half = u.half = u.width // 2 if u.width > 128 else u.width
            u.slots, u.ready = [], []
            for t in range(u.width // half):
                s = (state["slot"] + t) % NS
                hv = WH[:, s, 0:u.nk * half].rearrange("p (k c) -> p k c", k=u.nk)
                lv = WL[:, s, 0:u.nk * half].rearrange("p (k c) -> p k c", k=u.nk)
                src = rv[:, :, t * half:(t + 1) * half]
                act.wait(u.arrived, *slot_free[s])
                h = copy(act, hv, src)
                dve.wait(u.arrived, h)
                lo = diff(dve, lv, src, hv)
                u.slots.append(s)
                u.ready.append(lo)
            raw_free[r] = [lo]
            state["slot"] += 2

        def begin(u):
            pump()
            while state["split"] < min(len(units), u.i + 2):
                split_next()
                pump()

        def release_raw(u, step):
            raw_free[u.i % NR] = [step]
            pump()

        def release(u, step):
            for s in u.slots:
                slot_free[s] = [step]

        def wtile(u, n):
            per = max(1, u.half // 128)
            return n // per, (n % per) * 128

        def unit_mms(u, banks, xh, xl, kouter=False, evac=None, ncol=128):
            begin(u)
            n = len(banks)
            u.banks, u.last = banks, [None] * n

            def one(i, kt):
                t, c0 = wtile(u, i)
                s, b = u.slots[t], banks[i]
                if kt == 0:
                    pe.wait(*bfree[b])
                pe.wait(u.ready[t])
                k0 = kt * u.half + c0
                wh, wl = WH[:, s, k0:k0 + ncol], WL[:, s, k0:k0 + ncol]
                o = P[0:ncol, b, :]
                h, l = xh(kt), xl(kt)
                matmul(o, wh, h, kt == 0, False)
                matmul(o, wh, l, False, False)
                return matmul(o, wl, h, False, kt == u.nk - 1)

            if kouter:
                for kt in range(u.nk):
                    for i in range(n):
                        u.last[i] = one(i, kt)
                    yield 0.64 * n
                release(u, u.last[-1])
                if evac:
                    for i in range(n):
                        evac(i, banks[i], u.last[i])
            else:
                for i in range(n):
                    for kt in range(u.nk):
                        u.last[i] = one(i, kt)
                        if kt % 2 == 1:
                            yield 1.28
                    if i == n - 1:
                        release(u, u.last[-1])
                    if evac:
                        evac(i, banks[i], u.last[i])

        def vunit_mms(u, banks, evac):
            begin(u)
            s = u.slots[0]
            assert s % 2 == 0
            for tp in range(2):
                b = banks[tp]
                pe.wait(*bfree[b])
                pe.wait(u.ready[1])
                for q in range(2):
                    t = 2 * tp + q
                    o = P[:, b, 256 * q:256 * q + 256]
                    for kt in range(KT):
                        wh, wl = WH[:, s:s + 2, kt * 128:kt * 128 + 128], WL[:, s:s + 2, kt * 128:kt * 128 + 128]
                        h, l = HH[:, kt, 128 * t:128 * t + 128], HL[:, kt, 128 * t:128 * t + 128]
                        matmul(o, h, wh, kt == 0, False)
                        matmul(o, h, wl, False, False)
                        last = matmul(o, l, wh, False, kt == KT - 1)
                        if kt % 4 == 3:
                            yield 1.28
                if tp == 1:
                    release(u, last)
                evac(tp, b, last)

        def run(gen, steps=None):
            n = 0
            for _ in gen:
                n += 1
                if steps and n >= steps:
                    return

        norm = {}
        h_last = [None]

        def prep_tile(kt, ev, g0, sq_a, sq_b):
            g = GT[:, g0 + kt:g0 + kt + 1]
            act.wait(ev, h_last[0])
            hi = activ(HH[:, kt, :], XT[:, kt, :], AF.Identity, scale=g)
            dve.wait(ev, hi)
            lo = stt(dve, HL[:, kt, :], XT[:, kt, :], g, HH[:, kt, :], ALU.mult, ALU.subtract)
            norm.setdefault("h", {})[kt] = lo
            if kt == 0:
                norm["acc"] = activ(sq_a, XT[:, kt, :], AF.Square)
            else:
                if kt > 1:
                    act.wait(norm["acc"])
                s = activ(sq_b, XT[:, kt, :], AF.Square)
                lane = dve if kt == KT - 1 else pool
                lane.wait(s, norm["acc"])
                norm["acc"] = tt(lane, sq_a, sq_a, sq_b, ALU.add)

        def xh(kt):
            pe.wait(norm["h"][kt])
            return HH[:, kt, :]

        def xl(kt):
            return HL[:, kt, :]

        def norm_sums(sq_a, bank):
            pe.wait(norm["acc"], *bfree[bank])
            for t in range(4):
                m = matmul(P[:, bank, 2 * t:2 * t + 2], sq_a[:, 128 * t:128 * t + 128], ONES[:, 0:2], True, True)
            act.wait(m, *norm.get("rt_read", []))
            s = activ(STD, P[:, bank, 0:8:2], AF.Sqrt, scale=1.0 / D, bias=EPSC)
            bfree[bank] = [s]
            dve.wait(s)
            m = ts(dve, MS, P[:, bank, 0:8:2], 1.0 / D, ALU.mult, EPS, ALU.add)
            bfree[bank] = [m]
            norm["rt"] = rsqrt_step(RT, STD, MS, NW, m)

        def rsqrt_step(y, std, ms, w, ms_ev):
            a = recip(y, std)
            dve.wait(a, ms_ev)
            a = tt(dve, w, y, y, ALU.mult)
            dve.wait(a)
            a = tt(dve, w, w, ms, ALU.mult)
            dve.wait(a)
            a = ts(dve, w, w, -0.5, ALU.mult, 1.5, ALU.add)
            dve.wait(a)
            return tt(dve, y, y, w, ALU.mult)

        def norm_spread(diag, diag_free, bank):
            dve.wait(norm["rt"], *diag_free)
            for t in range(4):
                d = ts(dve, diag[:, 128 * t:128 * t + 128], IDN[:], RT[:, t:t + 1], ALU.mult)
            pe.wait(d, *bfree[bank])
            m = matmul(P[:, bank, :], ONES[:], diag, True, True)
            act.wait(m, *norm.get("rb_read", []))
            norm["rb"] = copy(act, RB[:], P[:, bank, :])
            bfree[bank] = [norm["rb"]]
            return m

        cslots = Slot(semaphore("s_const"))
        vslots = Slot(semaphore("s_vec"))
        xslots = [Slot(semaphore(f"s_x{i}")) for i in range(4)]
        XIN = at("XIN", [128, 4, D], F32, o_u)
        CIN = at("CIN", [128, 1024], F32, o_h)
        x_in = []
        for t in range(4):
            x_in.append(sp.dma(xslots[t], lambda e, t=t: e.dma_start(XIN[:, t, :], A["x"][0, 128 * t:128 * t + 128, :])))
            if t == 0:
                c_in = act.dma(cslots, lambda e: e.dma_start(IDN[:], A["c_idn"]))
                c_in = act.dma(cslots, lambda e: e.dma_start(CIN[:], A["c_small"]))
        vec_rows = [(A["norm_mix"].rearrange("o (k p) -> (o k) p", p=128), 0, 8, 0),
                    (A["norm_ffn"].rearrange("o (k p) -> (o k) p", p=128), 8, 8, 0),
                    (A["attn_norm_2"].rearrange("l (k p) -> (l k) p", p=128), 16, 16, 0),
                    (A["mlp_norm_2"].rearrange("l (k p) -> (l k) p", p=128), 32, 16, 0),
                    (A["hgrn_o_norm"], 52, 1, 0), (A["subln_norm_2"], 53, 2, 0),
                    (A["hgrn_lb_logits"].rearrange("l (k p) -> (l k) p", p=128), 55, 8, 0),
                    (A["final_norm_2"][0:128].rearrange("(o p) -> o p", o=1), 63, 1, 0)]
        for c in (0, 64):
            vec_rows += [(A["q_norm"], 48, 1, c), (A["k_norm"][0], 49, 3, c),
                         (A["cmp_pos_k"][0], 64, 32, c), (A["cmp_pos_v"][0], 96, 32, c)]
        for src, r0, n, c in vec_rows:
            v_in = act.dma(vslots, lambda e, src=src, r0=r0, n=n, c=c: e.dma_start(
                VEC[r0:r0 + n, c:c + src.shape[-1]], src))
        pool(lambda e: e.memset(ONES[:], 1.0))
        ones = pool(lambda e: e.memset(EPSC, EPS))
        dve.wait(c_in)
        copy(dve, BLK[:], CIN[:, 0:128])
        copy(dve, MASKB[:].rearrange("p a b -> p (a b)"), CIN[:, 128:640])
        copy(dve, M01[:], CIN[:, 640:768])
        c_ready = copy(dve, IDB[:], IDN[:])

        pe.wait(v_in, c_in, ones, c_ready)
        m = transpose(P[:, 7, 0:128], VEC[:], IDN[:])
        dve.wait(m)
        gt_ready = copy(dve, GT[:], P[:, 7, 0:128])
        bfree[7] = [gt_ready]
        act.wait(gt_ready)
        pool.wait(gt_ready)

        SQA = at("SQA", [128, T], F32, o_a)
        SQB = at("SQB", [128, T], F32, o_a + 2048)
        DIAG = at("DIAG", [128, T], F32, o_a + 4096)

        xt_ev = [None] * KT

        def load_x():
            h_last[0] = c_ready
            norm["h"] = {}
            for kt in range(KT):
                b = kt % 6
                pe.wait(*bfree[b])
                for t in range(4):
                    pe.wait(x_in[t])
                    m = transpose(P[:, b, 128 * t:128 * t + 128], XIN[:, t, 128 * kt:128 * kt + 128], IDN[:])
                dve.wait(m)
                ev = copy(dve, XT[:, kt, :], P[:, b, :])
                bfree[b] = [ev]
                xt_ev[kt] = ev
                prep_tile(kt, ev, 0, SQA[:], SQB[:])

        load_x()

        def ffn(g_up, planned, chunks, gated, last_layer, g_next):
            TG = [at(f"TG{g_up}_{i}", [128, T], F32, o_a + 6144 + 2048 * i) for i in range(4)]
            TS = [at(f"TS{g_up}_{i}", [128, T], F32, o_a + 14336 + 2048 * i) for i in range(4)]
            TU = [at(f"TU{g_up}_{i}", [128, T], F32, o_a + 22528 + 2048 * i) for i in range(4)]
            tg_free, ts_free, tu_free = [None] * 4, [None] * 4, [None] * 4
            u_ready = {}
            u_last = [None]
            ring = [0]
            todo = list(planned)
            pending = []
            first = [True]

            def banks(n):
                got = [(ring[0] + i) % 6 for i in range(n)]
                ring[0] += n
                return got

            def hidden(j, n, src_step, lane_lo):
                act.wait(src_step, u_last[0])
                h = copy(act, UH[:, j, :], TU[n][:])
                lane_lo.wait(src_step, h, u_last[0])
                u_ready[j] = diff(lane_lo, UL[:, j, :], TU[n][:], UH[:, j, :])
                tu_free[n] = u_ready[j]

            gates = {}

            def ev_gate(j, b, ev):
                n = j % 4
                dve.wait(ev, norm["rb"], tg_free[n])
                g = tt(dve, TG[n][:], P[:, b, :], RB[:], ALU.mult)
                bfree[b] = [g]
                act.wait(g, ts_free[n])
                s = activ(TS[n][:], TG[n][:], AF.Silu)
                tg_free[n] = s
                pool.wait(s, norm["rb"])
                gates[j] = tt(pool, TS[n][:], TS[n][:], RB[:], ALU.mult)

            def ev_up(j, b, ev):
                n = j % 4
                dve.wait(ev, gates[j], tu_free[n])
                u = tt(dve, TU[n][:], P[:, b, :], TS[n][:], ALU.mult)
                bfree[b] = [u]
                ts_free[n] = u
                hidden(j, n, u, dve)

            def ev_relu2(j, b, ev):
                n = j % 4
                dve.wait(ev, norm["rb"], tg_free[n])
                a = tt(dve, TG[n][:], P[:, b, :], RB[:], ALU.mult)
                bfree[b] = [a]
                dve.wait(a, tu_free[n])
                u = stt(dve, TU[n][:], TG[n][:], 0.0, TG[n][:], ALU.max, ALU.mult)
                tg_free[n] = u
                hidden(j, n, u, dve)

            def up_unit(evac, j0):
                u = todo.pop(0)
                bs = banks(2)
                if first[0]:
                    first[0] = False
                    run(unit_mms(u, bs, xh, xl, kouter=True))
                    norm_sums(SQA, 6)
                    pending.append(lambda: [evac(j0 + i, bs[i], u.last[i]) for i in range(2)])
                    return
                gen = unit_mms(u, bs, xh, xl, kouter=True)
                if pending:
                    run(gen, 3)
                    norm_spread(DIAG[:], [], 7)
                    pending.pop()()
                run(gen)
                for i in range(2):
                    evac(j0 + i, bs[i], u.last[i])
                h_last[0] = u.last[1]

            def uh(kt):
                pe.wait(u_ready[kt])
                return UH[:, kt, :]

            def ul(kt):
                return UL[:, kt, :]

            if last_layer:
                XK = at("XK", [128, 4, D], F32, o_a + 31 * 1024)
                FG = at("FG", [128, D], F32, o_a + 47 * 1024)
                OUT = at("OUT", [128, 4, D], F32, o_a + 51 * 1024)
                SQ = at("SQ", [128, 256], F32, o_a + 67 * 1024)
                SS = SM[:, 44:60].rearrange("p (t o) -> p t o", t=4)
                gslot = Slot(semaphore("s_fg"))
                fg_in = sp.dma(gslot, lambda e: e.dma_start(
                    FG[:], A["final_norm_2"].rearrange("(o d) -> o d", o=1).partition_broadcast(128)[:, 0]))
                xk_ev = [[None] * 4 for _ in range(4)]

                def turn_x():
                    for t in range(4):
                        for half in range(2):
                            b = 6 + half
                            pe.wait(*bfree[b])
                            for k in range(4):
                                kt = 4 * half + k
                                pe.wait(xt_ev[kt])
                                m = transpose(P[:, b, 128 * k:128 * k + 128], XT[:, kt, 128 * t:128 * t + 128], IDN[:])
                            act.wait(m)
                            c = copy(act, XK[:, t, 512 * half:512 * half + 512], P[:, b, :])
                            bfree[b] = [c]
                            for o in (2 * half, 2 * half + 1):
                                xk_ev[t][o] = c
                        yield

                def down_tok(u, o, final):
                    bs = banks(4)
                    begin(u)
                    s = u.slots[0]

                    def one(t, kt):
                        pe.wait(u.ready[1], u_ready[kt])
                        w = slice(128 * kt, 128 * kt + 128)
                        wh, wl = WH[:, s:s + 2, w], WL[:, s:s + 2, w]
                        tok = slice(128 * t, 128 * t + 128)
                        h, lw = UH[:, kt, tok], UL[:, kt, tok]
                        p = P[:, bs[t], 0:256]
                        matmul(p, h, wh, kt == 0, False)
                        matmul(p, h, wl, False, False)
                        return matmul(p, lw, wh, False, kt == u.nk - 1)

                    last = [None] * 4
                    for t in range(4):
                        pe.wait(*bfree[bs[t]])
                        if final:
                            for kt in range(u.nk):
                                last[t] = one(t, kt)
                    if not final:
                        for kt in range(u.nk):
                            for t in range(4):
                                last[t] = one(t, kt)
                    release(u, last[3])
                    u_last[0] = last[3]
                    for t in range(4):
                        x = XK[:, t, 256 * o:256 * o + 256]
                        dve.wait(last[t], xk_ev[t][o])
                        xk_ev[t][o] = tt(dve, x, P[:, bs[t], 0:256], x, ALU.add)
                        bfree[bs[t]] = [xk_ev[t][o]]
                        if final:
                            act.wait(xk_ev[t][o], sq_free[0])
                            sq_free[0] = activ(SQ[:], x, AF.Square, accum=SS[:, t, o:o + 1])
                            if o == 3:
                                finish(t)

                sq_free = [None]
                oslots = [Slot(semaphore(f"s_out{t}")) for t in range(4)]
                stored = []

                def finish(t):
                    r = STD[:, t:t + 1]
                    dve.wait(sq_free[0])
                    a = dve(lambda e: e.tensor_reduce(r, SS[:, t, :], AX.X, ALU.add))
                    act.wait(a)
                    a = activ(r, r, AF.Sqrt, scale=1.0 / D, bias=EPSC)
                    dve.wait(a)
                    a = recip(RT[:, t:t + 1], r)
                    dve.wait(a, fg_in)
                    y = stt(dve, OUT[:, t, :], XK[:, t, :], RT[:, t:t + 1], FG[:], ALU.mult, ALU.mult)
                    sp.wait(y)
                    stored.append(sp.dma(oslots[t], lambda e: e.dma_start(out[0, 128 * t:128 * t + 128, :], OUT[:, t, :])))

                turner = turn_x()

            for ci, n in enumerate(chunks):
                if gated:
                    for j in range(0, n, 2):
                        up_unit(ev_gate, j)
                        up_unit(ev_up, j)
                else:
                    for j in range(0, n, 2):
                        up_unit(ev_relu2, j)
                        if last_layer and j > 2:
                            next(turner, None)
                            next(turner, None)
                final = ci == len(chunks) - 1
                if final:
                    norm["h"] = {}
                for o in range(0, KT, 2):
                    u = todo.pop(0)
                    if last_layer:
                        down_tok(u, o // 2, final)
                        continue
                    bs = banks(2)
                    run(unit_mms(u, bs, uh, ul, kouter=True))
                    for i in range(2):
                        dve.wait(u.last[i], xt_ev[o + i])
                        xt_ev[o + i] = tt(dve, XT[:, o + i, :], P[:, bs[i], :], XT[:, o + i, :], ALU.add)
                        bfree[bs[i]] = [xt_ev[o + i]]
                        if final:
                            prep_tile(o + i, xt_ev[o + i], g_next, SQA[:], SQB[:])
                    u_last[0] = u.last[1]
            assert not todo
            if last_layer:
                sp.wait(*stored)

        def plan_ffn1():
            w, wd = A["w_gate_up"][0], A["w_down"][0]
            got = []
            for n, j0 in ((8, 0), (8, 8), (6, 16)):
                for j in range(j0, j0 + n, 2):
                    got.append(plan([w[:, 128 * j:128 * j + 256]], KT))
                    got.append(plan([w[:, D_FF + 128 * j:D_FF + 128 * j + 256]], KT))
                for o in range(0, D, 256):
                    got.append(plan([wd[128 * j0:128 * (j0 + n), o:o + 256]], n))
            return got

        def plan_ffn2(l):
            w, wd = A["w_ff1_2"][l], A["w_ff2_2"][l]
            got = []
            for j0 in range(0, 32, 8):
                for j in range(j0, j0 + 8, 2):
                    got.append(plan([w[:, 128 * j:128 * j + 256]], KT))
                for o in range(0, D, 256):
                    got.append(plan([wd[128 * j0:128 * (j0 + 8), o:o + 256]], 8))
            return got

        W1 = A["w_in"][0]
        C_Q, C_KC, C_VC, C_KS, C_VS, C_KW, C_VW, C_G, C_HQ, C_HF, C_HI, C_HG = (
            0, 512, 640, 768, 896, 1024, 1152, 1280, 1304, 1816, 2328, 2840)

        def wcols(c, n=128):
            return W1[:, c:c + n]

        m1 = {}
        for name, src in (("hqf0", [wcols(C_HQ), wcols(C_HF)]),
                          ("hi0", [wcols(C_HI, 256)]),
                          ("hqf1", [wcols(C_HQ + 128), wcols(C_HF + 128)]),
                          ("hg0", [wcols(C_HG, 256)]),
                          ("cmp", [wcols(C_KC, 256)]),
                          ("hqf2", [wcols(C_HQ + 256), wcols(C_HF + 256)]),
                          ("hi1", [wcols(C_HI + 256, 256)]),
                          ("hqf3", [wcols(C_HQ + 384), wcols(C_HF + 384)]),
                          ("hg1", [wcols(C_HG + 256, 256)]),
                          ("ksw", [wcols(C_KS), wcols(C_KW)]),
                          ("vsw", [wcols(C_VS), wcols(C_VW)]),
                          ("gate", [wcols(C_G, 24)]),
                          ("q0", [wcols(C_Q, 256)]),
                          ("q1", [wcols(C_Q + 256, 256)])):
            m1[name] = plan(src, KT)
        for name, r, c in (("wh0", 512, 0), ("wh1", 512, 512), ("wn0", 0, 0), ("wn1", 0, 512)):
            m1[name] = plan([A["w_out"][0][r:r + 512, c:c + 512]], 4)
        p1 = plan_ffn1()

        KB = 1024

        class attention_forms:
            SPOT = {3: (2, 0, 512), 2: (3, 0, 384), 0: (3, 384, 128), 1: (4, 0, 256)}
            ORDER = (3, 2, 0, 1)

            def __init__(self, pf, ph, pl):
                self.pf, self.ph, self.pl = pf, ph, pl
                self.pf_free = [[] for _ in pf]
                self.pt_free = [[] for _ in ph]
                self.turned = {}
                self.t_next = 0

            @staticmethod
            def cols(t):
                c = {3: 0, 2: 512, 0: 896, 1: 1024}[t]
                return c, c + 128 * (t + 1)

            @staticmethod
            def trow(j):
                c = {0: 0, 1: 512, 3: 896, 2: 1024}[j]
                return c, c + 512 - 128 * j

            def scores(self, q, hh, ll, mask):
                self.s_ev = {}
                for t in self.ORDER:
                    b, c, n = self.SPOT[t]
                    if c == 0:
                        pe.wait(*bfree[b])
                    o = P[:, b, c:c + n]
                    matmul(o, q[:, 128 * t:128 * t + 128], hh[:, 0:n], True, False)
                    matmul(o, q[:, 128 * t:128 * t + 128], ll[:, 0:n], False, False)
                    self.s_ev[t] = matmul(P[:, b, c + n - 128:c + n], IDB[:], MASKB[:, mask, :], False, True)

            def scores2(self, q, hh, lo, x, mask):
                own = slice(64 * x, 64 * x + 64)
                self.s_ev = {}
                for t in self.ORDER:
                    b, c, n = self.SPOT[t]
                    if c == 0:
                        pe.wait(*bfree[b])
                    o = P[:, b, c:c + n]
                    matmul(o, q[:, 128 * t:128 * t + 128], hh[:, 0:n], True, False)
                    matmul(o, q[own, 128 * t:128 * t + 128], lo[own, 0:n], False, False)
                    self.s_ev[t] = matmul(P[:, b, c + n - 128:c + n], IDB[:], MASKB[:, mask, :], False, True)
                return self.s_ev[1]

            def values3(self, n, vh, vl):
                k = n % len(self.ph)
                pe.wait(*self.turned[n])
                for j in range(4):
                    c = self.trow(j)
                    o = P[:, 7, 128 * j:512]
                    matmul(o, vh(j), self.ph[k][:, c[0]:c[1]], j == 0, False)
                    matmul(o, vh(j), self.pl[k][:, c[0]:c[1]], False, False)
                    m = matmul(o, vl(j), self.ph[k][:, c[0]:c[1]], False, j == 3)
                self.pt_free[k] = [m]
                return m

            def spot(self, t):
                b, c, n = self.SPOT[t]
                return P[:, b, c:c + n]

            def row_max(self, st, scale, scale_ev, free):
                dve.wait(*free)
                for t in self.ORDER:
                    dve.wait(self.s_ev[0 if t == 2 else t])
                    o, i = st[:, t:t + 1], self.spot(t)
                    m = dve(lambda e, o=o, i=i: e.tensor_reduce(o, i, AX.X, ALU.max))
                dve.wait(m, scale_ev)
                return stt(dve, st[:, 4:8], st[:, 0:4], -1.0, scale, ALU.mult, ALU.mult)

            def exps(self, n, st, scale, h, neg):
                i = n % len(self.pf)
                act.wait(neg, *self.pf_free[i])
                for t in self.ORDER:
                    c = self.cols(t)
                    x = activ(self.pf[i][:, c[0]:c[1]], self.spot(t), AF.Exp, scale=scale[:, t, h:h + 1],
                              bias=st[:, 4 + t:5 + t], accum=st[:, 8 + t:9 + t])
                    bfree[self.SPOT[t][0]] = [x]
                return x

            def turn(self, n, ready, i=None):
                i, k = n % len(self.pf) if i is None else i, n % len(self.ph)
                pf, ph, pl = self.pf[i], self.ph[k], self.pl[k]
                pe.wait(*ready)
                evs = []
                for js in ((0,), (1, 3), (2,)):
                    b = 5 + self.t_next % 2
                    self.t_next += 1
                    pe.wait(*bfree[b])
                    c0, w = self.trow(js[0])[0], 0
                    for j in js:
                        for t in range(j, 4):
                            c = self.cols(t)[0] + 128 * j
                            m = transpose(P[:, b, w:w + 128], pf[:, c:c + 128], IDN[:])
                            w += 128
                    act.wait(m, *self.pt_free[k])
                    hi = copy(act, ph[:, c0:c0 + w], P[:, b, 0:w])
                    dve.wait(hi)
                    lo = diff(dve, pl[:, c0:c0 + w], P[:, b, 0:w], ph[:, c0:c0 + w])
                    bfree[b] = [lo]
                    evs.append(lo)
                self.pf_free[i] = [m]
                self.turned[n] = evs

            def values(self, n, v, first, stop=False):
                k = n % len(self.ph)
                pe.wait(*self.turned[n])
                for j in range(4):
                    c = self.trow(j)
                    o = P[:, 7, 128 * j:512]
                    matmul(o, v(j), self.ph[k][:, c[0]:c[1]], first and j == 0, False)
                    m = matmul(o, v(j), self.pl[k][:, c[0]:c[1]], False, stop and j == 3)
                self.pt_free[k] = [m]
                return m

            fold_free = [[], []]

            def fold(self, h, ev, tmp, both, kt0):
                tf, bf = self.fold_free
                act.wait(ev, *tf)
                c = copy(act, tmp[0:64, :], P[64:128, 7, :])
                dve.wait(c, *(bf if h % 2 == 0 else []))
                own = slice(64 * (h % 2), 64 * (h % 2) + 64)
                a = tt(dve, both[own, :], P[0:64, 7, :], tmp[0:64, :], ALU.add)
                bfree[7] = [a]
                self.fold_free = [[a], bf]
                if h % 2:
                    kt = kt0 + h // 2
                    mix_halves(kt, both[:], a)
                    self.fold_free[1] = [mix_ev[kt]]

        mix_ev = {}

        def mix_halves(kt, src, ev):
            act.wait(ev)
            hi = copy(act, UH[:, kt, :], src)
            dve.wait(ev, hi)
            mix_ev[kt] = diff(dve, UL[:, kt, :], src, UH[:, kt, :])

        def mixer1():
            QS = [at(f"QS{h}", [128, T], F32R, o_a + (6 + 2 * h) * KB) for h in range(8)]
            HS = []
            for i in range(2):
                o = o_a + (6 + 8 * i) * KB
                HS.append((at(f"HQ{i}", [128, T], F32, o), at(f"HK{i}", [128, T], F32, o + 2 * KB),
                           at(f"HT{i}", [128, 1024], F32, o + 4 * KB)))
            KS = [[[at(f"KS{b}{g}{x}", [128, T], F32R, o_a + (22 + 8 * b + 4 * g + 2 * x) * KB) for x in range(2)]
                   for g in range(2)] for b in range(2)]
            CW1 = [at(f"CW1{i}", [128, 16, 128], F32, o_a + (22 + 8 * i) * KB) for i in range(2)]
            VN = at("VN", [128, 4, 4, 128], F32R, o_a + 38 * KB)
            o = o_a + 46 * KB
            KCH = at("KCH", [128, 2, 32], F32R, o)
            KCL = at("KCL", [128, 2, 32], F32R, o + 256)
            VCS = at("VCS", [128, 2, 128], F32R, o + 512)
            GATE = at("GATE", [128, 4, 24], F32, o + 1536)
            QSC = at("QSC", [128, 4, 8], F32, o + 1920)
            QW = at("QW", [128, 3, 32], F32, o_a + 512)
            HV = [at(f"HV{i}", [128, 4, 256], F32, o_a + (48 + 4 * i) * KB) for i in range(2)]
            EV = [at(f"EV{i}", [128, T], F32, o_a + (56 + 2 * i) * KB) for i in range(4)]
            TM = [at(f"TM{i}", [128, T], F32, o_a + (64 + 2 * i) * KB) for i in range(2)]
            o = o_a + 68 * KB
            CWS = [at(f"CWS{i}", [128, 2, 64], F32, o + 512 * i) for i in range(2)]
            ATD = [at(f"ATD{i}", [128, 4, 128], F32, o_u + 16384 * i) for i in range(2)]
            ATO = [at(f"ATO{i}", [128, 768], F32, o_u + 16384 * i + 2048) for i in range(2)]
            CG = [at(f"CG{i}", [128, 5, 64], F32, o_u + 16384 * i + 5120) for i in range(2)]
            GR = at("GR", [128, 2, 128], F32, o_u + 6400)
            G = [at(f"G{h}", [128, T], F32, o_u + 16384 + 2048 * (4 + h)) for h in range(4)]
            KCX = at("KCX", [128, 2, T], F32, o_a + 2 * KB)
            KNB = [(at("KN0", [128, T], F32, o_a + 48 * KB), at("KN1", [128, T], F32, o_a + 50 * KB)),
                   (at("KN2", [128, T], F32, o_a + 2 * KB), at("KN3", [128, T], F32, o_a + 4 * KB))]
            HM = at("HM", [128, 6, 128], F32, CS_off)

            hslot = Slot(semaphore("s_hm"))
            hm_in = act.dma(hslot, lambda e: e.dma_start(HM[:], A["c_hg"]))
            cslot = Slot(semaphore("s_cw"))
            for i, (w1, w2) in enumerate((("cmp_k_w1", "cmp_k_w2"), ("cmp_v_w1", "cmp_v_w2"))):
                src = A[w1][0].rearrange("(a r d) n -> a d r n", a=2, r=16)
                for a in range(2):
                    act.dma(cslot, lambda e, i=i, a=a, src=src: e.dma_start(CW1[i][64 * a:64 * a + 64, :, :], src[a]))
                for a in range(2):
                    cw_in = act.dma(cslot, lambda e, i=i, a=a, w2=w2: e.dma_start(CWS[i][:, a, :], A[w2][0]))

            load_lambdas()

            dve.wait(gt_ready)
            d = tt(dve, SM[:, 40:44], GT[:, 55:59], GT[:, 59:63], ALU.subtract)
            act.wait(d)
            l = activ(LB, SM[:, 40:44], AF.Sigmoid)
            dve.wait(l)
            ts(dve, LB1, LB, -1.0, ALU.mult, 1.0, ALU.add)
            small = ts(dve, QFOLD, GT[:, 49:52], GT[:, 48:49], ALU.mult)
            dve.wait(small)

            ev_free = [[] for _ in range(4)]
            ev_next = [0]

            def ev_take():
                i = ev_next[0] % 4
                ev_next[0] += 1
                return i, EV[i][:]

            def scaled(o, b, ev, free):
                dve.wait(ev, norm["rb"], *free)
                return tt(dve, o, P[:, b, :], RB[:], ALU.mult)

            head_in, v_in, g_in, set_free, v_free = {}, {}, {}, [[], []], [[], []]

            def ev_hqf(h):
                hq, hk, ht = HS[h % 2]

                def evac(i, b, ev):
                    x_i, x = ev_take()
                    y_i, y = ev_take()
                    a = scaled(x, b, ev, ev_free[x_i])
                    bfree[b] = [a]
                    act.wait(a, *ev_free[y_i])
                    s = activ(y, x, AF.Sigmoid)
                    if i == 0:
                        pool.wait(s, *set_free[h % 2])
                        q = tt(pool, hq[:], x, y, ALU.mult)
                        ev_free[x_i], ev_free[y_i] = [q], [q]
                        head_in[h] = [q]
                    else:
                        dve.wait(s, *set_free[h % 2])
                        f = ts(dve, ht[:, 0:T], y, LB1[:, h:h + 1], ALU.mult, LB[:, h:h + 1], ALU.add)
                        dve.wait(f)
                        k = ts(dve, hk[:], ht[:, 0:T], -1.0, ALU.mult, 1.0, ALU.add)
                        ev_free[x_i], ev_free[y_i] = [s], [f]
                        head_in[h] += [k]
                return evac

            def ev_hi(p):
                def evac(tp, b, ev):
                    for q in range(2):
                        t = 2 * tp + q
                        act.wait(ev, norm["rt"], *v_free[p])
                        c = activ(HV[p][:, t, :], P[:, b, 256 * q:256 * q + 256], AF.Identity, scale=RT[:, t:t + 1])
                    bfree[b] = [c]
                    v_in[p] = c
                return evac

            def ev_hg(p):
                def evac(i, b, ev):
                    h = 2 * p + i
                    x_i, x = ev_take()
                    y_i, y = ev_take()
                    a = scaled(x, b, ev, ev_free[x_i])
                    bfree[b] = [a]
                    act.wait(a, *ev_free[y_i])
                    s = activ(y, x, AF.Sigmoid)
                    pool.wait(s)
                    g_in[h] = tt(pool, G[h][:], x, y, ALU.mult)
                    ev_free[x_i], ev_free[y_i] = [g_in[h]], [g_in[h]]
                return evac

            def hgrn(h):
                par, p = h % 2, h // 2
                hq, hk, ht = HS[par]
                atd, ato, tm = ATD[par], ATO[par], TM[par]
                bank, obank = 2 + par, 4 + par
                at_free = hgrn_at[par]
                pool.wait(*at_free)
                z = zero(pool, atd[:])
                q_ev, k_ev, t_ev = head_in[h][0], head_in[h][1], head_in[h][1]
                wrote = z
                for n, lev in enumerate((0, 1, 2, 4, 8, 16, 32, 64)):
                    pe.wait(q_ev, k_ev, *bfree[bank])
                    for j in range(4):
                        m = matmul(P[:, bank, 128 * j:128 * j + 128], hk[:, 128 * j:128 * j + 128],
                                   hq[:, 128 * j:128 * j + 128], True, True)
                    pb = P[:, bank, :].rearrange("p (j t) -> p j t", j=4)
                    if lev <= 16:
                        dve.wait(m, wrote, hm_in)
                        mk = HM[:, n, :].bitcast(U32).unsqueeze(1).to_broadcast([128, 4, 128])
                        wrote = dve(lambda e, mk=mk, pb=pb: e.copy_predicated(atd[:], mk, pb))
                        hm_last[0] = wrote
                    else:
                        act.wait(m, wrote)
                        for r in range(0, 128, 2 * lev):
                            c = copy(act, atd[r:r + lev, :, r + lev:r + 2 * lev], pb[r:r + lev, :, r + lev:r + 2 * lev])
                        wrote = c
                    bfree[bank] = [wrote]
                    if lev == 0:
                        dve.wait(m, q_ev)
                        q_ev = tt(dve, hq[:], hq[:], ht[:, 0:T], ALU.mult)
                    else:
                        q_ev, k_ev, t_ev = double(hq, hk, ht, lev, m, q_ev, k_ev, t_ev)
                    yield 0.82
                pe.wait(q_ev, k_ev, *bfree[bank])
                matmul(P[:, bank, 0:128], hk[:, 0:128], hq[:, 128:256], True, True)
                m = matmul(P[:, bank, 128:256], hk[:, 256:384], hq[:, 384:512], True, True)
                act.wait(m)
                copy(act, ato[:, 0:128], P[:, bank, 0:128])
                wrote2 = copy(act, ato[:, 640:768], P[:, bank, 128:256])
                bfree[bank] = [wrote2]
                q_ev, k_ev, t_ev = double(hq, hk, ht, 128, m, q_ev, k_ev, t_ev)
                yield 0.41
                pe.wait(q_ev, k_ev, *bfree[bank])
                matmul(P[:, bank, 0:256], hk[:, 0:128], hq[:, 256:512], True, True)
                m = matmul(P[:, bank, 256:512], hk[:, 128:256], hq[:, 256:512], True, True)
                set_free[par] = [m]
                act.wait(m)
                wrote2 = copy(act, ato[:, 128:640], P[:, bank, :])
                bfree[bank] = [wrote2]
                yield 0.84
                v = HV[p]
                pe.wait(wrote, wrote2, v_in[p], *bfree[obank])
                for j in range(4):
                    matmul(P[:, obank, 128 * j:128 * j + 128], v[:, j, 128 * par:128 * par + 128], atd[:, j, :], j == 0, False)
                yield 0.82
                for j, (c, n) in enumerate(((0, 384), (384, 256), (640, 128))):
                    m = matmul(P[:, obank, 512 - n:512], v[:, j, 128 * par:128 * par + 128], ato[:, c:c + n], False, j == 2)
                hgrn_at[par] = [m]
                v_free[p].append(m)
                act.wait(m)
                s = activ(tm[:], P[:, obank, :], AF.Square)
                yield 1.26
                pe.wait(s, *bfree[bank])
                m = matmul(P[:, bank, :], ONES[:], tm[:], True, True)
                act.wait(m)
                s = activ(tm[:], P[:, bank, :], AF.Sqrt, scale=1.0 / 128, bias=EPSC)
                bfree[bank] = [s]
                yield 0.85
                dve.wait(s)
                r = recip(tm[:], tm[:])
                dve.wait(r)
                y = stt(dve, tm[:], P[:, obank, :], GT[:, 52:53], tm[:], ALU.mult, ALU.mult)
                bfree[obank] = [y]
                dve.wait(y, g_in[h])
                y = tt(dve, tm[:], tm[:], G[h][:], ALU.mult)
                mix_halves(4 + h, tm[:], y)
                yield 0.0

            hgrn_at = [[], []]

            def double(hq, hk, ht, lev, m, q_ev, k_ev, t_ev):
                nb = T // (2 * lev)
                base = {1: 0, 2: 512, 4: 768, 8: 896, 16: 960, 32: 992, 64: 1008, 128: 1016}[lev]
                nxt = base + 2 * nb
                tv = ht[:, base:base + 2 * nb].rearrange("p (n s) -> p n s", s=2)
                qv = hq[:].rearrange("p (n s l) -> p n s l", s=2, l=lev)
                kv = hk[:].rearrange("p (n s l) -> p n s l", s=2, l=lev)
                pool.wait(m, k_ev, t_ev)
                k2 = tt(pool, kv[:, :, 0, :], kv[:, :, 0, :], tv[:, :, 1:2].to_broadcast([128, nb, lev]), ALU.mult)
                t2 = t_ev
                if lev < 128:
                    t2 = tt(pool, ht[:, nxt:nxt + nb], tv[:, :, 0], tv[:, :, 1], ALU.mult)
                dve.wait(m, q_ev, t_ev)
                q2 = tt(dve, qv[:, :, 1, :], qv[:, :, 1, :], tv[:, :, 0:1].to_broadcast([128, nb, lev]), ALU.mult)
                return q2, k2, t2

            cmp_src, kcx_free = {}, []

            def ev_cmp(i, b, ev):
                x_i, x = ev_take()
                cmp_src[i] = (x, x_i, scaled(x, b, ev, ev_free[x_i]))
                bfree[b] = [cmp_src[i][2]]

            def compress():
                free = [norm["spread"]]
                for i in range(2):
                    x, x_i, ev = cmp_src[i]
                    dve.wait(ev, *free)
                    for g in range(2):
                        r = slice(64 * g, 64 * g + 64)
                        pos = GT[r, 64 + 32 * i:96 + 32 * i]
                        xa = x[r, :].rearrange("p (n s) -> p n s", s=16)
                        ka = KCX[0:64, g, :].rearrange("p (n s) -> p n s", s=16)
                        kb = KCX[64:128, g, :].rearrange("p (n s) -> p n s", s=16)
                        tt(dve, ka, xa, pos[:, 0:16].unsqueeze(1).to_broadcast([64, 32, 16]), ALU.add)
                        c = tt(dve, kb[:, 0:31, :], xa[:, 1:32, :],
                               pos[:, 16:32].unsqueeze(1).to_broadcast([64, 31, 16]), ALU.add)
                    ev_free[x_i] = [c]
                    yield 0.0
                    pe.wait(c, cw_in, *bfree[6])
                    kv = KCX[:].rearrange("p g (n s) -> p g n s", s=16)
                    o = P[:, 6, 0:64].rearrange("p (g n) -> p g n", g=2)[:, :, 0:31]
                    for r in range(16):
                        m = matmul(o, CW1[i][:, r, :], kv[:, :, 0:31, r], r == 0, r == 15)
                        if r % 8 == 7:
                            yield 1.6
                    free = [m]
                    kcx_done[0] = m
                    hs, u, w, th, gl = (CG[i][:, k, :].rearrange("p (g n) -> p g n", g=2) for k in range(5))
                    z = zero(pool, gl)
                    v = slice(0, 31)
                    dve.wait(m)
                    a = copy(dve, hs[:, :, v], o)
                    bfree[6] = [a]
                    dve.wait(a)
                    a = tt(dve, u[:, :, v], hs[:, :, v], hs[:, :, v], ALU.mult)
                    dve.wait(a)
                    a = ts(dve, w[:, :, v], u[:, :, v], 0.044715, ALU.mult, 1.0, ALU.add)
                    dve.wait(a)
                    a = tt(dve, u[:, :, v], w[:, :, v], hs[:, :, v], ALU.mult)
                    act.wait(a)
                    a = activ(th[:, :, v], u[:, :, v], AF.Tanh, scale=float(np.sqrt(2 / np.pi)))
                    dve.wait(a)
                    a = ts(dve, w[:, :, v], th[:, :, v], 1.0, ALU.add, 0.5, ALU.mult)
                    dve.wait(a, z)
                    a = tt(dve, gl[:, :, v], w[:, :, v], hs[:, :, v], ALU.mult)
                    yield 0.0
                    if i == 0:
                        pe.wait(a, *bfree[6])
                        m = matmul(P[:, 6, 0:64], CWS[0][:].rearrange("p a d -> p (a d)"), CG[0][:, 4, :], True, True)
                        act.wait(m)
                        s = activ(CG[0][:, 1, :], P[:, 6, 0:64], AF.Square)
                        yield 0.2
                        pe.wait(s, *bfree[7])
                        m = matmul(P[:, 7, 0:64], BLK[:], CG[0][:, 1, :], True, True)
                        act.wait(m)
                        s = activ(CG[0][:, 2, :], P[:, 7, 0:64], AF.Sqrt, scale=1.0 / 64, bias=EPSC)
                        bfree[7] = [s]
                        dve.wait(s)
                        r_ = recip(CG[0][:, 3, :], CG[0][:, 2, :])
                        dve.wait(r_)
                        y = stt(dve, CG[0][:, 0, :], P[:, 6, 0:64], QFOLD[:, 0:1], CG[0][:, 3, :], ALU.mult, ALU.mult)
                        bfree[6] = [y]
                        act.wait(y)
                        kh = KCH[:].rearrange("p g n -> p (g n)")
                        hi = copy(act, kh, CG[0][:, 0, :])
                        dve.wait(hi)
                        kc_ev[0] = diff(dve, KCL[:].rearrange("p g n -> p (g n)"), CG[0][:, 0, :], kh)
                        yield 0.2
                    else:
                        dve.wait(a)
                        a = copy(dve, GR[:].rearrange("p g (r n) -> p g r n", r=4),
                                 gl.unsqueeze(2).to_broadcast([128, 2, 4, 32]))
                        pe.wait(a, *bfree[6])
                        for g in range(2):
                            m = matmul(P[:, 6, 64 * g:64 * g + 64], GR[:, g, :], CWS[1][:, 0, :], True, True)
                        pv = P[:, 6, 0:128].rearrange("p (g d) -> p g d", g=2)
                        act.wait(m)
                        hi = copy(act, VCS[:, :, 0:64], pv)
                        dve.wait(hi)
                        kc_ev[1] = diff(dve, VCS[:, :, 64:128], pv, VCS[:, :, 0:64])
                        bfree[6] = [kc_ev[1]]
                        yield 0.4

            kc_ev, kcx_done = [None, None], [None]

            ksw_in, ks_ev = {}, {}

            def ev_ksw(i, b, ev):
                kn = KNB[i][0]
                ksw_in[i] = scaled(kn[:], b, ev, v_free[0] if i == 0 else [kcx_done[0]])
                bfree[b] = [ksw_in[i]]

            def nsa_keys():
                for i in range(2):
                    kn, sq = KNB[i]
                    act.wait(ksw_in[i], *(v_free[0] if i == 0 else [kcx_done[0]]))
                    s = activ(sq[:], kn[:], AF.Square)
                    yield 0.0
                    pe.wait(s, *bfree[7])
                    m = matmul(P[:, 7, :], BLK[:], sq[:], True, True)
                    act.wait(m)
                    s = activ(sq[:], P[:, 7, :], AF.Sqrt, scale=1.0 / 64, bias=EPSC)
                    (x_i, ms), (y_i, w) = ev_take(), ev_take()
                    dve.wait(s, *ev_free[x_i], *ev_free[y_i])
                    m = ts(dve, ms, P[:, 7, :], 1.0 / 64, ALU.mult, EPS, ALU.add)
                    bfree[7] = [m]
                    r = rsqrt_step(sq[:], sq[:], ms, w, m)
                    ev_free[x_i], ev_free[y_i] = [r], [r]
                    yield 0.85
                    dve.wait(r)
                    y = stt(dve, kn[:], kn[:], QFOLD[:, 1 + i:2 + i], sq[:], ALU.mult, ALU.mult)
                    act.wait(y)
                    for g in range(2):
                        own = slice(64 * g, 64 * g + 64)
                        other = slice(64 - 64 * g, 128 - 64 * g)
                        hh, ll = KS[i][g]
                        c = copy(act, hh[own, :], kn[own, :])
                        c2 = copy(act, hh[other, :], kn[own, :])
                        dve.wait(y, c)
                        diff(dve, ll[own, :], kn[own, :], hh[own, :])
                        ks_ev[(i, g)] = [c2, diff(dve, ll[other, :], kn[own, :], hh[own, :])]
                        yield 0.0

            vn_ev = [None] * 4

            def ev_vsw(tp, b, ev):
                src = [P[:, b, 256 * q:256 * q + 256].rearrange("p (n d) -> p n d", n=4) for q in range(2)]
                act.wait(ev, norm["rt"])
                for q in range(2):
                    t = 2 * tp + q
                    hi = activ(VN[:, t, :, 0:64], src[q], AF.Identity, scale=RT[:, t:t + 1])
                dve.wait(ev, hi, norm["rt"])
                for q in range(2):
                    t = 2 * tp + q
                    vn_ev[t] = stt(dve, VN[:, t, :, 64:128], src[q], RT[:, t:t + 1], VN[:, t, :, 0:64],
                                   ALU.mult, ALU.subtract)
                bfree[b] = [vn_ev[2 * tp + 1]]

            gate_in, gate_ev = [None], [None]

            def ev_gate(i, b, ev):
                x_i, x = ev_take()
                dve.wait(ev, norm["rb"], *ev_free[x_i])
                a = tt(dve, x[0:24, :], P[0:24, b, :], RB[0:24, :], ALU.mult)
                bfree[b] = [a]
                act.wait(a)
                gate_in[0] = activ(x[0:24, :], x[0:24, :], AF.Sigmoid)
                gate_in.append((x_i, x))

            def gate_turn():
                x_i, x = gate_in[1]
                pe.wait(gate_in[0], *bfree[6])
                for t in range(4):
                    m = transpose(P[:, 6, 24 * t:24 * t + 24], x[0:24, 128 * t:128 * t + 128], IDN[0:24, 0:24])
                ev_free[x_i] = [m]
                dve.wait(m)
                gate_ev[0] = copy(dve, GATE[:].rearrange("p t c -> p (t c)"), P[:, 6, 0:96])
                bfree[6] = [gate_ev[0]]

            q_ev, q_sq = {}, {}

            def ev_q(u):
                def evac(i, b, ev):
                    j = 2 * u + i
                    x_i, x = ev_take()
                    act.wait(ev, *ev_free[x_i])
                    q_sq[j] = (activ(x, P[:, b, :], AF.Square), x, x_i)
                    act.wait(*set_free[0], *set_free[1])
                    copy(act, QS[2 * j][0:64, :], P[0:64, b, :])
                    c = copy(act, QS[2 * j + 1][64:128, :], P[64:128, b, :])
                    dve.wait(c)
                    d = diff(dve, QS[2 * j][64:128, :], P[0:64, b, :], QS[2 * j][0:64, :])
                    q_ev[2 * j] = d
                    d = diff(dve, QS[2 * j + 1][0:64, :], P[64:128, b, :], QS[2 * j + 1][64:128, :])
                    q_ev[2 * j + 1] = d
                    bfree[b] = [d]
                return evac

            def q_sums(j):
                s, x, x_i = q_sq[j]
                pe.wait(s, *(bfree[7] if j == 0 else []))
                for t in range(4):
                    c = 2 * (4 * j + t)
                    m = matmul(P[:, 7, c:c + 2], x[:, 128 * t:128 * t + 128], BLK[:, 0:128:64], True, True)
                ev_free[x_i] = [m]
                return m

            qsc_ev = [None]

            def q_scale(m):
                pq = P[:, 7, 0:32].rearrange("p (j t c) -> p t j c", j=4, t=4)
                w = SM[:, 32:36]
                dve.wait(m, norm["rt"])
                a = tt(dve, w, RT, RT, ALU.mult)
                dve.wait(a)
                qv = QW[:, 0, :].rearrange("p (t j c) -> p t j c", t=4, c=2)
                a = tt(dve, qv, pq, w.unsqueeze(2).unsqueeze(3).to_broadcast([128, 4, 4, 2]), ALU.mult)
                bfree[7] = [a]
                dve.wait(a)
                a = ts(dve, QW[:, 0, :], QW[:, 0, :], 1.0 / 64, ALU.mult, EPS, ALU.add)
                act.wait(a)
                b = activ(QW[:, 1, :], QW[:, 0, :], AF.Sqrt)
                dve.wait(b)
                a = rsqrt_step(QSC[:].rearrange("p t h -> p (t h)"), QW[:, 1, :], QW[:, 0, :], QW[:, 2, :], a)
                a2 = ts(dve, SM[:, 36:40], RT, 0.125, ALU.mult)
                dve.wait(a, a2)
                qsc_ev[0] = tt(dve, QSC[:], QSC[:], SM[:, 36:40].unsqueeze(2).to_broadcast([128, 4, 8]), ALU.mult)

            def main(name, banks, evac=None, **kw):
                return unit_mms(m1[name], banks, xh, xl, evac=evac, **kw)

            g0 = main("hqf0", (2, 3), kouter=True)
            run(g0)
            norm_sums(SQA, 6)
            gen = vunit_mms(m1["hi0"], (0, 1), ev_hi(0))
            run(gen, 3)
            norm["spread"] = norm_spread(DIAG[:], [], 7)
            lambdas()
            e = ev_hqf(0)
            for i in range(2):
                e(i, 2 + i, m1["hqf0"].last[i])
            run(gen)
            run(main("hqf1", (0, 1), ev_hqf(1)))

            def weave(mains, sides, rate=1.0):
                owed = 0.0
                for g in mains:
                    for c in g:
                        owed += c * rate
                        while sides and owed > 0:
                            s = sides.pop(0)
                            got = next(s, None)
                            if got is not None:
                                owed -= max(got, 0.3)
                                sides.append(s)
                while sides and rate >= 99:
                    s = sides.pop(0)
                    if next(s, None) is not None:
                        sides.append(s)

            def drain(sides):
                while sides:
                    s = sides.pop(0)
                    if next(s, None) is not None:
                        sides.append(s)

            sides = [hgrn(0), hgrn(1)]
            run(main("hg0", (0, 1), ev_hg(0)))
            weave([main("cmp", (0, 1), ev_cmp)], sides)
            sides.append(compress())
            weave([main("hqf2", (0, 1), None)], sides)
            drain(sides)
            for i in range(2):
                ev_hqf_2 = ev_hqf(2)
                ev_hqf_2(i, i, m1["hqf2"].last[i])
            run(vunit_mms(m1["hi1"], (0, 1), ev_hi(1)))
            run(main("hqf3", (0, 1), ev_hqf(3)))
            run(main("hg1", (0, 1), ev_hg(1)))
            sides = [hgrn(2), hgrn(3)]
            weave([main("ksw", (0, 1), ev_ksw)], sides)
            sides.append(nsa_keys())
            weave([vunit_mms(m1["vsw"], (0, 1), ev_vsw)], sides)
            weave([main("gate", (0,), ev_gate, ncol=24)], sides)
            drain(sides)
            gate_turn()
            run(main("q0", (0, 1), ev_q(0)))
            q_sums(0)
            q_sums(1)
            run(main("q1", (0, 1), ev_q(1)))
            q_sums(2)
            q_scale(q_sums(3))
            h_last[0] = m1["q1"].last[1]
            PC = at("PC", [128, 4, 8, 32], F32, o_a + 48 * KB)
            EC = at("EC", [128, 4, 8, 32], F32, o_a + 52 * KB)
            PCH = at("PCH", [128, 2, T], F32R, o_a + 56 * KB)
            PCL = at("PCL", [128, 2, T], F32R, o_a + 60 * KB)
            STC = at("STC", [128, 3, 32], F32, o_a)
            ST = at("ST", [128, 4, 16], F32, o_a + 69 * KB)
            ev_done = [s for f in ev_free for s in f]

            def cmp_scores():
                pe.wait(*kc_ev, *bfree[5], *bfree[6], q_ev[7], q_ev[6])
                for t in range(4):
                    b = 5 + t // 2
                    for h in range(8):
                        o = P[:, b, 256 * (t % 2) + 32 * h:256 * (t % 2) + 32 * h + 32]
                        q = QS[h][:, 128 * t:128 * t + 128]
                        matmul(o, q, KCH[:, h // 4, :], True, False)
                        matmul(o, q, KCL[:, h // 4, :], False, False)
                        m = matmul(o, IDB[:], MASKB[:, 3, 32 * t:32 * t + 32], False, True)
                dve.wait(m, qsc_ev[0])
                for i in range(2):
                    pv = P[:, 5 + i, :].rearrange("p (a n) -> p a n", n=32)
                    mx = STC[:, 0, 16 * i:16 * i + 16]
                    ec = EC[:, 2 * i:2 * i + 2].rearrange("p t h n -> p (t h) n")
                    a = dve(lambda e, mx=mx, pv=pv: e.tensor_reduce(mx, pv, AX.X, ALU.max))
                    dve.wait(a)
                    a = tt(dve, ec, pv, mx.unsqueeze(2).to_broadcast([128, 16, 32]), ALU.subtract)
                    bfree[5 + i] = [a]
                    qs = QSC[:, 2 * i:2 * i + 2, :].rearrange("p t h -> p (t h)")
                    pool.wait(a, qsc_ev[0])
                    a = tt(pool, ec, ec, qs.unsqueeze(2).to_broadcast([128, 16, 32]), ALU.mult)
                    act.wait(a)
                    x = activ(ec, ec, AF.Exp)
                    dve.wait(x)
                    sm = STC[:, 1, 16 * i:16 * i + 16]
                    a = dve(lambda e, sm=sm, ec=ec: e.tensor_reduce(sm, ec, AX.X, ALU.add))
                    dve.wait(a)
                    a = recip(STC[:, 2, 16 * i:16 * i + 16], sm)
                    dve.wait(a, gate_ev[0])
                    gt = GATE[:, 2 * i:2 * i + 2, 0:24:3]
                    a = tt(dve, STC[:, 2, 16 * i:16 * i + 16].rearrange("p (t h) -> p t h", t=2),
                           STC[:, 2, 16 * i:16 * i + 16].rearrange("p (t h) -> p t h", t=2), gt, ALU.mult)
                    pool.wait(a, x)
                    pc = PC[:, 2 * i:2 * i + 2].rearrange("p t h n -> p (t h) n")
                    a = tt(pool, ec, ec, STC[:, 2, 16 * i:16 * i + 16].unsqueeze(2).to_broadcast([128, 16, 32]), ALU.mult)
                    pool.wait(a)
                    for t in range(2 * i, 2 * i + 2):
                        a = tt(pool, PC[:, t], EC[:, t],
                               M01[:, 32 * t:32 * t + 32].unsqueeze(1).to_broadcast([128, 8, 32]), ALU.mult)
                    pc_ev[i] = a

            pc_ev, pct_ev = [None, None], [None, None]

            def cmp_turn():
                for g in range(2):
                    pe.wait(*pc_ev, *bfree[5 + g])
                    for t in range(4):
                        m = transpose(P[:, 5 + g, 128 * t:128 * t + 128],
                                      PC[:, t, 4 * g:4 * g + 4, :].rearrange("p h n -> p (h n)"), IDN[:])
                    act.wait(m, *ev_done)
                    hi = copy(act, PCH[:, g, :], P[:, 5 + g, :])
                    dve.wait(hi)
                    pct_ev[g] = diff(dve, PCL[:, g, :], P[:, 5 + g, :], PCH[:, g, :])
                    bfree[5 + g] = [pct_ev[g]]

            PF = [at(f"PF{i}", [128, 1280], F32, o_h + 5 * KB * i) for i in range(2)]
            PH = [at(f"PH{i}", [128, 1280], F32R, o_h + (10 + 5 * i) * KB) for i in range(2)]
            PL = [at(f"PL{i}", [128, 1280], F32R, o_h + (20 + 5 * i) * KB) for i in range(2)]
            items = [(h, b) for h in range(8) for b in range(2)]
            W = attention_forms(PF, PH, PL)
            soft, turned, head_done = {}, {}, {}

            def scores(n):
                h, b = items[n]
                g = h // 4
                hh, ll = KS[b][g]
                pe.wait(q_ev[h], *ks_ev[(b, g)])
                W.scores(QS[h], hh, ll, 0)
                st = ST[:, n % 4, :]
                neg = W.row_max(st, QSC[:, :, h], qsc_ev[0], soft.get(n - 4, []))
                x = W.exps(n, st, QSC, h, neg)
                dve.wait(x)
                a = recip(st[:, 8:12], st[:, 8:12])
                dve.wait(a, gate_ev[0])
                a = tt(dve, st[:, 8:12], st[:, 8:12], GATE[:, :, 3 * h + 1 + b], ALU.mult)
                pool.wait(a, x)
                for t in range(4):
                    c = W.cols(t)
                    p = PF[n % 2][:, c[0]:c[1]]
                    a = tt(pool, p, p, st[:, 8 + t:9 + t].to_broadcast([128, c[1] - c[0]]), ALU.mult)
                soft[n] = [a]

            def turn(n):
                W.turn(n, soft[n])

            def values(n):
                h, b = items[n]
                g = h // 4
                if b == 0:
                    pe.wait(*bfree[7], *vn_ev)
                last = W.values(n, lambda j: VN[:, j, 2 * b + g, :], b == 0)
                if b == 1:
                    pe.wait(pct_ev[g], kc_ev[1])
                    r = slice(32 * (h % 4), 32 * (h % 4) + 32)
                    matmul(P[:, 7, :], VCS[r, g, :], PCH[r, g, :], False, False)
                    last = matmul(P[:, 7, :], VCS[r, g, :], PCL[r, g, :], False, True)
                    W.fold(h, last, TM[0], TM[1], 0)

            def nsa():
                cmp_scores()
                yield 8.0
                for n in range(len(items) + 2):
                    if n < len(items):
                        scores(n)
                        yield 1.4
                    if n == 1:
                        cmp_turn()
                        yield 0.9
                    if 1 <= n <= len(items):
                        turn(n - 1)
                        yield 1.1
                    if n >= 2:
                        values(n - 2)
                        yield 1.6

            def out_tiles(names, kt0, evac):
                for name in names:
                    u = m1[name]
                    o0 = 4 * int(name[-1])

                    def ev(i, b, m, o0=o0):
                        evac(o0 + i, b, m)
                    yield from unit_mms(u, (0, 1, 0, 1), lambda kt: mixh(kt0 + kt), lambda kt: UL[:, kt0 + kt, :], evac=ev)

            def mixh(kt):
                pe.wait(mix_ev[kt])
                return UH[:, kt, :]

            def add_x(o, b, m):
                dve.wait(m, xt_ev[o])
                xt_ev[o] = tt(dve, XT[:, o, :], P[:, b, :], XT[:, o, :], ALU.add)
                bfree[b] = [xt_ev[o]]

            def add_x_last(o, b, m):
                add_x(o, b, m)
                prep_tile(o, xt_ev[o], 8, SQA[:], SQB[:])

            fill = out_tiles(("wh0", "wh1"), 4, add_x)
            owed = 0.0
            for c in nsa():
                owed += c * 0.25
                while owed > 0:
                    d = next(fill, None)
                    if d is None:
                        break
                    owed -= d
            run(fill)
            norm["h"] = {}
            rotary_tables()
            run(out_tiles(("wn0", "wn1"), 0, add_x_last))

        LAMV = at("LAMV", [128, 4, 2, 64], F32, o_u + 16384)

        def load_lambdas():
            for i, n in enumerate(("lam_q1_2", "lam_k1_2", "lam_q2_2", "lam_k2_2")):
                lam_in[0] = act.dma(lamslot, lambda e, i=i, n=n: e.dma_start(
                    LAMV[:, i], A[n].partition_broadcast(128)))

        def lambdas():
            dve.wait(lam_in[0])
            a = tt(dve, LAMV[:, 0], LAMV[:, 0], LAMV[:, 1], ALU.mult)
            b = tt(dve, LAMV[:, 2], LAMV[:, 2], LAMV[:, 3], ALU.mult)
            dve.wait(a, b)
            dve(lambda e: e.tensor_reduce(SM[:, 48:50], LAMV[:, 0], AX.X, ALU.add))
            c = dve(lambda e: e.tensor_reduce(SM[:, 50:52], LAMV[:, 2], AX.X, ALU.add))
            act.wait(c)
            x = activ(SM[:, 52:56], SM[:, 48:52], AF.Exp)
            dve.wait(x)
            a = tt(dve, LAM, SM[:, 52:54], SM[:, 54:56], ALU.subtract)
            dve.wait(a)
            for l in range(2):
                lam_ev[0] = ts(dve, LAM[:, l:l + 1], LAM[:, l:l + 1], 0.8 - 0.6 * float(np.exp(-0.3 * l)), ALU.add)

        def rotary_tables():
            act.wait(hm_last[0])
            for i in range(2):
                cs_in[0] = act.dma(csslot, lambda e, i=i: e.dma_start(CS[:, i, :], A["c_rope"][i]))

        m2 = [{}, {}]

        def plan_mixer2(l):
            w, wo = A["w_in_2"][l], A["w_o_2"][l]
            for part, c in (("s", 0), ("d", 1536)):
                for name in ("qk0", "v0", "qk1", "qk2", "v1", "qk3"):
                    i = int(name[-1])
                    if name[0] == "q":
                        src = [w[:, c + 128 * i:c + 128 * i + 128], w[:, c + 512 + 128 * i:c + 512 + 128 * i + 128]]
                    else:
                        src = [w[:, c + 1024 + 256 * i:c + 1280 + 256 * i]]
                    m2[l][part + name] = plan(src, KT)
            for part, r in (("a", 0), ("b", 512)):
                for i in range(2):
                    m2[l][part + str(i)] = plan([wo[r:r + 512, 512 * i:512 * i + 512]], 4)

        def mixer2(l):
            M = m2[l]
            init = 0.8 - 0.6 * float(np.exp(-0.3 * l))

            def nm(x):
                return f"{x}_{l}"

            o = o_a + 6 * KB
            QSET = [[at(nm(f"QT{i}{x}"), [128, T], F32R, o + (10 * i + 2 * x) * KB) for x in range(2)] for i in range(2)]
            KSET = [[at(nm(f"KT{i}{x}"), [128, T], F32R, o + (10 * i + 4 + 2 * x) * KB) for x in range(2)] for i in range(2)]
            KLO = [at(nm(f"KL{i}"), [128, T], F32R, o + (10 * i + 8) * KB) for i in range(2)]
            o = o_a + 26 * KB
            VSET = [at(nm(f"VS{i}"), [128, 4, 512], F32R, o + 8 * KB * i) for i in range(2)]
            o = o_a + 42 * KB
            E = [at(nm(f"E{i}"), [128, 1280], F32, o + 5 * KB * i) for i in range(2)]
            PH = [at(nm("PH"), [128, 1280], F32R, o + 10 * KB)]
            PL = [at(nm("PL"), [128, 1280], F32R, o + 15 * KB)]
            TMD = at(nm("TMD"), [128, T], F32, o + 20 * KB)
            ST = at(nm("ST"), [128, 4, 16], F32, o + 22 * KB)
            u_at = [o_u + 2048 * i for i in range(8)] + [o_u + 16384 + 2048 * i for i in range(8)]
            EV = [at(nm(f"EV{i}"), [128, T], F32, u_at[k]) for i, k in enumerate((4, 5, 12, 13))]
            TM = [at(nm(f"TM{i}"), [128, T], F32, u_at[k]) for i, k in enumerate((7, 15))]
            RO = [at(nm(f"RO{i}"), [128, T], F32, o_a + 2 * KB * i) for i in range(3)] + [at(nm("RO3"), [128, T], F32, u_at[6])]

            W = attention_forms(E, PH, PL)
            set_free, vset_free = [[], []], [[], []]
            qk_ready, v_ready, have = {}, {}, set()
            ev_free, ev_next = [[] for _ in range(4)], [0]

            def ev_take():
                i = ev_next[0] % 4
                ev_next[0] += 1
                return i, EV[i][:]

            def demand(cond):
                while not cond():
                    next(side)

            def q_halves(dst, src, ev, free):
                act.wait(ev, *free)
                for x in range(2):
                    own = slice(64 * x, 64 * x + 64)
                    c = copy(act, dst[x][own, :], src[own, :])
                dve.wait(ev, c)
                for x in range(2):
                    own, other = slice(64 * x, 64 * x + 64), slice(64 - 64 * x, 128 - 64 * x)
                    d = diff(dve, dst[x][other, :], src[own, :], dst[x][own, :])
                return d

            def k_halves(dst, lo, src, ev, free):
                act.wait(ev, *free)
                for x in range(2):
                    own = slice(64 * x, 64 * x + 64)
                    c = copy(act, dst[x][own, :], src[own, :])
                dve.wait(ev, c)
                for x in range(2):
                    own, other = slice(64 * x, 64 * x + 64), slice(64 - 64 * x, 128 - 64 * x)
                    diff(dve, lo[own, :], src[own, :], dst[x][own, :])
                    d = copy(dve, dst[x][other, :], dst[x][own, :])
                return d

            def ev_sqk(p):
                def evac(i, b, ev):
                    n = p % 2
                    demand(lambda: set_free[n] is not None)
                    x_i, x = ev_take()
                    dve.wait(ev, norm["rb"], *ev_free[x_i])
                    if i == 0:
                        a = stt(dve, x, P[:, b, :], 0.125, RB[:], ALU.mult, ALU.mult)
                        bfree[b] = [a]
                        d = q_halves(QSET[n], x, a, set_free[n])
                        qk_ready[("s", p)] = [d]
                    else:
                        a = tt(dve, x, P[:, b, :], RB[:], ALU.mult)
                        bfree[b] = [a]
                        d = k_halves(KSET[n], KLO[n], x, a, set_free[n])
                        qk_ready[("s", p)] += [d]
                        set_free[n] = None
                        have.add(("s", p))
                    ev_free[x_i] = [d]
                return evac

            def ev_v(part, p):
                def evac(tp, b, ev):
                    demand(lambda: vset_free[p] is not None)
                    vs = VSET[p]
                    act.wait(ev, norm["rt"], *vset_free[p])
                    dv = []
                    for q in range(2):
                        t = 2 * tp + q
                        src = P[:, b, 256 * q:256 * q + 256]
                        if part == "s":
                            src = src.rearrange("p (n d) -> p n d", n=4)
                            dst = vs[:, t, :].rearrange("p (n x d) -> p n x d", n=4, x=2)
                            hi, lo = dst[:, :, 0, :], dst[:, :, 1, :]
                        else:
                            hi, lo = vs[:, t, 0:256], vs[:, t, 256:512]
                        c = activ(hi, src, AF.Identity, scale=RT[:, t:t + 1])
                        dv.append((lo, src, RT[:, t:t + 1], hi))
                    dve.wait(ev, c, norm["rt"])
                    for lo, src, r, hi in dv:
                        d = stt(dve, lo, src, r, hi, ALU.mult, ALU.subtract)
                    bfree[b] = [d]
                    v_ready.setdefault((part, p), []).append(d)
                    if tp == 1:
                        vset_free[p] = None
                        have.add((part + "v", p))
                return evac

            ro_free = [[] for _ in range(4)]
            rslots = [Slot(semaphore(nm(f"s_ro{i}"))) for i in range(1)]

            def ev_dqk(h):
                def evac(i, b, ev):
                    n = h % 2
                    demand(lambda: set_free[n] is not None)
                    r, rr, t1, t2 = RO
                    if i == 0:
                        act.wait(ev, *ro_free[0])
                        a = copy(act, r[:], P[:, b, :])
                    else:
                        dve.wait(ev, norm["rb"], *ro_free[0])
                        a = tt(dve, r[:], P[:, b, :], RB[:], ALU.mult)
                    bfree[b] = [a]
                    act.wait(a, *ro_free[1])
                    for k in range(4):
                        src = 32 * (k ^ 1)
                        m = act.dma(rslots[0], lambda e, k=k, src=src: e.dma_start(rr[32 * k:32 * k + 32, :], r[src:src + 32, :]))
                    dve.wait(a, cs_in[0], *ro_free[2])
                    c = tt(dve, t1[:], r[:], CS[:, 0, :], ALU.mult)
                    pool.wait(m, cs_in[0], *ro_free[3])
                    s = tt(pool, t2[:], rr[:], CS[:, 1, :], ALU.mult)
                    ro_free[0], ro_free[1] = [c, m], [s]
                    dve.wait(c, s)
                    a = tt(dve, t1[:], t1[:], t2[:], ALU.add)
                    ro_free[3] = [a]
                    if i == 0:
                        d = q_halves(QSET[n], t1, a, set_free[n])
                        qk_ready[("d", h)] = [d]
                    else:
                        d = k_halves(KSET[n], KLO[n], t1, a, set_free[n])
                        qk_ready[("d", h)] += [d]
                        set_free[n] = None
                        have.add(("d", h))
                    ro_free[2] = [d]
                return evac

            flat = P[:, 2:5, :].rearrange("p b c -> p (b c)")[:, 0:1280]
            w_ev, s_done = {}, {}

            def sb_scores(h):
                p, x = h // 2, h % 2
                n = p % 2
                pe.wait(*qk_ready[("s", p)])
                m = W.scores2(QSET[n][x], KSET[n][x], KLO[n], x, 1)
                if x == 1:
                    set_free[n] = [m]
                s_done[h] = m

            def sb_soft(h):
                act.wait(s_done[h], *W.pf_free[0])
                bt = activ(E[0][:], flat, AF.Sigmoid)
                act.wait(*W.pf_free[1])
                kp = activ(E[1][:], flat, AF.Sigmoid, scale=-1.0)
                for b in (2, 3, 4):
                    bfree[b] = [kp]
                dve.wait(kp)
                for t in range(4):
                    c0, c1 = W.cols(t)
                    v = E[1][:, slice(c1 - 1, c0 - 1 if c0 else None, -1)]
                    one = ONES[:, 0:1].to_broadcast([128, c1 - c0])
                    s = dve(lambda e, v=v, one=one: e.tensor_tensor_scan(v, v, one, 1.0, ALU.mult, ALU.mult))
                pool.wait(s, bt)
                a = tt(pool, E[0][:, 0:1279], E[0][:, 0:1279], E[1][:, 1:1280], ALU.mult)
                W.pf_free[1] = [a]
                w_ev[h] = a

            def sb_turn(h):
                W.turn(h, [w_ev[h]], 0)

            def sb_values(h):
                p = h // 4
                pe.wait(*bfree[7], *v_ready[("s", p)])
                m = W.values(h, lambda j: VSET[p][:, j, 128 * (h % 4):128 * (h % 4) + 128], True, True)
                if h % 4 == 3:
                    vset_free[p] = [m]
                W.fold(h, m, TM[0], TM[1], 0)

            RT8 = SM[:, 36:40]
            c0_ev, a_ev, df_sum = {}, {}, {}

            def df_scores(h, mp):
                n = h % 2
                pe.wait(*qk_ready[("d", h)])
                m = W.scores2(QSET[n][mp], KSET[n][mp], KLO[n], mp, 2)
                if mp == 1:
                    set_free[n] = [m]

            def df_soft(h, mp):
                st = ST[:, (2 * h + mp) % 4, :]
                neg = W.row_max(st, RT8, rt8[0], df_sum.get((h - 2, mp), []))
                x = W.exps(mp, st, RT8.unsqueeze(2), 0, neg)
                dve.wait(x)
                a = recip(st[:, 8:12], st[:, 8:12])
                if mp == 1:
                    dve.wait(a, lam_ev[0])
                    a = ts(dve, st[:, 8:12], st[:, 8:12], LAM[:, l:l + 1], ALU.mult)
                    pool.wait(a, x)
                    for t in W.ORDER:
                        c = W.cols(t)
                        p = E[1][:, c[0]:c[1]]
                        b = tt(pool, p, p, st[:, 8 + t:9 + t].to_broadcast([128, c[1] - c[0]]), ALU.mult)
                    dve.wait(b, c0_ev[h])
                    st0 = ST[:, (2 * h) % 4, :]
                    for t in W.ORDER:
                        c = W.cols(t)
                        p = E[0][:, c[0]:c[1]]
                        b = stt(dve, p, p, st0[:, 8 + t:9 + t], E[1][:, c[0]:c[1]], ALU.mult, ALU.subtract)
                    W.pf_free[1] = [b]
                    df_sum[(h, 0)] = df_sum[(h, 1)] = [b]
                    a_ev[h] = b
                else:
                    c0_ev[h] = a

            def df_turn(h):
                W.turn(h, [a_ev[h]], 0)

            def df_values(h):
                p = h // 2
                pe.wait(*bfree[7], *v_ready[("d", p)])
                c = 128 * (h % 2)
                m = W.values3(h, lambda j: VSET[p][:, j, c:c + 128], lambda j: VSET[p][:, j, 256 + c:384 + c])
                if h % 2 == 1:
                    vset_free[p] = [m]
                act.wait(m, *tmd_free[0])
                df_sq[h] = activ(TMD[:], P[:, 7, :], AF.Square)

            tmd_free, df_sq = [[]], {}

            def df_norm(h):
                b = 5 + W.t_next % 2
                W.t_next += 1
                pe.wait(df_sq[h], *bfree[b])
                m = matmul(P[:, b, :], ONES[:], TMD[:], True, True)
                act.wait(m)
                s = activ(TMD[:], P[:, b, :], AF.Sqrt, scale=1.0 / 128, bias=EPSC)
                bfree[b] = [s]
                dve.wait(s)
                r = recip(TMD[:], TMD[:])
                dve.wait(r, sln[0])
                y = stt(dve, TMD[:], P[:, 7, :], SM[:, 44 + l:45 + l], TMD[:], ALU.mult, ALU.mult)
                bfree[7] = [y]
                mix_halves(4 + h, TMD[:], y)
                tmd_free[0] = [mix_ev[4 + h]]

            def attention():
                for n in range(8 + 2):
                    if n < 8:
                        while ("s", n // 2) not in have:
                            yield None
                        sb_scores(n)
                        yield 1.4
                    if n >= 2:
                        while ("sv", (n - 2) // 4) not in have:
                            yield None
                        sb_values(n - 2)
                        yield 1.2
                    if 1 <= n <= 8:
                        sb_turn(n - 1)
                        yield 1.1
                    if n < 8:
                        sb_soft(n)
                for n in range(4 + 2):
                    if n < 4:
                        while ("d", n) not in have:
                            yield None
                        df_scores(n, 0)
                        yield 1.4
                    if n >= 2:
                        while ("dv", (n - 2) // 2) not in have:
                            yield None
                        df_values(n - 2)
                        yield 1.8
                    if 1 <= n <= 4:
                        df_turn(n - 1)
                        yield 1.1
                    if n < 4:
                        df_soft(n, 0)
                        df_scores(n, 1)
                        yield 1.4
                        df_soft(n, 1)
                    if n >= 2:
                        df_norm(n - 2)
                        yield 0.9

            side = attention()
            owed = [0.0]

            def weave(gen, rate):
                for c in gen:
                    owed[0] += c * rate
                    while owed[0] > 0:
                        d = next(side, "end")
                        if d is None or d == "end":
                            owed[0] = 0.0
                            break
                        owed[0] -= d

            def unit(name, banks, evac, **kw):
                return unit_mms(M[name], banks, xh, xl, evac=evac, **kw)

            run(unit("sqk0", (2, 3), None, kouter=True))
            norm_sums(SQA, 6)
            gen = vunit_mms(M["sv0"], (0, 1), ev_v("s", 0))
            run(gen, 3)
            norm_spread(DIAG[:], [], 7)
            dve.wait(norm["rt"])
            rt8 = [ts(dve, RT8, RT, 0.125, ALU.mult)]
            sln = [ts(dve, SM[:, 44 + l:45 + l], GT[:, 53 + l:54 + l], 1.0 - init, ALU.mult)]
            e = ev_sqk(0)
            for i in range(2):
                e(i, 2 + i, M["sqk0"].last[i])
            run(gen)
            weave(unit("sqk1", (0, 1), ev_sqk(1)), 0.4)
            for part in "sd":
                if part == "d":
                    weave(unit("dqk0", (0, 1), ev_dqk(0)), RATE)
                    weave(vunit_mms(M["dv0"], (0, 1), ev_v("d", 0)), RATE)
                    weave(unit("dqk1", (0, 1), ev_dqk(1)), RATE)
                qk = ev_sqk if part == "s" else ev_dqk
                weave(unit(part + "qk2", (0, 1), qk(2)), RATE)
                weave(vunit_mms(M[part + "v1"], (0, 1), ev_v(part, 1)), RATE)
                weave(unit(part + "qk3", (0, 1), qk(3)), RATE)
            h_last[0] = M["dqk3"].last[1]

            def mixh(kt):
                pe.wait(mix_ev[kt])
                return UH[:, kt, :]

            def out_tiles(part, kt0, evac):
                for i in range(2):
                    yield from unit_mms(M[part + str(i)], (0, 1, 0, 1), lambda kt: mixh(kt0 + kt),
                                        lambda kt: UL[:, kt0 + kt, :],
                                        evac=lambda k, b, m, i=i: evac(4 * i + k, b, m))

            def add_x(o, b, m):
                dve.wait(m, xt_ev[o])
                xt_ev[o] = tt(dve, XT[:, o, :], P[:, b, :], XT[:, o, :], ALU.add)
                bfree[b] = [xt_ev[o]]

            def add_x_last(o, b, m):
                add_x(o, b, m)
                prep_tile(o, xt_ev[o], 32 + 8 * l, SQA[:], SQB[:])

            weave(out_tiles("a", 0, add_x), RATE_W)
            for _ in side:
                pass
            norm["h"] = {}
            run(out_tiles("b", 4, add_x_last))

        RATE, RATE_W = 0.9, 1.2
        lamslot, lam_in = Slot(semaphore("s_lam")), [None]
        csslot = Slot(semaphore("s_cs"))
        cs_in, hm_last, lam_ev = [None], [None], [None]
        for l in range(2):
            plan_mixer2(l)
            if l == 0:
                p2 = [plan_ffn2(0)]
        p2.append(plan_ffn2(1))
        def phases():
            mixer1()
            ffn(8, p1, (8, 8, 6), True, False, 16)
            mixer2(0)
            ffn(32, p2[0], (8, 8, 8, 8), False, False, 24)
            mixer2(1)
            ffn(40, p2[1], (8, 8, 8, 8), False, True, None)

        phases()

        for lane in lanes:
            lane.number()
        block = ctx.enter_context(nc.Block())

        @block.tensor
        def _(e):
            pe.play(e)

        @block.scalar
        def _(e):
            act.play(e)

        @block.vector
        def _(e):
            dve.play(e)

        @block.gpsimd
        def _(e):
            pool.play(e)

        @block.sync
        def _(e):
            sp.play(e)


def constants():
    i = np.arange(128)
    t, s = i[:, None], i[None, :]
    c = np.zeros((128, 1024), np.float32)
    c[:, 0:128] = (t // 64 == s // 64)
    c[:, 128:256] = np.where(s <= t, 0, NEG)
    c[:, 256:384] = np.where(s < t, 0, NEG)
    c[:, 384:512] = np.where(s // 64 <= t // 64, 0, NEG)
    tok = 128 * (np.arange(128) // 32)[None, :] + t
    n = (np.arange(128) % 32)[None, :]
    seen = (16 * n + 31 <= tok) & (n < 31)
    c[:, 512:640] = np.where(seen, 0, NEG)
    c[:, 640:768] = seen
    d = np.arange(0, 64, 2, dtype=np.float32)
    inv = (np.float32(1.0) / (np.float32(10000.0) ** (d / np.float32(64)))).astype(np.float32)
    ang = np.arange(T, dtype=np.float32)[None, :] * inv[i % 32][:, None]
    rope = np.stack([np.cos(ang), np.where(t % 64 < 32, -1, 1) * np.sin(ang)]).astype(np.float32)
    hg = np.zeros((128, 6, 128), np.float32)
    hg[:, 0, :] = np.eye(128)
    for n, h in enumerate((1, 2, 4, 8, 16)):
        a, b = t, s
        hg[:, n + 1, :] = (a // (2 * h) == b // (2 * h)) & (a // h % 2 == 0) & (b // h % 2 == 1)
    return {"c_rope": rope, "c_hg": hg, "c_idn": np.eye(128, dtype=np.float32), "c_small": c}


_INS = ["x", "norm_mix", "w_in", "q_norm", "k_norm", "cmp_pos_k", "cmp_pos_v", "cmp_k_w1", "cmp_k_w2", "cmp_v_w1",
        "cmp_v_w2", "hgrn_lb_logits", "hgrn_o_norm", "w_out", "norm_ffn", "w_gate_up", "w_down", "w_in_2", "w_o_2",
        "attn_norm_2", "subln_norm_2", "lam_q1_2", "lam_k1_2", "lam_q2_2", "lam_k2_2", "mlp_norm_2", "w_ff1_2",
        "w_ff2_2", "final_norm_2"]
_OUTS = [((1, 512, 1024), "float32")]


def kernel(**inputs):
    import numpy as _np
    import concourse.bacc as _bacc
    from concourse import mybir as _mybir
    from concourse.bass_utils import run_bass_kernel_spmd as _run

    nc = _bacc.Bacc("TRN2", target_bir_lowering=False, num_devices=1)
    given = {name: inputs[name] for name in _INS}
    given.update(constants())
    arrays, aps = {}, {}
    for name, value in given.items():
        a = _np.ascontiguousarray(value)
        arrays[f"in_{name}_dram"] = a
        aps[name] = nc.dram_tensor(f"in_{name}_dram", a.shape, _mybir.dt.from_np(a.dtype), kind="ExternalInput").ap()
    shape, dtype = _OUTS[0]
    out = nc.dram_tensor("out_0_dram", shape, _mybir.dt.from_np(_np.dtype(dtype)), kind="ExternalOutput").ap()
    program(nc, aps, out)
    r = _run(nc, [arrays], core_ids=[0])
    return r.results[0]["out_0_dram"]
```

```python
import numpy as np
import concourse.bass as bass
from concourse import mybir
from concourse.alu_op_type import AluOpType as ALU
from contextlib import ExitStack

F32 = mybir.dt.float32
F32R = mybir.dt.float32r
BF16 = mybir.dt.bfloat16
U32 = mybir.dt.uint32
AF = mybir.ActivationFunctionType
AX = mybir.AxisListType

T = 512
D = 1024
KT = D // 128
NEG = -1e30
EPS = 1e-6
D_FF = 2816
D_FF2 = 4096


class Step:

    def __init__(self, end, sem=None, value=None):
        self.end, self.sem, self.value, self.signals = end, sem, value, False


class Slot:

    def __init__(self, sem):
        self.sem, self.count = sem, 0


class Lane:
    dma_end = 0.0

    def __init__(self, sem, hop):
        self.sem, self.hop, self.items, self.clock, self.ready = sem, hop, [], 0.0, 0.0

    def __call__(self, fn, cost):
        self.clock = max(self.clock, self.ready) + cost
        self.ready = 0.0
        step = Step(self.clock)
        self.items.append((step, fn))
        return step

    def wait(self, *steps):
        for s in steps:
            if s is not None:
                s.signals = True
                self.ready = max(self.ready, s.end + self.hop)
                self.items.append((s, None))

    def dma(self, slot, fn, cost):
        slot.count += 16
        self.clock = max(self.clock, self.ready) + 0.05
        self.ready = 0.0
        Lane.dma_end = max(self.clock + 1.6, Lane.dma_end) + cost
        step = Step(Lane.dma_end + 1.6, slot.sem, slot.count)
        self.items.append((step, fn))
        return step

    def number(self):
        n = 0
        for step, fn in self.items:
            if fn is not None and step.sem is None and step.signals:
                n += 1
                step.sem, step.value = self.sem, n

    def play(self, eng):
        seen = {}
        for step, fn in self.items:
            if fn is None:
                if seen.get(step.sem.name, 0) < step.value:
                    eng.wait_ge(step.sem, step.value)
                    seen[step.sem.name] = step.value
                continue
            ins = fn(eng)
            if step.sem is not None:
                ins.then_inc(step.sem, 1 if step.sem is self.sem else 16)


class Hold:

    def __init__(self):
        self.free = []

    def give(self, *steps):
        self.free = list(steps)


class Tasks:

    LOOK = 0.35
    SLACK = 0.0

    def __init__(self):
        self.now, self.queue, self.parked, self.count = 0.0, [], [], 0

    def push(self, time, task, lane=None):
        self.count += 1
        self.queue.append((max(time, self.now), self.count, task, lane))

    def start(self, task, *after):
        self.push(max([s.end for s in after if s is not None], default=0.0), task)

    def run(self):
        while self.queue:
            first = min(self.queue, key=lambda q: q[:2])
            self.queue.remove(first)
            self.now, _, task, lane = first
            if lane is not None and lane.clock - self.LOOK > self.now:
                self.push(lane.clock - self.LOOK, task, lane)
                continue
            try:
                got = next(task)
            except StopIteration:
                got = ()
                task = None
            if task is None:
                pass
            elif isinstance(got, Lane):
                self.push(got.clock - self.LOOK, task, got)
            elif callable(got):
                self.parked.append((got, task))
            else:
                got = got if isinstance(got, (tuple, list)) else (got,)
                self.push(max([s.end + self.SLACK for s in got if s is not None], default=0.0), task)
            still = []
            for cond, t in self.parked:
                if cond():
                    self.push(self.now, t)
                else:
                    still.append((cond, t))
            self.parked = still
        assert not self.parked, "tasks wait for each other"


def take(*holds):
    while not all(h.free is not None for h in holds):
        yield lambda: all(h.free is not None for h in holds)
    got = [s for h in holds for s in h.free]
    for h in holds:
        h.free = None
    yield got
    return got


def take_one(holds):
    while not any(h.free is not None for h in holds):
        yield lambda: any(h.free is not None for h in holds)
    h = min((h for h in holds if h.free is not None), key=lambda h: max([s.end for s in h.free if s is not None], default=0.0))
    got, h.free = h.free, None
    yield got
    return h, got


def program(nc, A, out):
    ctx = ExitStack()
    with ctx:
        def semaphore(name):
            return ctx.enter_context(nc.semaphore(name))

        pe, act, dve, pool, sp = (Lane(semaphore(n), hop) for n, hop in (
            ("s_pe", 0.25), ("s_act", 0.18), ("s_dve", 0.18), ("s_pool", 0.18), ("s_sp", 0.1)))
        lanes = (pe, act, dve, pool, sp)
        Lane.dma_end = 0.0
        tasks = Tasks()
        start = tasks.start

        base = (nc.sbuf_base + 63) // 64 * 64
        room = nc.sbuf_usable_end - base

        def at(name, shape, dt, off):
            size = int(np.prod(shape[1:])) * mybir.dt.size(dt)
            assert off % 32 == 0 and off + size <= room, (name, off, size, room)
            return nc.alloc_sbuf_tensor_at(name, shape, dt, offset=base + off)

        KB = 1024
        NR, NS = 2, 4
        o_x = 0
        o_h = o_x + 16384
        o_raw = o_h + 32768
        o_ws = o_raw + NR * 8192
        o_u = o_ws + NS * 8192
        o_c = o_u + 32768
        XT = at("XT", [128, KT, T], F32, o_x)
        HH = at("HH", [128, KT, T], F32R, o_h)
        HL = at("HL", [128, KT, T], F32R, o_h + 16384)
        RAW = at("RAW", [128, NR, 2048], F32, o_raw)
        WH = at("WH", [128, NS, 1024], F32R, o_ws)
        WL = at("WL", [128, NS, 1024], F32R, o_ws + NS * 4096)
        UH = at("UH", [128, KT, T], F32R, o_u)
        UL = at("UL", [128, KT, T], F32R, o_u + 16384)
        P = ctx.enter_context(nc.psum_tensor("ps", [128, 8, 512], F32))

        off = [o_c]

        def const(name, shape, dt):
            t = at(name, shape, dt, off[0])
            off[0] += (int(np.prod(shape[1:])) * mybir.dt.size(dt) + 31) // 32 * 32
            return t

        BM = const("BM", [128, 384], F32)
        IDN, BLK, M01 = BM[:, 0:128], BM[:, 128:256], BM[:, 256:384]
        IDB = const("IDB", [128, 128], BF16)
        ONES = const("ONES", [128, 128], F32)
        MASKB = const("MASKB", [128, 4, 128], BF16)
        GT = const("GT", [128, 128], F32)
        CS_off = off[0]
        CS = const("CS", [128, 2, T], F32)
        RB = const("RB", [128, T], F32)
        SM = const("SM", [128, 64], F32)
        RT = SM[:, 0:4]
        STD = SM[:, 4:8]
        EPSC = SM[:, 8:9]
        LB = SM[:, 12:16]
        LB1 = SM[:, 16:20]
        QFOLD = SM[:, 20:23]
        LAM = SM[:, 24:26]
        MS = SM[:, 28:32]
        NW = SM[:, 60:64]
        o_a = (off[0] + 63) // 64 * 64

        def cols(a):
            return int(np.prod(a.shape[1:]))

        def matmul(o, l, r, start, stop):
            n = cols(r)
            if r.dtype == F32:
                c = max(0.2, n * 1.65e-3)
            else:
                c = max(0.053 if r.dtype == BF16 else 0.103, n * 0.417e-3)
            return pe(lambda e: e.matmul(o, l, r, start=start, stop=stop), c)

        def transpose(o, i, ident):
            return pe(lambda e: e.transpose(o, i, ident), 0.107)

        def vcost(lane, n, fast=False):
            if lane is dve:
                return 0.06 + n * (0.52e-3 if fast else 1.04e-3)
            if lane is pool:
                return 0.2 + n * 2e-3
            return 0.17 + n * 0.7e-3

        def tt(lane, o, a, b, op):
            return lane(lambda e: e.tensor_tensor(o, a, b, op), vcost(lane, cols(o)))

        def ts(lane, o, a, s1, op0, s2=None, op1=None):
            c = vcost(lane, cols(o), True)
            if op1 is None:
                return lane(lambda e: e.tensor_scalar(o, a, s1, None, op0), c)
            return lane(lambda e: e.tensor_scalar(o, a, s1, s2, op0, op1), c)

        def stt(lane, o, a, s, b, op0, op1):
            return lane(lambda e: e.scalar_tensor_tensor(o, a, s, b, op0, op1), vcost(lane, cols(o)) + 0.06)

        def copy(lane, o, a):
            c = vcost(lane, cols(o), True)
            if lane is act:
                return lane(lambda e: e.copy(o, a), c)
            return lane(lambda e: e.tensor_copy(o, a), c)

        table = [None]

        def activ(o, a, func, scale=1.0, bias=None, accum=None):
            kw = {}
            if bias is not None:
                kw["bias"] = bias
            if accum is not None:
                kw["accum_out"] = accum
            c = 0.2 + cols(o) * 0.72e-3
            kind = AF.Exp if func == AF.Ln else func
            if kind not in (AF.Identity, AF.Square, table[0]):
                table[0] = kind
                c += 1.3
            return act(lambda e: e.activation(o, a, func, scale=scale, **kw), c)

        def scale_rows(o, a, col):
            n = cols(o)
            if dve.clock + vcost(dve, n, True) <= pool.clock + vcost(pool, n):
                return dve, lambda: ts(dve, o, a, col, ALU.mult)
            return pool, lambda: tt(pool, o, a, col.to_broadcast([128, n]), ALU.mult)

        def recip(o, a):
            return dve(lambda e: e.reciprocal(o, a), 0.06 + cols(o) * 6.3e-3)

        def zero(lane, o):
            return lane(lambda e: e.memset(o, 0.0), 0.46)

        def diff(lane, o, a, b):
            return tt(lane, o, a, b, ALU.subtract)

        def dma(lane, slot, o, i):
            return lane.dma(slot, lambda e: e.dma_start(o, i), int(np.prod(o.shape)) * 4 / 350e3)

        bank = [Hold() for _ in range(8)]
        for b in range(8):
            bank[b].i = b

        class Unit:
            pass

        units = []

        def plan(src_cols, nk):
            u = Unit()
            u.src, u.nk, u.arrived = src_cols, nk, None
            u.width = sum(s.shape[-1] for s in src_cols)
            u.half = u.width // 2 if u.width > 128 else u.width
            u.slots, u.ready = [], [None] * (u.width // u.half)
            u.i = len(units)
            units.append(u)
            return u

        wslots = [Slot(semaphore(f"s_w{i}")) for i in range(NR)]
        raw = [Hold() for _ in range(NR)]
        wslot = [Hold() for _ in range(NS)]
        loads = [0]
        small_loads = {}

        def pump():
            while loads[0] < len(units) and raw[loads[0] % NR].free is not None:
                u = units[loads[0]]
                r = u.i % NR
                sp.wait(*raw[r].free)
                raw[r].free = None
                c = 0
                for s in u.src:
                    w = s.shape[-1]
                    dst = RAW[:, r, 0:u.nk * u.width].rearrange("p (k c) -> p k c", k=u.nk)[:, :, c:c + w]
                    u.arrived = dma(sp, wslots[r], dst, s.rearrange("(k p) c -> p k c", p=128))
                    c += w
                loads[0] += 1
                if u.i in small_loads:
                    small_loads[u.i]()

        def splitter():
            for u in units:
                r = u.i % NR
                while u.arrived is None:
                    yield lambda: u.arrived is not None
                rv = RAW[:, r, 0:u.nk * u.width].rearrange("p (k c) -> p k c", k=u.nk)
                for t in range(u.width // u.half):
                    s = (2 * u.i + t) % NS
                    u.slots.append(s)
                    hv = WH[:, s, 0:u.nk * u.half].rearrange("p (k c) -> p k c", k=u.nk)
                    lv = WL[:, s, 0:u.nk * u.half].rearrange("p (k c) -> p k c", k=u.nk)
                    src = rv[:, :, t * u.half:(t + 1) * u.half]
                    got = yield from take(wslot[s])
                    yield u.arrived
                    yield act
                    act.wait(u.arrived, *got)
                    h = copy(act, hv, src)
                    yield h
                    n = cols(hv)
                    lane = dve if dve.clock + vcost(dve, n) <= pool.clock + vcost(pool, n) else pool
                    yield lane
                    lane.wait(h)
                    u.ready[t] = diff(lane, lv, src, hv)
                raw[r].give(*u.ready)
                pump()

        def wtile(u, n):
            per = max(1, u.half // 128)
            return n // per, (n % per) * 128

        class Halves:

            def __init__(self, hi, lo):
                self.hi, self.lo, self.ev, self.used = hi, lo, {}, {}

        H, U = Halves(HH, HL), Halves(UH, UL)

        def unit(u, src, ring, evac, k0=0, kouter=False, ncol=128):
            n = (u.width + 127) // 128
            tiles = [(i, kt) for kt in range(u.nk) for i in range(n)] if kouter else \
                    [(i, kt) for i in range(n) for kt in range(u.nk)]
            held = [None] * n
            for i, kt in tiles:
                t, c0 = wtile(u, i)
                if kt == 0:
                    held[i] = yield from take_one(ring)
                while u.ready[t] is None or k0 + kt not in src.ev:
                    yield lambda: u.ready[t] is not None and k0 + kt in src.ev
                yield u.ready[t], src.ev[k0 + kt]
                yield pe
                s, b = u.slots[t], held[i][0].i
                a = kt * u.half + c0
                wh, wl = WH[:, s, a:a + ncol], WL[:, s, a:a + ncol]
                o = P[0:ncol, b, :]
                h, l = src.hi[:, k0 + kt, :], src.lo[:, k0 + kt, :]
                if kt == 0:
                    pe.wait(*held[i][1])
                pe.wait(u.ready[t], src.ev[k0 + kt])
                matmul(o, wh, h, kt == 0, False)
                matmul(o, wh, l, False, False)
                src.used[k0 + kt] = m = matmul(o, wl, h, False, kt == u.nk - 1)
                if kt == u.nk - 1:
                    if i == n - 1 or wtile(u, i + 1)[0] != t:
                        wslot[s].give(m)
                    start(evac(i, held[i][0], m), m)

        def vunit(u, ring, evac):
            for tp in range(2):
                b, got = yield from take_one(ring)
                for q in range(2):
                    t = 2 * tp + q
                    o = P[:, b.i, 256 * q:256 * q + 256]
                    for kt in range(KT):
                        while None in u.ready:
                            yield lambda: None not in u.ready
                        yield u.ready
                        yield pe
                        s = u.slots[0]
                        w = slice(128 * kt, 128 * kt + 128)
                        wh, wl = WH[:, s:s + 2, w], WL[:, s:s + 2, w]
                        h, l = HH[:, kt, 128 * t:128 * t + 128], HL[:, kt, 128 * t:128 * t + 128]
                        if q == 0 and kt == 0:
                            pe.wait(*got)
                        pe.wait(H.ev[kt], *u.ready)
                        matmul(o, h, wh, kt == 0, False)
                        matmul(o, h, wl, False, False)
                        H.used[kt] = m = matmul(o, l, wh, False, kt == KT - 1)
                if tp == 1:
                    wslot[s].give(m)
                    wslot[s + 1].give(m)
                start(evac(tp, b, m), m)

        class Norm:

            def __init__(self):
                self.n, self.done, self.rt, self.rb = 0, 0, None, None

        norms = []
        rt_read, rb_read = {}, {}
        SQA = at("SQA", [128, T], F32, o_a)
        SQ = [at("SQ0", [128, T], F32, o_a + 2048), at("SQ1", [128, T], F32, o_a + 4096)]
        DIAG = at("DIAG", [128, T], F32, o_a + 4096)
        sqa, sq = Hold(), [Hold(), Hold()]

        def has_rt(norm):
            while norm.rt is None:
                yield lambda: norm.rt is not None
            yield norm.rt

        def has_rb(norm):
            while norm.rb is None:
                yield lambda: norm.rb is not None
            yield norm.rb

        def new_norm():
            norms.append(Norm())
            H.ev = {}

        def prep_tile(kt, ev, g0, x=None):
            x = XT[:, kt, :] if x is None else x
            norm = norms[-1]
            g = GT[:, g0 + kt:g0 + kt + 1]
            act.wait(ev, H.used.get(kt))
            hi = activ(HH[:, kt, :], x, AF.Identity, scale=g)
            yield hi
            dve.wait(ev, hi)
            H.ev[kt] = stt(dve, HL[:, kt, :], x, g, HH[:, kt, :], ALU.mult, ALU.subtract)
            norm.n += 1
            if norm.n == 1:
                got = yield from take(sqa)
                yield act
                act.wait(ev, *got)
                s = activ(SQA[:], x, AF.Square)
                sqa.give(s)
                last = [s]
            else:
                i = norm.n % 2
                got = yield from take(sq[i])
                yield act
                act.wait(ev, *got)
                s = activ(SQ[i][:], x, AF.Square)
                last = [s]
                yield s
                got = yield from take(sqa)
                lane = dve if norm.done == KT - 1 else pool
                lane.wait(s, *got)
                a = tt(lane, SQA[:], SQA[:], SQ[i][:], ALU.add)
                sqa.give(a)
                sq[i].give(a)
            norm.done += 1
            if norm.done == KT:
                start(norm_sums(norm), *sqa.free)
            return last

        def norm_sums(norm):
            got = yield from take(sqa)
            b, bgot = yield from take_one(bank[6:8])
            pe.wait(*got, *bgot)
            for t in range(4):
                m = matmul(P[:, b.i, 2 * t:2 * t + 2], SQA[:, 128 * t:128 * t + 128], ONES[:, 0:2], True, True)
            sqa.give(m)
            yield m
            act.wait(m, *rt_read.values())
            s = activ(STD, P[:, b.i, 0:8:2], AF.Sqrt, scale=1.0 / D, bias=EPSC)
            yield s
            dve.wait(s)
            m = ts(dve, MS, P[:, b.i, 0:8:2], 1.0 / D, ALU.mult, EPS, ALU.add)
            b.give(m)
            dve.wait(*rt_read.values())
            rt = rsqrt_step(RT, STD, MS, NW, m)
            dve.wait(rt)
            for t in range(4):
                d = ts(dve, DIAG[:, 128 * t:128 * t + 128], IDN, RT[:, t:t + 1], ALU.mult)
            norm.rt = d
            yield d
            b, bgot = yield from take_one(bank[6:8])
            pe.wait(d, *bgot)
            m = matmul(P[:, b.i, :], ONES[:], DIAG[:], True, True)
            yield m
            act.wait(m, *rb_read.values())
            norm.rb = copy(act, RB[:], P[:, b.i, :])
            b.give(norm.rb)

        def rsqrt_step(y, std, ms, w, ms_ev):
            a = recip(y, std)
            dve.wait(a, ms_ev)
            a = tt(dve, w, y, y, ALU.mult)
            dve.wait(a)
            a = tt(dve, w, w, ms, ALU.mult)
            dve.wait(a)
            a = ts(dve, w, w, -0.5, ALU.mult, 1.5, ALU.add)
            dve.wait(a)
            return tt(dve, y, y, w, ALU.mult)

        cslot, gslot, mslot = (Slot(semaphore(n)) for n in ("s_const", "s_vec", "s_mask"))
        xslots = [Slot(semaphore(f"s_x{i}")) for i in range(2)]
        XIN = at("XIN", [128, 4, D], F32, o_u)
        MIN = at("MIN", [128, 512], F32, o_a + 38 * KB)
        HM = at("HM", [128, 6, 128], F32, CS_off)
        CW1 = [at(f"CW1{i}", [128, 16, 128], F32, o_a + (22 + 8 * i) * KB) for i in range(2)]
        CWS = [at(f"CWS{i}", [128, 2, 64], F32, o_a + 68 * KB + 512 * i) for i in range(2)]
        LAMV = at("LAMV", [128, 4, 2, 64], F32, o_a + 40 * KB)
        x_in, got_in = {}, {}

        def load_x(half):
            c = slice(512 * half, 512 * half + 512)
            x_in[half] = dma(sp, xslots[half], XIN[:, :, c], A["x"][0].rearrange("(t p) d -> p t d", p=128)[:, :, c])

        def load_masks():
            got_in["mask"] = dma(sp, mslot, MIN[:], A["c_mask"])
            got_in["hm"] = dma(sp, Slot(semaphore("s_hm")), HM[:], A["c_hg"])

        wc_slot = [Slot(semaphore(f"s_cw{i}")) for i in range(2)]

        def load_cmp(i):
            src = A[("cmp_k_w1", "cmp_v_w1")[i]][0].rearrange("(a r d) n -> a d r n", a=2, r=16)
            for a in range(2):
                dma(sp, wc_slot[i], CW1[i][64 * a:64 * a + 64, :, :], src[a])
            for a in range(2):
                got_in[("cw", i)] = dma(sp, wc_slot[i], CWS[i][:, a, :], A[("cmp_k_w2", "cmp_v_w2")[i]][0])

        def load_lambdas():
            got_in["lam"] = dma(sp, Slot(semaphore("s_lam")), LAMV[:].rearrange("p a l d -> p (a l d)"),
                                A["p_lam"].partition_broadcast(128))

        small_loads.update({0: lambda: load_x(1), 1: load_masks, 2: lambda: load_cmp(0), 3: lambda: load_cmp(1),
                            4: load_lambdas})

        def opening():
            gt = got_in["gt"]
            ones = pool(lambda e: e.memset(ONES[:], 1.0), 0.3)
            eps = pool(lambda e: e.memset(EPSC, EPS), 0.1)
            act.wait(gt, eps)
            dve.wait(gt, eps, got_in["idn"])
            pool.wait(gt, got_in["idn"])
            pe.wait(ones, got_in["idn"])
            for kt in range(KT):
                b, got = yield from take_one(bank[0:6])
                yield x_in[kt // 4]
                pe.wait(x_in[kt // 4], *got)
                for t in range(4):
                    m = transpose(P[:, b.i, 128 * t:128 * t + 128], XIN[:, t, 128 * kt:128 * kt + 128], IDN)
                start(x_tile(kt, b, m), m)

        def small_things():
            copy(dve, IDB[:], IDN)
            while "mask" not in got_in:
                yield lambda: "mask" in got_in
            yield got_in["mask"]
            dve.wait(got_in["mask"])
            got_in["maskb"] = copy(dve, MASKB[:].rearrange("p a b -> p (a b)"), MIN[:])
            d = tt(dve, SM[:, 40:44], GT[:, 55:59], GT[:, 59:63], ALU.subtract)
            act.wait(d)
            l = activ(LB, SM[:, 40:44], AF.Sigmoid)
            dve.wait(l)
            ts(dve, LB1, LB, -1.0, ALU.mult, 1.0, ALU.add)
            q = ts(dve, QFOLD, GT[:, 49:52], GT[:, 48:49], ALU.mult)
            dve.wait(q)
            got_in["small"] = q

        def x_tile(kt, b, m):
            lane = dve
            lane.wait(m)
            xt_ev[kt] = copy(lane, XT[:, kt, :], P[:, b.i, :])
            b.give(xt_ev[kt])
            yield xt_ev[kt]
            yield from prep_tile(kt, xt_ev[kt], 0)

        def lambdas():
            while "lam" not in got_in:
                yield lambda: "lam" in got_in
            yield got_in["lam"]
            dve.wait(got_in["lam"])
            a = tt(dve, LAMV[:, 0], LAMV[:, 0], LAMV[:, 1], ALU.mult)
            b = tt(dve, LAMV[:, 2], LAMV[:, 2], LAMV[:, 3], ALU.mult)
            dve.wait(a, b)
            dve(lambda e: e.tensor_reduce(SM[:, 48:50], LAMV[:, 0], AX.X, ALU.add), 0.2)
            c = dve(lambda e: e.tensor_reduce(SM[:, 50:52], LAMV[:, 2], AX.X, ALU.add), 0.2)
            yield c
            act.wait(c)
            x = activ(SM[:, 52:56], SM[:, 48:52], AF.Exp)
            yield x
            dve.wait(x)
            a = tt(dve, LAM, SM[:, 52:54], SM[:, 54:56], ALU.subtract)
            dve.wait(a)
            for l in range(2):
                got_in["lambda"] = ts(dve, LAM[:, l:l + 1], LAM[:, l:l + 1], 0.8 - 0.6 * float(np.exp(-0.3 * l)), ALU.add)

        xt_ev = [None] * KT

        def add_x(o, b, m, then=None):
            dve.wait(m, xt_ev[o])
            xt_ev[o] = tt(dve, XT[:, o, :], P[:, b.i, :], XT[:, o, :], ALU.add)
            b.give(xt_ev[o])
            if then is not None:
                yield xt_ev[o]
                yield from prep_tile(o, xt_ev[o], then)

        def ffn(name, units, chunks, gated, g_next):
            TG = [at(f"TG{name}_{i}", [128, T], F32, o_a + 6144 + 2048 * i) for i in range(4)]
            TS = [at(f"TS{name}_{i}", [128, T], F32, o_a + 14336 + 2048 * i) for i in range(4)]
            TU = [at(f"TU{name}_{i}", [128, T], F32, o_a + 22528 + 2048 * i) for i in range(4)]
            tg, tsi, tu = ([Hold() for _ in range(4)] for _ in range(3))
            todo = list(units)
            norm = norms[-1]
            gates = {}

            def hidden(j, n, u):
                yield u
                act.wait(u, U.used.get(j))
                h = copy(act, UH[:, j, :], TU[n][:])
                yield h
                dve.wait(u, h, U.used.get(j))
                U.ev[j] = diff(dve, UL[:, j, :], TU[n][:], UH[:, j, :])
                tu[n].give(U.ev[j])

            def ev_gate(j0):
                def evac(i, b, m):
                    j = j0 + i
                    n = j % 4
                    yield from has_rb(norm)
                    got = yield from take(tg[n])
                    dve.wait(m, norm.rb, *got)
                    g = tt(dve, TG[n][:], P[:, b.i, :], RB[:], ALU.mult)
                    rb_read["dve"] = g
                    b.give(g)
                    yield g
                    got = yield from take(tsi[n])
                    act.wait(g, *got)
                    s = activ(TS[n][:], TG[n][:], AF.Silu)
                    tg[n].give(s)
                    yield s
                    pool.wait(s, norm.rb)
                    gates[j] = tt(pool, TS[n][:], TS[n][:], RB[:], ALU.mult)
                    rb_read["pool"] = gates[j]
                return evac

            def ev_up(j0):
                def evac(i, b, m):
                    j = j0 + i
                    n = j % 4
                    while j not in gates:
                        yield lambda: j in gates
                    yield gates[j]
                    got = yield from take(tu[n])
                    dve.wait(m, gates[j], *got)
                    u = tt(dve, TU[n][:], P[:, b.i, :], TS[n][:], ALU.mult)
                    del gates[j]
                    b.give(u)
                    tsi[n].give(u)
                    yield from hidden(j, n, u)
                return evac

            def ev_relu2(j0):
                def evac(i, b, m):
                    j = j0 + i
                    n = j % 4
                    yield from has_rb(norm)
                    got = yield from take(tg[n])
                    dve.wait(m, norm.rb, *got)
                    a = tt(dve, TG[n][:], P[:, b.i, :], RB[:], ALU.mult)
                    rb_read["dve"] = a
                    b.give(a)
                    got = yield from take(tu[n])
                    dve.wait(a, *got)
                    u = stt(dve, TU[n][:], TG[n][:], 0.0, TG[n][:], ALU.max, ALU.mult)
                    tg[n].give(u)
                    yield from hidden(j, n, u)
                return evac

            for ci, n in enumerate(chunks):
                U.ev = {}
                for j in range(0, n, 2):
                    first = ci == 0 and j == 0
                    if gated:
                        yield from unit(todo.pop(0), H, bank, ev_gate(j), kouter=first)
                        yield from unit(todo.pop(0), H, bank, ev_up(j), kouter=first)
                    else:
                        yield from unit(todo.pop(0), H, bank, ev_relu2(j), kouter=first)
                final = ci == len(chunks) - 1
                if final:
                    new_norm()
                for o in range(0, KT, 2):
                    def evac(i, b, m, o=o):
                        return add_x(o + i, b, m, g_next if final else None)
                    yield from unit(todo.pop(0), U, bank, evac, kouter=o == 0)

        def ffn_last(units):
            TG = [at(f"TGz_{i}", [128, T], F32, o_a + 6144 + 2048 * i) for i in range(4)]
            TU = [at(f"TUz_{i}", [128, T], F32, o_a + 22528 + 2048 * i) for i in range(4)]
            tg, tu = ([Hold() for _ in range(4)] for _ in range(2))
            XK = at("XK", [128, 4, D], F32, o_a + 31 * KB)
            FG = at("FG", [128, D], F32, o_a + 47 * KB)
            OUT = at("OUT", [128, 4, D], F32, o_a + 51 * KB)
            SQK = at("SQK", [128, 256], F32, o_a + 67 * KB)
            SS = SM[:, 44:60].rearrange("p (t o) -> p t o", t=4)
            todo = list(units)
            norm = norms[-1]
            fslot = Slot(semaphore("s_fg"))
            oslots = [Slot(semaphore(f"s_out{t}")) for t in range(4)]
            xk_ev = [[None] * 4 for _ in range(4)]
            fg = []
            sqk = Hold()

            def ev_relu2(j0):
                def evac(i, b, m):
                    j = j0 + i
                    n = j % 4
                    yield from has_rb(norm)
                    got = yield from take(tg[n])
                    dve.wait(m, norm.rb, *got)
                    a = tt(dve, TG[n][:], P[:, b.i, :], RB[:], ALU.mult)
                    b.give(a)
                    got = yield from take(tu[n])
                    dve.wait(a, *got)
                    u = stt(dve, TU[n][:], TG[n][:], 0.0, TG[n][:], ALU.max, ALU.mult)
                    tg[n].give(u)
                    yield u
                    act.wait(u, U.used.get(j))
                    h = copy(act, UH[:, j, :], TU[n][:])
                    yield h
                    dve.wait(u, h, U.used.get(j))
                    U.ev[j] = diff(dve, UL[:, j, :], TU[n][:], UH[:, j, :])
                    tu[n].give(U.ev[j])
                return evac

            def turn_x():
                for t in range(4):
                    for half in range(2):
                        b, got = yield from take_one(bank)
                        yield pe
                        pe.wait(*got)
                        for k in range(4):
                            kt = 4 * half + k
                            pe.wait(xt_ev[kt])
                            m = transpose(P[:, b.i, 128 * k:128 * k + 128], XT[:, kt, 128 * t:128 * t + 128], IDN)
                        yield m
                        act.wait(m)
                        c = copy(act, XK[:, t, 512 * half:512 * half + 512], P[:, b.i, :])
                        b.give(c)
                        for o in (2 * half, 2 * half + 1):
                            xk_ev[t][o] = c

            def down(u, o, final):
                held = [None] * 4
                order = [(t, kt) for t in range(4) for kt in range(u.nk)]
                if o == 0:
                    order = [(t, kt) for p in (0, 2) for kt in range(u.nk) for t in (p, p + 1)]
                for t, kt in order:
                    if held[t] is None:
                        held[t] = yield from take_one(bank)
                    while None in u.ready or kt not in U.ev:
                        yield lambda: None not in u.ready and kt in U.ev
                    yield u.ready + [U.ev[kt]]
                    yield pe
                    s, b = u.slots[0], held[t][0]
                    w = slice(128 * kt, 128 * kt + 128)
                    wh, wl = WH[:, s:s + 2, w], WL[:, s:s + 2, w]
                    tok = slice(128 * t, 128 * t + 128)
                    h, l = UH[:, kt, tok], UL[:, kt, tok]
                    p = P[:, b.i, 0:256]
                    if kt == 0:
                        pe.wait(*held[t][1])
                    pe.wait(U.ev[kt], *u.ready)
                    matmul(p, h, wh, kt == 0, False)
                    matmul(p, h, wl, False, False)
                    U.used[kt] = m = matmul(p, l, wh, False, kt == u.nk - 1)
                    if kt == u.nk - 1:
                        if t == 3:
                            wslot[s].give(m)
                            wslot[s + 1].give(m)
                        start(ev_down(t, o, b, m, final), m)

            def ev_down(t, o, b, m, final):
                x = XK[:, t, 256 * o:256 * o + 256]
                while xk_ev[t][o] is None:
                    yield lambda: xk_ev[t][o] is not None
                yield xk_ev[t][o]
                dve.wait(m, xk_ev[t][o])
                a = xk_ev[t][o] = tt(dve, x, P[:, b.i, 0:256], x, ALU.add)
                b.give(a)
                if not final:
                    return
                yield a
                got = yield from take(sqk)
                act.wait(a, *got)
                s = activ(SQK[:], x, AF.Square, accum=SS[:, t, o:o + 1])
                sqk.give(s)
                squares[t].append(s)
                if len(squares[t]) < 4:
                    return
                yield squares[t]
                r = STD[:, t:t + 1]
                dve.wait(*squares[t])
                a = dve(lambda e: e.tensor_reduce(r, SS[:, t, :], AX.X, ALU.add), 0.07)
                yield a
                act.wait(a)
                a = activ(r, r, AF.Sqrt, scale=1.0 / D, bias=EPSC)
                yield a
                dve.wait(a)
                a = recip(RT[:, t:t + 1], r)
                dve.wait(a, *fg)
                y = stt(dve, OUT[:, t, :], XK[:, t, :], RT[:, t:t + 1], FG[:], ALU.mult, ALU.mult)
                sp.wait(y)
                stored.append(dma(sp, oslots[t], out[0, 128 * t:128 * t + 128, :], OUT[:, t, :]))

            stored, squares = [], [[], [], [], []]
            for ci in range(4):
                U.ev = {}
                for j in range(0, 8, 2):
                    yield from unit(todo.pop(0), H, bank, ev_relu2(j), kouter=ci == 0 and j == 0)
                    if ci == 0 and j == 2:
                        sp.wait(*xt_ev)
                        fg.append(dma(sp, fslot, FG[:], A["final_norm_2"].rearrange("(o d) -> o d", o=1).partition_broadcast(128)[:, 0]))
                        start(turn_x())
                for o in range(4):
                    yield from down(todo.pop(0), o, ci == 3)
            while len(stored) < 4:
                yield lambda: len(stored) == 4
            sp.wait(*stored)

        W1 = A["w_in"][0]
        C_Q, C_KC, C_VC, C_KS, C_VS, C_KW, C_VW, C_G, C_HQ, C_HF, C_HI, C_HG = (
            0, 512, 640, 768, 896, 1024, 1152, 1280, 1304, 1816, 2328, 2840)

        def wcols(c, n=128):
            return W1[:, c:c + n]

        def plan_mixer1():
            got = {}
            for name, src in (("hqf0", [wcols(C_HQ), wcols(C_HF)]),
                              ("hi0", [wcols(C_HI, 256)]),
                              ("hqf1", [wcols(C_HQ + 128), wcols(C_HF + 128)]),
                              ("hg0", [wcols(C_HG, 256)]),
                              ("cmp", [wcols(C_KC, 256)]),
                              ("hqf2", [wcols(C_HQ + 256), wcols(C_HF + 256)]),
                              ("hi1", [wcols(C_HI + 256, 256)]),
                              ("hqf3", [wcols(C_HQ + 384), wcols(C_HF + 384)]),
                              ("hg1", [wcols(C_HG + 256, 256)]),
                              ("ksw", [wcols(C_KS), wcols(C_KW)]),
                              ("gate", [wcols(C_G, 24)]),
                              ("q0", [wcols(C_Q, 256)]),
                              ("q1", [wcols(C_Q + 256, 256)]),
                              ("vsw", [wcols(C_VS), wcols(C_VW)])):
                got[name] = plan(src, KT)
            for name, r, c in (("wh0", 512, 0), ("wh1", 512, 512)):
                got[name] = plan([A["w_out"][0][r:r + 512, c:c + 512]], 4)
            for name, r in (("wn0", 0), ("wn1", 256)):
                got[name] = plan([A["w_out"][0][r:r + 256, :]], 2)
            return got

        class Ring:

            def __init__(self, bufs):
                self.all = [Hold() for _ in bufs]
                for i, (h, b) in enumerate(zip(self.all, bufs)):
                    h.i, h.buf = i, b
                self.n = 0

            def next(self):
                self.n += 1
                h = self.all[(self.n - 1) % len(self.all)]
                got = yield from take(h)
                return h, got

            def pair(self):
                self.n += 2
                a, b = (self.all[(self.n - k) % len(self.all)] for k in (2, 1))
                got = yield from take(a, b)
                return a, b, got

        SPOT = {3: (2, 0, 512), 2: (3, 0, 384), 0: (3, 384, 128), 1: (4, 0, 256)}
        CHUNKS = ((2, (3,)), (3, (2, 0)), (4, (1,)))

        def spot(t):
            b, c, n = SPOT[t]
            return P[:, b, c:c + n]

        def scol(t):
            c = {3: 0, 2: 512, 0: 896, 1: 1024}[t]
            return c, c + 128 * (t + 1)

        def trow(j):
            c = {0: 0, 1: 512, 3: 896, 2: 1024}[j]
            return c, c + 512 - 128 * j

        class Order:

            def __init__(self):
                self.n = 0

            def turn(self, n):
                while self.n != n:
                    yield lambda: self.n == n

            def done(self):
                self.n += 1

        def row_softmax(b, ts_, st, scale, h, scale_ev, pf, m, got, free):
            yield m
            dve.wait(m, *free)
            for t in ts_:
                o, i = st[:, t:t + 1], spot(t)
                a = dve(lambda e, o=o, i=i: e.tensor_reduce(o, i, AX.X, ALU.max), vcost(dve, cols(i)))
            dve.wait(a, scale_ev)
            r = slice(min(ts_), max(ts_) + 1, max(1, max(ts_) - min(ts_)))
            a = stt(dve, st[:, 4:8][:, r], st[:, 0:4][:, r], -1.0, scale[:, r, h], ALU.mult, ALU.mult)
            yield a
            act.wait(a, *got, *free)
            for t in ts_:
                c = scol(t)
                x = activ(pf[:, c[0]:c[1]], spot(t), AF.Exp, scale=scale[:, t, h:h + 1], bias=st[:, 4 + t:5 + t],
                          accum=st[:, 8 + t:9 + t])
            bank[b].give(x)
            yield x
            dve.wait(x)
            a = recip(st[:, 8:12][:, r], st[:, 8:12][:, r])
            return r, x, a

        def turn(pf, ready, pt, got, order):
            evs = []
            ph, pl = pt.buf

            def halves(b, c0, w, m):
                yield m
                act.wait(m, *got)
                hi = copy(act, ph[:, c0:c0 + w], P[:, b.i, 0:w])
                yield hi
                dve.wait(hi, *got)
                lo = diff(dve, pl[:, c0:c0 + w], P[:, b.i, 0:w], ph[:, c0:c0 + w])
                b.give(lo)
                evs.append(lo)

            for js in ((0,), (1, 3), (2,)):
                b, free = yield from take_one(bank[5:7])
                pe.wait(*ready, *free)
                c0, w = trow(js[0])[0], 0
                for j in js:
                    for t in range(j, 4):
                        c = scol(t)[0] + 128 * j
                        m = transpose(P[:, b.i, w:w + 128], pf.buf[:, c:c + 128], IDN)
                        w += 128
                start(halves(b, c0, w, m), m)
            pf.give(m)
            order.done()
            while len(evs) < 3:
                yield lambda: len(evs) == 3
            yield evs
            return evs

        def mix_halves(kt, src, ev):
            act.wait(ev)
            hi = copy(act, UH[:, kt, :], src)
            yield hi
            dve.wait(ev, hi)
            U.ev[kt] = diff(dve, UL[:, kt, :], src, UH[:, kt, :])

        def values(v, ph, pl, ready, first, stop):
            pe.wait(*ready)
            for j in range(4):
                c = trow(j)
                o = P[:, 7, 128 * j:512]
                matmul(o, v(j), ph[:, c[0]:c[1]], first and j == 0, False)
                m = matmul(o, v(j), pl[:, c[0]:c[1]], False, stop and j == 3)
            return m

        def fold(h, m, tmp, both, mix_free=None):
            if h % 2 == 0:
                both.got = yield from take(both)
            got = yield from take(tmp)
            act.wait(m, *got)
            c = copy(act, tmp.buf[0:64, :], P[64:128, 7, :])
            yield c
            dve.wait(c, *both.got)
            own = slice(64 * (h % 2), 64 * (h % 2) + 64)
            a = tt(dve, both.buf[own, :], P[0:64, 7, :], tmp.buf[0:64, :], ALU.add)
            bank[7].give(a)
            tmp.give(a)
            if h % 2:
                if mix_free is not None:
                    got = yield from mix_free(h // 2)
                    act.wait(*got)
                    dve.wait(*got)
                yield a
                yield from mix_halves(h // 2, both.buf[:], a)
                both.give(U.ev[h // 2])

        def out_tiles(u, k0, o0, ring, then):
            def evac(i, b, m):
                return add_x(o0 + i, b, m, then)
            return unit(u, U, ring, evac, k0=k0)

        def mixer1(m1):
            QS = [at(f"QS{h}", [128, T], F32R, o_a + (6 + 2 * h) * KB) for h in range(8)]
            HS = []
            for i in range(2):
                o = o_a + (6 + 8 * i) * KB
                HS.append((at(f"HQ{i}", [128, T], F32, o), at(f"HK{i}", [128, T], F32, o + 2 * KB),
                           at(f"HT{i}", [128, 1024], F32, o + 4 * KB)))
            KS = [[[at(f"KS{b}{g}{x}", [128, T], F32R, o_a + (22 + 8 * b + 4 * g + 2 * x) * KB) for x in range(2)]
                   for g in range(2)] for b in range(2)]
            VN = at("VN", [128, 4, 4, 128], F32R, o_a + 38 * KB)
            o = o_a + 46 * KB
            KCH = at("KCH", [128, 2, 32], F32R, o)
            KCL = at("KCL", [128, 2, 32], F32R, o + 256)
            VCS = at("VCS", [128, 2, 128], F32R, o + 512)
            GATE = at("GATE", [128, 4, 24], F32, o + 1536)
            QSC = at("QSC", [128, 4, 8], F32, o + 1920)
            QW = at("QW", [128, 3, 32], F32, o_a + 512)
            HV = [at(f"HV{i}", [128, 4, 256], F32, o_a + (48 + 4 * i) * KB) for i in range(2)]
            EV = Ring([at(f"EV{i}", [128, T], F32, o_a + (56 + 2 * i) * KB) for i in range(4)])
            TM = Ring([at(f"TM{i}", [128, T], F32, o_a + (64 + 2 * i) * KB) for i in range(2)])
            ATD = [at(f"ATD{i}", [128, 4, 128], F32, o_u + 16384 * i) for i in range(2)]
            ATO = [at(f"ATO{i}", [128, 768], F32, o_u + 16384 * i + 2048) for i in range(2)]
            CG = [at(f"CG{i}", [128, 5, 64], F32, o_u + 16384 * i + 5120) for i in range(2)]
            GR = at("GR", [128, 2, 128], F32, o_u + 6400)
            G = [at(f"G{h}", [128, T], F32, o_u + 16384 + 2048 * (4 + h)) for h in range(4)]
            KCX = at("KCX", [128, 2, T], F32, o_a + 2 * KB)
            KNB = [(at("KN0", [128, T], F32, o_a + 48 * KB), at("KN1", [128, T], F32, o_a + 50 * KB)),
                   (at("KN2", [128, T], F32, o_a + 2 * KB), at("KN3", [128, T], F32, o_a + 4 * KB))]
            U.ev = {}
            norm = norms[-1]

            def scaled(o, b, ev, free):
                dve.wait(ev, norm.rb, *free)
                a = tt(dve, o, P[:, b.i, :], RB[:], ALU.mult)
                rb_read["dve"] = a
                b.give(a)
                return a

            head_set, hv = [Hold(), Hold()], [Hold(), Hold()]
            head_in, v_in, g_in, set_got = {}, {}, {}, {}
            hgrn_at = [Hold(), Hold()]

            def ev_hqf(h):
                hq, hk, ht = HS[h % 2]

                def evac(i, b, m):
                    yield from has_rb(norm)
                    xb, yb, got = yield from EV.pair()
                    x, y = xb.buf[:], yb.buf[:]
                    a = scaled(x, b, m, got)
                    yield a
                    act.wait(a, *got)
                    s = activ(y, x, AF.Sigmoid)
                    if h not in set_got:
                        set_got[h] = None
                        set_got[h] = yield from take(head_set[h % 2])
                    while set_got[h] is None:
                        yield lambda: set_got[h] is not None
                    yield s
                    if i == 0:
                        pool.wait(s, *set_got[h])
                        q = tt(pool, hq[:], x, y, ALU.mult)
                        xb.give(q)
                        yb.give(q)
                        head_in[(h, 0)] = q
                    else:
                        while "small" not in got_in:
                            yield lambda: "small" in got_in
                        dve.wait(s, got_in["small"], *set_got[h])
                        f = ts(dve, ht[:, 0:T], y, LB1[:, h:h + 1], ALU.mult, LB[:, h:h + 1], ALU.add)
                        dve.wait(f)
                        k = ts(dve, hk[:], ht[:, 0:T], -1.0, ALU.mult, 1.0, ALU.add)
                        xb.give(s)
                        yb.give(f)
                        head_in[(h, 1)] = k
                return evac

            def ev_hi(p):
                def evac(tp, b, m):
                    yield from has_rt(norm)
                    if tp == 0:
                        set_got[("v", p)] = yield from take(hv[p])
                    while ("v", p) not in set_got:
                        yield lambda: ("v", p) in set_got
                    act.wait(m, norm.rt, *set_got[("v", p)])
                    for q in range(2):
                        t = 2 * tp + q
                        c = activ(HV[p][:, t, :], P[:, b.i, 256 * q:256 * q + 256], AF.Identity, scale=RT[:, t:t + 1])
                    rt_read["act"] = c
                    b.give(c)
                    v_in[(p, tp)] = c
                return evac

            def ev_hg(p):
                def evac(i, b, m):
                    h = 2 * p + i
                    yield from has_rb(norm)
                    xb, yb, got = yield from EV.pair()
                    x, y = xb.buf[:], yb.buf[:]
                    a = scaled(x, b, m, got)
                    yield a
                    act.wait(a, *got)
                    s = activ(y, x, AF.Sigmoid)
                    yield s
                    pool.wait(s)
                    g_in[h] = tt(pool, G[h][:], x, y, ALU.mult)
                    xb.give(g_in[h])
                    yb.give(g_in[h])
                return evac

            heads_done, v_read = [], {}

            def hgrn(h):
                par, p = h % 2, h // 2
                hq, hk, ht = HS[par]
                atd, ato = ATD[par], ATO[par]
                ring = [bank[2 + par], bank[4 + par]]
                v = HV[p]
                while (h, 0) not in head_in or (h, 1) not in head_in or "hm" not in got_in:
                    yield lambda: (h, 0) in head_in and (h, 1) in head_in and "hm" in got_in
                q_ev, k_ev, t_ev = head_in[(h, 0)], head_in[(h, 1)], head_in[(h, 1)]
                got = yield from take(hgrn_at[par])
                pool.wait(*got)
                wrote = [zero(pool, atd[:])]
                yield q_ev, k_ev
                for n, lev in enumerate((0, 1, 2, 4, 8, 16, 32, 64)):
                    b, got = yield from take_one(ring)
                    pe.wait(q_ev, k_ev, *got)
                    w = 64 if lev else 128
                    pb = P[:, b.i, 0:4 * w].rearrange("p (j t) -> p j t", j=4)
                    for j in range(4):
                        qj = hq[:, 128 * j:128 * j + 128]
                        if lev:
                            qj = qj.rearrange("p (n s l) -> p n s l", s=2, l=lev)[:, :, 1, :]
                        m = matmul(pb[:, j, :] if not lev else pb[:, j, :].rearrange("p (n l) -> p n l", l=lev),
                                   hk[:, 128 * j:128 * j + 128], qj, True, True)
                    yield m
                    if lev == 0:
                        dve.wait(m, q_ev)
                        q_ev = tt(dve, hq[:], hq[:], ht[:, 0:T], ALU.mult)
                    else:
                        q_ev, k_ev, t_ev = double(hq, hk, ht, lev, m, q_ev, k_ev, t_ev)
                    if lev <= 16:
                        mk = HM[:, n, :].bitcast(U32)
                        to, src = atd[:], pb
                        if lev:
                            mk = mk.rearrange("p (n s l) -> p n s l", s=2, l=lev)[:, :, 1, :]
                            mk = mk.unsqueeze(1).to_broadcast([128, 4, 64 // lev, lev])
                            to = to.rearrange("p j (n s l) -> p j n s l", s=2, l=lev)[:, :, :, 1, :]
                            src = src.rearrange("p j (n l) -> p j n l", l=lev)
                        else:
                            mk = mk.unsqueeze(1).to_broadcast([128, 4, 128])
                        dve.wait(m, got_in["hm"], *wrote)
                        c = dve(lambda e, mk=mk, to=to, src=src: e.copy_predicated(to, mk, src), vcost(dve, 4 * w))
                        hm_last[0] = c
                    else:
                        act.wait(m, *wrote)
                        for r in range(0, 128, 2 * lev):
                            c = copy(act, atd[r:r + lev, :, r + lev:r + 2 * lev], pb[r:r + lev, :, r // 2:r // 2 + lev])
                    wrote = [c]
                    b.give(c)
                    yield q_ev, k_ev
                b, got = yield from take_one(ring)
                pe.wait(q_ev, k_ev, *got)
                matmul(P[:, b.i, 0:128], hk[:, 0:128], hq[:, 128:256], True, True)
                m = matmul(P[:, b.i, 128:256], hk[:, 256:384], hq[:, 384:512], True, True)
                yield m
                q_ev, k_ev, t_ev = double(hq, hk, ht, 128, m, q_ev, k_ev, t_ev)
                act.wait(m)
                copy(act, ato[:, 0:128], P[:, b.i, 0:128])
                c = copy(act, ato[:, 640:768], P[:, b.i, 128:256])
                b.give(c)
                wrote.append(c)
                yield q_ev, k_ev
                b, got = yield from take_one(ring)
                pe.wait(q_ev, k_ev, *got)
                matmul(P[:, b.i, 0:256], hk[:, 0:128], hq[:, 256:512], True, True)
                m = matmul(P[:, b.i, 256:512], hk[:, 128:256], hq[:, 256:512], True, True)
                head_set[par].give(m)
                yield m
                act.wait(m)
                c = copy(act, ato[:, 128:640], P[:, b.i, :])
                b.give(c)
                wrote.append(c)
                while (p, 0) not in v_in or (p, 1) not in v_in:
                    yield lambda: (p, 0) in v_in and (p, 1) in v_in
                yield c
                ob, got = yield from take_one(ring)
                pe.wait(v_in[(p, 0)], v_in[(p, 1)], *wrote, *got)
                for j in range(4):
                    matmul(P[:, ob.i, 128 * j:128 * j + 128], v[:, j, 128 * par:128 * par + 128], atd[:, j, :], j == 0, False)
                for j, (c, n) in enumerate(((0, 384), (384, 256), (640, 128))):
                    m = matmul(P[:, ob.i, 512 - n:512], v[:, j, 128 * par:128 * par + 128], ato[:, c:c + n], False, j == 2)
                hgrn_at[par].give(m)
                heads_done.append(m)
                v_read.setdefault(p, []).append(m)
                if len(v_read[p]) == 2:
                    hv[p].give(*v_read[p])
                yield m
                tb, got = yield from TM.next()
                tm = tb.buf
                act.wait(m, *got)
                s = activ(tm[:], P[:, ob.i, :], AF.Square)
                yield s
                b, got = yield from take_one(ring)
                pe.wait(s, *got)
                m = matmul(P[:, b.i, :], ONES[:], tm[:], True, True)
                yield m
                act.wait(m)
                s = activ(tm[:], P[:, b.i, :], AF.Sqrt, scale=1.0 / 128, bias=EPSC)
                b.give(s)
                yield s
                dve.wait(s)
                for k in range(4):
                    r = recip(tm[:, 128 * k:128 * k + 128], tm[:, 128 * k:128 * k + 128])
                    yield r
                dve.wait(r)
                y = stt(dve, tm[:], P[:, ob.i, :], GT[:, 52:53], tm[:], ALU.mult, ALU.mult)
                ob.give(y)
                while h not in g_in:
                    yield lambda: h in g_in
                yield y, g_in[h]
                dve.wait(y, g_in[h])
                y = tt(dve, tm[:], tm[:], G[h][:], ALU.mult)
                yield y
                yield from mix_halves(4 + h, tm[:], y)
                tb.give(U.ev[4 + h])

            def double(hq, hk, ht, lev, m, q_ev, k_ev, t_ev):
                nb = T // (2 * lev)
                base = {1: 0, 2: 512, 4: 768, 8: 896, 16: 960, 32: 992, 64: 1008, 128: 1016}[lev]
                nxt = base + 2 * nb
                tv = ht[:, base:base + 2 * nb].rearrange("p (n s) -> p n s", s=2)
                qv = hq[:].rearrange("p (n s l) -> p n s l", s=2, l=lev)
                kv = hk[:].rearrange("p (n s l) -> p n s l", s=2, l=lev)
                pool.wait(m, k_ev, t_ev)
                k2 = tt(pool, kv[:, :, 0, :], kv[:, :, 0, :], tv[:, :, 1:2].to_broadcast([128, nb, lev]), ALU.mult)
                t2 = t_ev
                if lev < 128:
                    t2 = tt(pool, ht[:, nxt:nxt + nb], tv[:, :, 0], tv[:, :, 1], ALU.mult)
                dve.wait(m, q_ev, t_ev)
                q2 = tt(dve, qv[:, :, 1, :], qv[:, :, 1, :], tv[:, :, 0:1].to_broadcast([128, nb, lev]), ALU.mult)
                return q2, k2, t2

            cmp_src = {}
            kc_ev, kcx_done = [None, None], [None]

            def ev_cmp(i, b, m):
                yield from has_rb(norm)
                xb, xg = yield from EV.next()
                cmp_src[i] = (xb, scaled(xb.buf[:], b, m, xg))

            def compress():
                for i in range(2):
                    while i not in cmp_src or ("cw", i) not in got_in:
                        yield lambda: i in cmp_src and ("cw", i) in got_in
                    xb, ev = cmp_src[i]
                    yield ev
                    x = xb.buf
                    free = [norm.rb] if i == 0 else [m]
                    dve.wait(ev, *free)
                    for g in range(2):
                        r = slice(64 * g, 64 * g + 64)
                        pos = GT[r, 64 + 32 * i:96 + 32 * i]
                        xa = x[r, :].rearrange("p (n s) -> p n s", s=16)
                        ka = KCX[0:64, g, :].rearrange("p (n s) -> p n s", s=16)
                        kb = KCX[64:128, g, :].rearrange("p (n s) -> p n s", s=16)
                        tt(dve, ka, xa, pos[:, 0:16].unsqueeze(1).to_broadcast([64, 32, 16]), ALU.add)
                        c = tt(dve, kb[:, 0:31, :], xa[:, 1:32, :],
                               pos[:, 16:32].unsqueeze(1).to_broadcast([64, 31, 16]), ALU.add)
                    xb.give(c)
                    yield c
                    b6, got = yield from take_one(bank[6:8])
                    kv = KCX[:].rearrange("p g (n s) -> p g n s", s=16)
                    o = P[:, b6.i, 0:64].rearrange("p (g n) -> p g n", g=2)[:, :, 0:31]
                    for r in range(16):
                        if r == 0:
                            pe.wait(c, got_in[("cw", i)], *got)
                        m = matmul(o, CW1[i][:, r, :], kv[:, :, 0:31, r], r == 0, r == 15)
                        if r % 4 == 3:
                            yield pe
                    kcx_done[0] = m
                    hs, u, w, th, gl = (CG[i][:, k, :].rearrange("p (g n) -> p g n", g=2) for k in range(5))
                    z = zero(pool, gl)
                    v = slice(0, 31)
                    yield m
                    dve.wait(m)
                    a = copy(dve, hs[:, :, v], o)
                    b6.give(a)
                    dve.wait(a)
                    a = tt(dve, u[:, :, v], hs[:, :, v], hs[:, :, v], ALU.mult)
                    dve.wait(a)
                    a = ts(dve, w[:, :, v], u[:, :, v], 0.044715, ALU.mult, 1.0, ALU.add)
                    dve.wait(a)
                    a = tt(dve, u[:, :, v], w[:, :, v], hs[:, :, v], ALU.mult)
                    yield a
                    act.wait(a)
                    a = activ(th[:, :, v], u[:, :, v], AF.Tanh, scale=float(np.sqrt(2 / np.pi)))
                    yield a
                    dve.wait(a)
                    a = ts(dve, w[:, :, v], th[:, :, v], 1.0, ALU.add, 0.5, ALU.mult)
                    dve.wait(a, z)
                    a = tt(dve, gl[:, :, v], w[:, :, v], hs[:, :, v], ALU.mult)
                    yield a
                    b6, got = yield from take_one(bank[6:8])
                    if i == 0:
                        pe.wait(a, *got)
                        m = matmul(P[:, b6.i, 0:64], CWS[0][:].rearrange("p a d -> p (a d)"), CG[0][:, 4, :], True, True)
                        yield m
                        act.wait(m)
                        s = activ(CG[0][:, 1, :], P[:, b6.i, 0:64], AF.Square)
                        yield s
                        b7, got = yield from take_one(bank[6:8])
                        pe.wait(s, *got)
                        m = matmul(P[:, b7.i, 0:64], BLK, CG[0][:, 1, :], True, True)
                        yield m
                        act.wait(m)
                        s = activ(CG[0][:, 2, :], P[:, b7.i, 0:64], AF.Sqrt, scale=1.0 / 64, bias=EPSC)
                        b7.give(s)
                        yield s
                        dve.wait(s)
                        r_ = recip(CG[0][:, 3, :], CG[0][:, 2, :])
                        dve.wait(r_)
                        y = stt(dve, CG[0][:, 0, :], P[:, b6.i, 0:64], QFOLD[:, 0:1], CG[0][:, 3, :], ALU.mult, ALU.mult)
                        b6.give(y)
                        yield y
                        act.wait(y)
                        kh = KCH[:].rearrange("p g n -> p (g n)")
                        hi = copy(act, kh, CG[0][:, 0, :])
                        yield hi
                        dve.wait(hi)
                        kc_ev[0] = diff(dve, KCL[:].rearrange("p g n -> p (g n)"), CG[0][:, 0, :], kh)
                    else:
                        dve.wait(a)
                        a = copy(dve, GR[:].rearrange("p g (r n) -> p g r n", r=4),
                                 gl.unsqueeze(2).to_broadcast([128, 2, 4, 32]))
                        yield a
                        pe.wait(a, *got)
                        for g in range(2):
                            m = matmul(P[:, b6.i, 64 * g:64 * g + 64], GR[:, g, :], CWS[1][:, 0, :], True, True)
                        pv = P[:, b6.i, 0:128].rearrange("p (g d) -> p g d", g=2)
                        yield m
                        act.wait(m)
                        hi = copy(act, VCS[:, :, 0:64], pv)
                        yield hi
                        dve.wait(hi)
                        kc_ev[1] = diff(dve, VCS[:, :, 64:128], pv, VCS[:, :, 0:64])
                        b6.give(kc_ev[1])

            ks_ev = {}

            def ev_ksw(i, b, m):
                kn, sq_ = KNB[i]
                if i == 0:
                    got = yield from take(hv[0])
                else:
                    while kc_ev[1] is None:
                        yield lambda: kc_ev[1] is not None
                    got = [kcx_done[0]]
                a = scaled(kn[:], b, m, got)
                yield a
                act.wait(a, *got)
                s = activ(sq_[:], kn[:], AF.Square)
                yield s
                b, got = yield from take_one(bank[6:8])
                pe.wait(s, *got)
                m = matmul(P[:, b.i, :], BLK, sq_[:], True, True)
                yield m
                act.wait(m)
                s = activ(sq_[:], P[:, b.i, :], AF.Sqrt, scale=1.0 / 64, bias=EPSC)
                xb, yb, got = yield from EV.pair()
                yield s
                dve.wait(s, *got)
                m = ts(dve, xb.buf[:], P[:, b.i, :], 1.0 / 64, ALU.mult, EPS, ALU.add)
                b.give(m)
                r = rsqrt_step(sq_[:], sq_[:], xb.buf[:], yb.buf[:], m)
                xb.give(r)
                yb.give(r)
                dve.wait(r)
                y = stt(dve, kn[:], kn[:], QFOLD[:, 1 + i:2 + i], sq_[:], ALU.mult, ALU.mult)
                while kc_ev[1] is None:
                    yield lambda: kc_ev[1] is not None
                yield y
                for g in range(2):
                    own = slice(64 * g, 64 * g + 64)
                    other = slice(64 - 64 * g, 128 - 64 * g)
                    hh, ll = KS[i][g]
                    act.wait(y)
                    c = copy(act, hh[own, :], kn[own, :])
                    c2 = copy(act, hh[other, :], kn[own, :])
                    yield c
                    dve.wait(y, c)
                    diff(dve, ll[own, :], kn[own, :], hh[own, :])
                    dve.wait(c2)
                    ks_ev[(i, g)] = [c2, diff(dve, ll[other, :], kn[own, :], hh[own, :])]

            vn_ev = [None] * 4

            def ev_vsw(tp, b, m):
                yield from has_rt(norm)
                src = [P[:, b.i, 256 * q:256 * q + 256].rearrange("p (n d) -> p n d", n=4) for q in range(2)]
                act.wait(m, norm.rt, got_in["maskb"])
                for q in range(2):
                    t = 2 * tp + q
                    hi = activ(VN[:, t, :, 0:64], src[q], AF.Identity, scale=RT[:, t:t + 1])
                rt_read["act"] = hi
                yield hi
                dve.wait(m, hi, norm.rt)
                for q in range(2):
                    t = 2 * tp + q
                    vn_ev[t] = stt(dve, VN[:, t, :, 64:128], src[q], RT[:, t:t + 1], VN[:, t, :, 0:64],
                                   ALU.mult, ALU.subtract)
                rt_read["dve"] = vn_ev[t]
                b.give(vn_ev[2 * tp + 1])

            gate_ev = [None]

            def ev_gate(i, b, m):
                yield from has_rb(norm)
                xb, xg = yield from EV.next()
                x = xb.buf
                dve.wait(m, norm.rb, *xg)
                a = tt(dve, x[0:24, :], P[0:24, b.i, :], RB[0:24, :], ALU.mult)
                rb_read["dve"] = a
                b.give(a)
                yield a
                act.wait(a)
                s = activ(x[0:24, :], x[0:24, :], AF.Sigmoid)
                yield s
                b, got = yield from take_one(bank[6:8])
                pe.wait(s, *got)
                for t in range(4):
                    m = transpose(P[:, b.i, 24 * t:24 * t + 24], x[0:24, 128 * t:128 * t + 128], IDN[0:24, 0:24])
                xb.give(m)
                yield m
                dve.wait(m)
                gate_ev[0] = copy(dve, GATE[:].rearrange("p t c -> p (t c)"), P[:, b.i, 0:96])
                b.give(gate_ev[0])

            q_ev, qsc_ev, q_sums = {}, [None], []
            qs_bank = bank[7]

            def ev_q(u):
                def evac(i, b, m):
                    j = 2 * u + i
                    xb, xg = yield from EV.next()
                    x = xb.buf[:]
                    act.wait(m, *xg)
                    s = activ(x, P[:, b.i, :], AF.Square)
                    while len(heads_done) < 4:
                        yield lambda: len(heads_done) == 4
                    yield s
                    act.wait(*heads_done)
                    copy(act, QS[2 * j][0:64, :], P[0:64, b.i, :])
                    c = copy(act, QS[2 * j + 1][64:128, :], P[64:128, b.i, :])
                    if j == 0:
                        qs_got = yield from take(qs_bank)
                        pe.wait(*qs_got)
                        q_sums.append(None)
                    while not q_sums:
                        yield lambda: q_sums
                    pe.wait(s)
                    for t in range(4):
                        cc = 2 * (4 * j + t)
                        mm = matmul(P[:, qs_bank.i, cc:cc + 2], x[:, 128 * t:128 * t + 128], BLK[:, 0:128:64], True, True)
                    xb.give(mm)
                    q_sums.append(mm)
                    if len(q_sums) == 5:
                        start(q_scale(), mm)
                    yield c
                    dve.wait(c, *heads_done)
                    d = diff(dve, QS[2 * j][64:128, :], P[0:64, b.i, :], QS[2 * j][0:64, :])
                    q_ev[2 * j] = d
                    d = diff(dve, QS[2 * j + 1][0:64, :], P[64:128, b.i, :], QS[2 * j + 1][64:128, :])
                    q_ev[2 * j + 1] = d
                    b.give(d)
                return evac

            def q_scale():
                pq = P[:, qs_bank.i, 0:32].rearrange("p (j t c) -> p t j c", j=4, t=4)
                w = SM[:, 32:36]
                dve.wait(*q_sums, norm.rt)
                a = tt(dve, w, RT, RT, ALU.mult)
                dve.wait(a)
                qv = QW[:, 0, :].rearrange("p (t j c) -> p t j c", t=4, c=2)
                a = tt(dve, qv, pq, w.unsqueeze(2).unsqueeze(3).to_broadcast([128, 4, 4, 2]), ALU.mult)
                qs_bank.give(a)
                dve.wait(a)
                a = ts(dve, QW[:, 0, :], QW[:, 0, :], 1.0 / 64, ALU.mult, EPS, ALU.add)
                yield a
                act.wait(a)
                b = activ(QW[:, 1, :], QW[:, 0, :], AF.Sqrt)
                yield b
                dve.wait(b)
                a = rsqrt_step(QSC[:].rearrange("p t h -> p (t h)"), QW[:, 1, :], QW[:, 0, :], QW[:, 2, :], a)
                a2 = ts(dve, SM[:, 36:40], RT, 0.125, ALU.mult)
                rt_read["dve"] = a2
                dve.wait(a, a2)
                qsc_ev[0] = tt(dve, QSC[:], QSC[:], SM[:, 36:40].unsqueeze(2).to_broadcast([128, 4, 8]), ALU.mult)

            PC = at("PC", [128, 4, 8, 32], F32, o_a + 48 * KB)
            EC = at("EC", [128, 4, 8, 32], F32, o_a + 52 * KB)
            PCH = at("PCH", [128, 2, T], F32R, o_a + 56 * KB)
            PCL = at("PCL", [128, 2, T], F32R, o_a + 60 * KB)
            STC = at("STC", [128, 3, 32], F32, o_a)
            pct_ev = [None, None]
            pc_ev, pc_read = [None, None], []

            def cmp_half(i):
                while len(q_ev) < 8 or qsc_ev[0] is None or gate_ev[0] is None or None in kc_ev or len(ks_ev) < 4:
                    yield lambda: (len(q_ev) == 8 and qsc_ev[0] is not None and gate_ev[0] is not None
                                   and None not in kc_ev and len(ks_ev) == 4)
                kn_read = [s for k in ks_ev.values() for s in k]
                yield list(q_ev.values()) + kc_ev + kn_read
                b, got = yield from take_one([bank[5], bank[6]])
                for t in (2 * i, 2 * i + 1):
                    yield pe
                    if t == 2 * i:
                        pe.wait(*kc_ev, *got, *q_ev.values(), got_in["maskb"])
                    for h in range(8):
                        c = 256 * (t % 2) + 32 * h
                        o = P[:, b.i, c:c + 32]
                        q = QS[h][:, 128 * t:128 * t + 128]
                        matmul(o, q, KCH[:, h // 4, :], True, False)
                        matmul(o, q, KCL[:, h // 4, :], False, False)
                        m = matmul(o, IDB[:], MASKB[:, 3, 32 * t:32 * t + 32], False, True)
                yield m
                pv = P[:, b.i, :].rearrange("p (a n) -> p a n", n=32)
                mx = STC[:, 0, 16 * i:16 * i + 16]
                ec = EC[:, 2 * i:2 * i + 2].rearrange("p t h n -> p (t h) n")
                dve.wait(m, qsc_ev[0])
                a = dve(lambda e: e.tensor_reduce(mx, pv, AX.X, ALU.max), 0.6)
                dve.wait(a)
                dve.wait(*heads_done)
                a = tt(dve, ec, pv, mx.unsqueeze(2).to_broadcast([128, 16, 32]), ALU.subtract)
                b.give(a)
                yield a
                qs = QSC[:, 2 * i:2 * i + 2, :].rearrange("p t h -> p (t h)")
                pool.wait(a, qsc_ev[0])
                a = tt(pool, ec, ec, qs.unsqueeze(2).to_broadcast([128, 16, 32]), ALU.mult)
                yield a
                act.wait(a)
                x = activ(ec, ec, AF.Exp)
                yield x
                dve.wait(x)
                sm = STC[:, 1, 16 * i:16 * i + 16]
                a = dve(lambda e: e.tensor_reduce(sm, ec, AX.X, ALU.add), 0.6)
                dve.wait(a)
                rc = STC[:, 2, 16 * i:16 * i + 16]
                a = recip(rc, sm)
                dve.wait(a, gate_ev[0])
                rt_ = rc.rearrange("p (t h) -> p t h", t=2)
                a = tt(dve, rt_, rt_, GATE[:, 2 * i:2 * i + 2, 0:24:3], ALU.mult)
                yield a
                pool.wait(a, x)
                a = tt(pool, ec, ec, rc.unsqueeze(2).to_broadcast([128, 16, 32]), ALU.mult)
                pool.wait(a, *kn_read)
                for t in range(2 * i, 2 * i + 2):
                    a = tt(pool, PC[:, t], EC[:, t],
                           M01[:, 32 * t:32 * t + 32].unsqueeze(1).to_broadcast([128, 8, 32]), ALU.mult)
                pc_ev[i] = a
                if None not in pc_ev:
                    free = yield from take(*EV.all)
                    for g in range(2):
                        start(cmp_turn(g, free), *pc_ev)

            def cmp_turn(g, free):
                b, got = yield from take_one([bank[5], bank[6]])
                pe.wait(*pc_ev, *got)
                for t in range(4):
                    m = transpose(P[:, b.i, 128 * t:128 * t + 128],
                                  PC[:, t, 4 * g:4 * g + 4, :].rearrange("p h n -> p (h n)"), IDN)
                pc_read.append(m)
                if len(pc_read) == 2:
                    PF.all[2].give(*pc_read, *pc_ev)
                yield m
                act.wait(m, *free)
                hi = copy(act, PCH[:, g, :], P[:, b.i, :])
                yield hi
                dve.wait(hi, *free)
                pct_ev[g] = diff(dve, PCL[:, g, :], P[:, b.i, :], PCH[:, g, :])
                b.give(pct_ev[g])

            PF = Ring([at(f"PF{i}", [128, 1280], F32, o) for i, o in enumerate((o_h, o_h + 5 * KB, o_a + 48 * KB))])
            PF.all[2].free = None
            PH = [at(f"PH{i}", [128, 1280], F32R, o_h + (10 + 5 * i) * KB) for i in range(2)]
            PL = [at(f"PL{i}", [128, 1280], F32R, o_h + (20 + 5 * i) * KB) for i in range(2)]
            PT = Ring(list(zip(PH, PL)))
            ST = at("ST", [128, 4, 16], F32, o_a + 69 * KB)
            STR = Ring([ST[:, i, :] for i in range(4)])
            s_order, t_order, v_order = Order(), Order(), Order()

            def item(n):
                h, br = n // 2, n % 2
                g = h // 4
                hh, ll = KS[br][g]
                q = QS[h]
                yield from s_order.turn(n)
                while h not in q_ev or (br, g) not in ks_ev or qsc_ev[0] is None or gate_ev[0] is None or not h_over:
                    yield lambda: h in q_ev and (br, g) in ks_ev and qsc_ev[0] is not None and gate_ev[0] is not None and h_over
                pf, pf_got = yield from PF.next()
                st, st_got = yield from STR.next()
                pf_got = pf_got + h_over
                scaled_ev = []

                def soft(b, ts_, m):
                    r, x, a = yield from row_softmax(b, ts_, st.buf, QSC, h, qsc_ev[0], pf.buf, m, pf_got, st_got)
                    dve.wait(a, gate_ev[0])
                    a = tt(dve, st.buf[:, 8:12][:, r], st.buf[:, 8:12][:, r], GATE[:, r, 3 * h + 1 + br], ALU.mult)
                    yield a
                    for t in ts_:
                        c = scol(t)
                        p = pf.buf[:, c[0]:c[1]]
                        lane, scale = scale_rows(p, p, st.buf[:, 8 + t:9 + t])
                        lane.wait(a, x)
                        scaled_ev.append(scale())

                for b, ts_ in CHUNKS:
                    got = yield from take(bank[b])
                    pe.wait(q_ev[h], *ks_ev[(br, g)], got_in["maskb"], *got)
                    for t in ts_:
                        o = spot(t)
                        k = slice(0, 128 * (t + 1))
                        qt = q[:, 128 * t:128 * t + 128]
                        matmul(o, qt, hh[:, k], True, False)
                        matmul(o, qt, ll[:, k], False, False)
                        m = matmul(o[:, 128 * t:128 * t + 128], IDB[:], MASKB[:, 0, :], False, True)
                    start(soft(b, ts_, m), m)
                s_order.done()
                while len(scaled_ev) < 4:
                    yield lambda: len(scaled_ev) == 4
                yield scaled_ev
                st.give(*scaled_ev)
                yield from t_order.turn(n)
                pt, pt_got = yield from PT.next()
                turned = yield from turn(pf, scaled_ev, pt, pt_got + h_over, t_order)
                ph, pl = pt.buf
                yield from v_order.turn(n)
                o_got = []
                if br == 0:
                    while None in vn_ev:
                        yield lambda: None not in vn_ev
                    o_got = yield from take(bank[7])
                elif pct_ev[g] is None:
                    while pct_ev[g] is None:
                        yield lambda: pct_ev[g] is not None
                    yield pct_ev[g]
                m = values(lambda j: VN[:, j, 2 * br + g, :], ph, pl, turned + vn_ev + o_got, br == 0, False)
                pt.give(m)
                if br == 1:
                    pe.wait(pct_ev[g], kc_ev[1])
                    r = slice(32 * (h % 4), 32 * (h % 4) + 32)
                    matmul(P[:, 7, :], VCS[r, g, :], PCH[r, g, :], False, False)
                    m = matmul(P[:, 7, :], VCS[r, g, :], PCL[r, g, :], False, True)
                    yield m
                    yield from fold(h, m, TM.all[0], TM.all[1])
                v_order.done()
                if n == 15:
                    ring.extend(bank[2:8])

            h_over = []

            ring = [bank[0], bank[1]]

            def main(name, evac, src=H, **kw):
                return unit(m1[name], src, ring, evac, **kw)

            yield from unit(m1["hqf0"], H, bank[2:6], ev_hqf(0), kouter=True)
            yield from vunit(m1["hi0"], ring, ev_hi(0))
            start(small_things())
            start(lambdas())
            start(hgrn(0))
            start(hgrn(1))
            yield from main("hqf1", ev_hqf(1))
            yield from main("hg0", ev_hg(0))
            yield from main("cmp", ev_cmp)
            start(compress())
            yield from main("hqf2", ev_hqf(2))
            start(hgrn(2))
            yield from vunit(m1["hi1"], ring, ev_hi(1))
            yield from main("hqf3", ev_hqf(3))
            start(hgrn(3))
            yield from main("hg1", ev_hg(1))
            yield from main("ksw", ev_ksw)
            yield from main("gate", ev_gate, ncol=24)
            yield from main("q0", ev_q(0))
            yield from main("q1", ev_q(1))
            for i in range(2):
                start(cmp_half(i))
            for n in range(16):
                start(item(n))
            yield from vunit(m1["vsw"], ring, ev_vsw)
            h_over.extend([H.used[kt] for kt in range(KT)])
            for i in range(2):
                yield from out_tiles(m1[f"wh{i}"], 4, 4 * i, ring, None)
            start(rotary_tables())
            yield from out_tiles(m1["wn0"], 0, 0, ring, None)
            new_norm()
            yield from out_tiles(m1["wn1"], 2, 0, ring, 8)

        csslot, cs_in, hm_last = Slot(semaphore("s_cs")), [None], [None]

        def rotary_tables():
            sp.wait(hm_last[0])
            for i in range(2):
                cs_in[0] = dma(sp, csslot, CS[:, i, :], A["c_rope"][i])
            yield None

        def plan_mixer2(l):
            got = {}
            w, wo = A["w_in_2"][l], A["w_o_2"][l]
            for part, c in (("d", 1536), ("s", 0)):
                for name in ("qk0", "v0", "qk1", "qk2", "qk3", "v1"):
                    i = int(name[-1])
                    if name[0] == "q":
                        src = [w[:, c + 128 * i:c + 128 * i + 128], w[:, c + 512 + 128 * i:c + 512 + 128 * i + 128]]
                    else:
                        src = [w[:, c + 1024 + 256 * i:c + 1280 + 256 * i]]
                    got[part + name] = plan(src, KT)
            for i in range(2):
                got[f"od{i}"] = plan([wo[512:1024, 512 * i:512 * i + 512]], 4)
            for i in range(2):
                got[f"os{i}"] = plan([wo[256 * i:256 * i + 256, :]], 2)
            return got

        def mixer2(l, M):
            init = 0.8 - 0.6 * float(np.exp(-0.3 * l))

            def nm(x):
                return f"{x}_{l}"

            o = o_a + 6 * KB
            u_at = [o_u + 2048 * i for i in range(8)] + [o_u + 16384 + 2048 * i for i in range(8)]
            sets = [[o + 2 * KB * i for i in range(5)], [o + (10 + 2 * i) * KB for i in range(5)],
                    [u_at[k] for k in (12, 13, 14, 15, 8)]]
            QSET = [[at(nm(f"QT{i}{x}"), [128, T], F32R, s[x]) for x in range(2)] for i, s in enumerate(sets)]
            KSET = [[at(nm(f"KT{i}{x}"), [128, T], F32R, s[2 + x]) for x in range(2)] for i, s in enumerate(sets)]
            KLO = [at(nm(f"KL{i}"), [128, T], F32R, s[4]) for i, s in enumerate(sets)]
            SET = {"d": (0, 1, 2, 0), "s": (1, 0, 1, 0)}
            o = o_a + 26 * KB
            VSET = [at(nm(f"VS{i}"), [128, 4, 512], F32R, o + 8 * KB * i) for i in range(2)]
            o = o_a + 42 * KB
            E0 = Ring([at(nm(f"E0{i}"), [128, 1280], F32, o + 5 * KB * i) for i in range(2)])
            E1 = Ring([at(nm("E1"), [128, 1280], F32, o + 10 * KB)])
            PT = Ring([(at(nm("PH"), [128, 1280], F32R, o + 15 * KB), at(nm("PL"), [128, 1280], F32R, o + 20 * KB))])
            TMD = Ring([at(nm("TMD"), [128, T], F32, o + 25 * KB)])
            ST = at(nm("ST"), [128, 4, 16], F32, o + 27 * KB)
            STR = Ring([ST[:, i, :] for i in range(4)])
            EV = Ring([at(nm(f"EV{i}"), [128, T], F32, u_at[k]) for i, k in enumerate((2, 10, 3, 11))])
            XO = [at(nm(f"XO{h}"), [128, T], F32, u_at[4 + h]) for h in range(4)]
            DN = at(nm("DN"), [128, 4, 16], F32, u_at[9])
            dn = Hold()
            dn.free = None
            RO = Ring([at(nm(f"RO{i}"), [128, T], F32, o_a + 2 * KB * i) for i in range(3)] + [at(nm("RO3"), [128, T], F32, u_at[1])])

            qk_set, v_set = [Hold() for _ in sets], [Hold(), Hold()]
            set_got, qk_ready, v_ready = {}, {}, {}
            U.ev = {}
            norm = norms[-1]

            def q_halves(dst, src, ev, got):
                yield ev
                act.wait(ev, *got)
                for x in range(2):
                    own = slice(64 * x, 64 * x + 64)
                    c = copy(act, dst[x][own, :], src[own, :])
                yield c
                dve.wait(ev, c, *got)
                for x in range(2):
                    own, other = slice(64 * x, 64 * x + 64), slice(64 - 64 * x, 128 - 64 * x)
                    d = diff(dve, dst[x][other, :], src[own, :], dst[x][own, :])
                return d

            def k_halves(dst, lo, src, ev, got):
                yield ev
                act.wait(ev, *got)
                for x in range(2):
                    own = slice(64 * x, 64 * x + 64)
                    c = copy(act, dst[x][own, :], src[own, :])
                yield c
                dve.wait(ev, c, *got)
                for x in range(2):
                    own, other = slice(64 * x, 64 * x + 64), slice(64 - 64 * x, 128 - 64 * x)
                    diff(dve, lo[own, :], src[own, :], dst[x][own, :])
                    d = copy(dve, dst[x][other, :], dst[x][own, :])
                return d

            def set_taken(key, hold):
                if key not in set_got:
                    set_got[key] = None
                    set_got[key] = yield from take(hold)
                while set_got[key] is None:
                    yield lambda: set_got[key] is not None
                return set_got[key]

            def halves(i, key, n, x, a, got):
                if i == 0:
                    d = yield from q_halves(QSET[n], x, a, got)
                else:
                    d = yield from k_halves(KSET[n], KLO[n], x, a, got)
                qk_ready.setdefault(key, []).append(d)
                return d

            def ev_sqk(p):
                def evac(i, b, m):
                    yield from has_rb(norm)
                    n = SET["s"][p]
                    got = yield from set_taken(("s", p), qk_set[n])
                    xb, xg = yield from EV.next()
                    x = xb.buf[:]
                    dve.wait(m, norm.rb, *xg)
                    a = stt(dve, x, P[:, b.i, :], 0.125 if i == 0 else 1.0, RB[:], ALU.mult, ALU.mult)
                    rb_read["dve"] = a
                    b.give(a)
                    d = yield from halves(i, ("s", p), n, x, a, got)
                    xb.give(d)
                return evac

            def ev_v(part, p):
                def evac(tp, b, m):
                    yield from has_rt(norm)
                    got = yield from set_taken((part + "v", p), v_set[p])
                    vs = VSET[p]
                    act.wait(m, norm.rt, *got)
                    dv = []
                    for q in range(2):
                        t = 2 * tp + q
                        src = P[:, b.i, 256 * q:256 * q + 256]
                        if part == "s":
                            src = src.rearrange("p (n d) -> p n d", n=4)
                            dst = vs[:, t, :].rearrange("p (n x d) -> p n x d", n=4, x=2)
                            hi, lo = dst[:, :, 0, :], dst[:, :, 1, :]
                        else:
                            hi, lo = vs[:, t, 0:256], vs[:, t, 256:512]
                        c = activ(hi, src, AF.Identity, scale=RT[:, t:t + 1])
                        dv.append((lo, src, RT[:, t:t + 1], hi))
                    rt_read["act"] = c
                    yield c
                    dve.wait(m, c, norm.rt, *got)
                    for lo, src, r, hi in dv:
                        d = stt(dve, lo, src, r, hi, ALU.mult, ALU.subtract)
                    rt_read["dve"] = d
                    b.give(d)
                    v_ready.setdefault((part, p), []).append(d)
                return evac

            ro = RO.all
            rslot = [Slot(semaphore(nm(f"s_ro{i}"))) for i in range(4)]

            def ev_dqk(h):
                def evac(i, b, m):
                    yield from has_rb(norm)
                    n = SET["d"][h]
                    got = yield from set_taken(("d", h), qk_set[n])
                    rb, rrb, rg = yield from RO.pair()
                    r, rr = rb.buf, rrb.buf
                    if i == 0:
                        act.wait(m, *rg)
                        a = copy(act, r[:], P[:, b.i, :])
                    else:
                        dve.wait(m, norm.rb, *rg)
                        a = tt(dve, r[:], P[:, b.i, :], RB[:], ALU.mult)
                        rb_read["dve"] = a
                    b.give(a)
                    yield a
                    sp.wait(a, *rg)
                    for k in range(4):
                        src = 32 * (k ^ 1)
                        s = dma(sp, rslot[rb.i], rr[32 * k:32 * k + 32, :], r[src:src + 32, :])
                    yield s
                    pool.wait(s, cs_in[0])
                    w = tt(pool, rr[:], rr[:], CS[:, 1, :], ALU.mult)
                    dve.wait(s, cs_in[0])
                    c = tt(dve, r[:], r[:], CS[:, 0, :], ALU.mult)
                    yield w
                    dve.wait(c, w)
                    a = tt(dve, r[:], r[:], rr[:], ALU.add)
                    rrb.give(a)
                    d = yield from halves(i, ("d", h), n, r, a, got)
                    rb.give(d)
                return evac

            s_order, t_order, v_order = Order(), Order(), Order()

            def scores2(b, ts_, n, x, mask, ready, got):
                own = slice(64 * x, 64 * x + 64)
                q, hh, lo = QSET[n][x], KSET[n][x], KLO[n]
                pe.wait(*ready, *got, got_in["maskb"])
                for t in ts_:
                    o = spot(t)
                    k = slice(0, 128 * (t + 1))
                    matmul(o, q[:, 128 * t:128 * t + 128], hh[:, k], True, False)
                    matmul(o, q[own, 128 * t:128 * t + 128], lo[own, k], False, False)
                    m = matmul(o[:, 128 * t:128 * t + 128], IDB[:], MASKB[:, mask, :], False, True)
                return m

            flat = P[:, 2:5, :].rearrange("p b c -> p (b c)")[:, 0:1280]

            def sb_head(h):
                p, x, n = h // 2, h % 2, SET["s"][h // 2]
                yield from s_order.turn(4 + h)
                while len(qk_ready.get(("s", p), [])) < 2:
                    yield lambda: len(qk_ready.get(("s", p), [])) == 2
                e0, got0 = yield from E0.next()
                for b, ts_ in CHUNKS:
                    got = yield from take(bank[b])
                    m = scores2(b, ts_, n, x, 1, qk_ready[("s", p)], got)
                if x == 1:
                    qk_set[n].give(m)
                s_order.done()
                yield m
                act.wait(m, *got0)
                bt = activ(e0.buf[:], flat, AF.Sigmoid)
                e1, got1 = yield from E1.next()
                act.wait(*got1)
                kp = activ(e1.buf[:], flat, AF.Sigmoid, scale=-1.0)
                for b, _ in CHUNKS:
                    bank[b].give(kp)
                yield kp
                dve.wait(kp)
                for t in range(4):
                    c0, c1 = scol(t)
                    v = e1.buf[:, slice(c1 - 1, c0 - 1 if c0 else None, -1)]
                    one = ONES[:, 0:1].to_broadcast([128, c1 - c0])
                    s = dve(lambda e, v=v, one=one: e.tensor_tensor_scan(v, v, one, 1.0, ALU.mult, ALU.mult),
                            vcost(dve, c1 - c0))
                yield s
                pool.wait(s, bt)
                w = tt(pool, e0.buf[:, 0:1279], e0.buf[:, 0:1279], e1.buf[:, 1:1280], ALU.mult)
                e1.give(w)
                yield w
                yield from t_order.turn(4 + h)
                pt, pt_got = yield from PT.next()
                turned = yield from turn(e0, [w], pt, pt_got, t_order)
                ph, pl = pt.buf
                yield from v_order.turn(4 + h)
                g = h // 4
                while len(v_ready.get(("s", g), [])) < 2:
                    yield lambda: len(v_ready.get(("s", g), [])) == 2
                got = yield from take(bank[7])
                c = 128 * (h % 4)
                m = values(lambda j: VSET[g][:, j, c:c + 128], ph, pl, turned + v_ready[("s", g)] + got, True, True)
                pt.give(m)
                v_order.done()
                yield m
                yield from fold(h, m, ro[0], ro[1], mix_free)
                if h == 7:
                    ring.extend(bank[2:8])

            def mix_free(kt):
                if kt >= 2:
                    while len(qk_ready.get(("s", 3), [])) < 2:
                        yield lambda: len(qk_ready.get(("s", 3), [])) == 2
                got = []
                for h in {0: [], 1: [ro[3], dn], 2: EV.all[0:2], 3: EV.all[2:4]}[kt]:
                    got += yield from take(h)
                return got

            RT8 = SM[:, 36:40]
            sln = SM[:, 44 + l:45 + l]

            def df_head(h):
                n, g = SET["d"][h], h // 2
                o_ = h
                yield from s_order.turn(o_)
                while len(qk_ready.get(("d", h), [])) < 2:
                    yield lambda: len(qk_ready.get(("d", h), [])) == 2
                es, sts, done = [], [], [[], []]

                def soft(mp, b, ts_, m, got, st_got):
                    r, x, a = yield from row_softmax(b, ts_, sts[mp].buf, RT8.unsqueeze(2), 0, rt8[0], es[mp].buf, m, got, st_got)
                    if mp == 1:
                        st = sts[1].buf
                        dve.wait(a, got_in["lambda"])
                        a = ts(dve, st[:, 8:12][:, r], st[:, 8:12][:, r], LAM[:, l:l + 1], ALU.mult)
                        yield a
                        for t in ts_:
                            c = scol(t)
                            p = es[1].buf[:, c[0]:c[1]]
                            lane, scale = scale_rows(p, p, st[:, 8 + t:9 + t])
                            lane.wait(a, x)
                            done[1].append(scale())
                    else:
                        done[0].append(a)

                for mp in range(2):
                    e, got = yield from (E0, E1)[mp].next()
                    st, st_got = yield from STR.next()
                    es.append(e)
                    sts.append(st)
                    for b, ts_ in CHUNKS:
                        bg = yield from take(bank[b])
                        m = scores2(b, ts_, n, mp, 2, qk_ready[("d", h)], bg)
                        start(soft(mp, b, ts_, m, got, st_got), m)
                qk_set[n].give(m)
                s_order.done()
                while len(done[0]) < 3 or len(done[1]) < 4:
                    yield lambda: len(done[0]) == 3 and len(done[1]) == 4
                yield done[0] + done[1]
                dve.wait(*done[0], *done[1])
                for t in (3, 2, 0, 1):
                    c = scol(t)
                    p = es[0].buf[:, c[0]:c[1]]
                    a = stt(dve, p, p, sts[0].buf[:, 8 + t:9 + t], es[1].buf[:, c[0]:c[1]], ALU.mult, ALU.subtract)
                es[1].give(a)
                sts[0].give(a)
                sts[1].give(a)
                yield a
                yield from t_order.turn(o_)
                pt, pt_got = yield from PT.next()
                turned = yield from turn(es[0], [a], pt, pt_got, t_order)
                ph, pl = pt.buf
                yield from v_order.turn(o_)
                while len(v_ready.get(("d", g), [])) < 2:
                    yield lambda: len(v_ready.get(("d", g), [])) == 2
                got = yield from take(bank[7])
                vs, c = VSET[g], 128 * (h % 2)
                pe.wait(*got, *turned, *v_ready[("d", g)])
                for j in range(4):
                    r = trow(j)
                    o = P[:, 7, 128 * j:512]
                    vh, vl = vs[:, j, c:c + 128], vs[:, j, 256 + c:384 + c]
                    matmul(o, vh, ph[:, r[0]:r[1]], j == 0, False)
                    matmul(o, vh, pl[:, r[0]:r[1]], False, False)
                    m = matmul(o, vl, ph[:, r[0]:r[1]], False, j == 3)
                pt.give(m)
                if h % 2 == 1:
                    v_set[g].give(m)
                v_order.done()
                yield m
                tb, got = yield from TMD.next()
                act.wait(m, *got)
                s = activ(tb.buf[:], P[:, 7, :], AF.Square)
                x = o_ev[h] = copy(act, XO[h][:], P[:, 7, :])
                bank[7].give(x)
                yield s
                b, got = yield from take_one(bank[5:7])
                pe.wait(s, *got)
                for t in range(4):
                    m = matmul(P[:, b.i, 2 * t:2 * t + 2], tb.buf[:, 128 * t:128 * t + 128], ONES[:, 0:2], True, True)
                tb.give(m)
                yield m
                dve.wait(m)
                ms = ts(dve, DN[:, 0, 4 * h:4 * h + 4], P[:, b.i, 0:8:2], 1.0 / 128, ALU.mult, EPS, ALU.add)
                b.give(ms)
                sums.append(ms)
                if len(sums) == 4:
                    start(df_norm(), ms)

            o_ev, sums = {}, []

            def df_norm():
                act.wait(*sums)
                s = activ(DN[:, 1, :], DN[:, 0, :], AF.Sqrt)
                yield s
                dve.wait(s, *sums)
                r = rsqrt_step(DN[:, 2, :], DN[:, 1, :], DN[:, 0, :], DN[:, 3, :], sums[-1])
                for h in range(4):
                    tb, got = yield from TMD.next()
                    dve.wait(r, *got)
                    for t in range(4):
                        c = 4 * h + t
                        d = ts(dve, tb.buf[:, 128 * t:128 * t + 128], IDN, DN[:, 2, c:c + 1], ALU.mult)
                    yield d
                    b, got = yield from take_one(bank[5:7])
                    pe.wait(d, *got)
                    m = matmul(P[:, b.i, :], ONES[:], tb.buf[:], True, True)
                    yield m
                    dve.wait(m, o_ev[h], sln_ev[0])
                    y = stt(dve, tb.buf[:], XO[h][:], sln, P[:, b.i, :], ALU.mult, ALU.mult)
                    b.give(y)
                    yield y
                    yield from mix_halves(4 + h, tb.buf[:], y)
                    tb.give(U.ev[4 + h])
                dn.give(d)

            rt8, sln_ev = [None], [None]

            def scales():
                yield from has_rt(norm)
                dve.wait(norm.rt)
                rt8[0] = ts(dve, RT8, RT, 0.125, ALU.mult)
                rt_read["dve"] = rt8[0]
                sln_ev[0] = ts(dve, sln, GT[:, 53 + l:54 + l], 1.0 - init, ALU.mult)

            ring = [bank[0], bank[1]]
            start(scales())
            for h in range(4):
                start(df_head(h))
            for h in range(8):
                start(sb_head(h))
            for part, ev in (("d", ev_dqk), ("s", ev_sqk)):
                if part == "d":
                    yield from unit(M["dqk0"], H, bank[2:5], ev_dqk(0), kouter=True)
                else:
                    yield from unit(M["sqk0"], H, ring, ev_sqk(0))
                yield from vunit(M[part + "v0"], ring, ev_v(part, 0))
                for i in (1, 2, 3):
                    yield from unit(M[f"{part}qk{i}"], H, ring, ev(i))
                yield from vunit(M[part + "v1"], ring, ev_v(part, 1))
            for i in range(2):
                yield from out_tiles(M[f"od{i}"], 4, 4 * i, ring, None)
            yield from out_tiles(M["os0"], 0, 0, ring, None)
            new_norm()
            yield from out_tiles(M["os1"], 2, 0, ring, 32 + 8 * l)

        def plan_ffn1():
            w, wd = A["w_gate_up"][0], A["w_down"][0]
            got = []
            for n, j0 in ((8, 0), (8, 8), (6, 16)):
                for j in range(j0, j0 + n, 2):
                    got.append(plan([w[:, 128 * j:128 * j + 256]], KT))
                    got.append(plan([w[:, D_FF + 128 * j:D_FF + 128 * j + 256]], KT))
                for o in range(0, D, 256):
                    got.append(plan([wd[128 * j0:128 * (j0 + n), o:o + 256]], n))
            return got

        def plan_ffn2(l):
            w, wd = A["w_ff1_2"][l], A["w_ff2_2"][l]
            got = []
            for j0 in range(0, 32, 8):
                for j in range(j0, j0 + 8, 2):
                    got.append(plan([w[:, 128 * j:128 * j + 256]], KT))
                for o in range(0, D, 256):
                    got.append(plan([wd[128 * j0:128 * (j0 + 8), o:o + 256]], 8))
            return got

        m1, f1 = plan_mixer1(), plan_ffn1()
        m20, f20 = plan_mixer2(0), plan_ffn2(0)
        m21, f21 = plan_mixer2(1), plan_ffn2(1)

        def whole():
            new_norm()
            got_in["idn"] = dma(sp, cslot, BM[:], A["c_idn"])
            load_x(0)
            got_in["gt"] = dma(sp, gslot, GT[:], A["p_vec"])
            pump()
            start(opening())
            start(splitter())
            yield from mixer1(m1)
            yield from ffn("1", f1, (8, 8, 6), True, 16)
            yield from mixer2(0, m20)
            yield from ffn("2", f20, (8, 8, 8, 8), False, 24)
            yield from mixer2(1, m21)
            yield from ffn_last(f21)

        start(whole())
        tasks.run()

        for lane in lanes:
            lane.number()
        block = ctx.enter_context(nc.Block())

        @block.tensor
        def _(e):
            pe.play(e)

        @block.scalar
        def _(e):
            act.play(e)

        @block.vector
        def _(e):
            dve.play(e)

        @block.gpsimd
        def _(e):
            pool.play(e)

        @block.sync
        def _(e):
            sp.play(e)


def constants(inputs):
    i = np.arange(128)
    t, s = i[:, None], i[None, :]
    tok = 128 * (np.arange(128) // 32)[None, :] + t
    n = (np.arange(128) % 32)[None, :]
    seen = (16 * n + 31 <= tok) & (n < 31)
    eye = np.eye(128, dtype=np.float32)
    idn = np.concatenate([eye, (t // 64 == s // 64).astype(np.float32), seen.astype(np.float32)], axis=1)
    mask = np.zeros((128, 512), np.float32)
    mask[:, 0:128] = np.where(s <= t, 0, NEG)
    mask[:, 128:256] = np.where(s < t, 0, NEG)
    mask[:, 256:384] = np.where(s // 64 <= t // 64, 0, NEG)
    mask[:, 384:512] = np.where(seen, 0, NEG)
    d = np.arange(0, 64, 2, dtype=np.float32)
    inv = (np.float32(1.0) / (np.float32(10000.0) ** (d / np.float32(64)))).astype(np.float32)
    ang = np.arange(T, dtype=np.float32)[None, :] * inv[i % 32][:, None]
    rope = np.stack([np.cos(ang), np.where(t % 64 < 32, -1, 1) * np.sin(ang)]).astype(np.float32)
    hg = np.zeros((128, 6, 128), np.float32)
    hg[:, 0, :] = eye
    for n, h in enumerate((1, 2, 4, 8, 16)):
        hg[:, n + 1, :] = (t // (2 * h) == s // (2 * h)) & (t // h % 2 == 0) & (s // h % 2 == 1)

    def vec(name):
        return np.asarray(inputs[name])

    rows = [vec(n).reshape(-1, 128) for n in ("norm_mix", "norm_ffn", "attn_norm_2", "mlp_norm_2")]
    rows += [np.concatenate([r, r], axis=1) for r in (vec("q_norm"), vec("k_norm")[0])]
    rows += [vec("hgrn_o_norm"), vec("subln_norm_2"), vec("hgrn_lb_logits").reshape(8, 128)]
    rows += [np.zeros((1, 128), np.float32)]
    rows += [np.concatenate([r, r], axis=1) for r in (vec("cmp_pos_k")[0], vec("cmp_pos_v")[0])]
    vecs = np.ascontiguousarray(np.concatenate(rows, axis=0).T)
    lam = np.concatenate([vec(n).reshape(1, 128) for n in ("lam_q1_2", "lam_k1_2", "lam_q2_2", "lam_k2_2")], axis=1)[0]
    return {"c_rope": rope, "c_hg": hg, "c_idn": idn, "c_mask": mask, "p_vec": vecs, "p_lam": lam}


_INS = ["x", "norm_mix", "w_in", "q_norm", "k_norm", "cmp_pos_k", "cmp_pos_v", "cmp_k_w1", "cmp_k_w2", "cmp_v_w1",
        "cmp_v_w2", "hgrn_lb_logits", "hgrn_o_norm", "w_out", "norm_ffn", "w_gate_up", "w_down", "w_in_2", "w_o_2",
        "attn_norm_2", "subln_norm_2", "lam_q1_2", "lam_k1_2", "lam_q2_2", "lam_k2_2", "mlp_norm_2", "w_ff1_2",
        "w_ff2_2", "final_norm_2"]
_OUTS = [((1, 512, 1024), "float32")]


def kernel(**inputs):
    import numpy as _np
    import concourse.bacc as _bacc
    from concourse import mybir as _mybir
    from concourse.bass_utils import run_bass_kernel_spmd as _run

    nc = _bacc.Bacc("TRN2", target_bir_lowering=False, num_devices=1)
    given = {name: inputs[name] for name in _INS}
    given.update(constants(inputs))
    arrays, aps = {}, {}
    for name, value in given.items():
        a = _np.ascontiguousarray(value)
        arrays[f"in_{name}_dram"] = a
        aps[name] = nc.dram_tensor(f"in_{name}_dram", a.shape, _mybir.dt.from_np(a.dtype), kind="ExternalInput").ap()
    shape, dtype = _OUTS[0]
    out = nc.dram_tensor("out_0_dram", shape, _mybir.dt.from_np(_np.dtype(dtype)), kind="ExternalOutput").ap()
    program(nc, aps, out)
    r = _run(nc, [arrays], core_ids=[0])
    return r.results[0]["out_0_dram"]
```

```python
import numpy as np
import concourse.bass as bass
from concourse import mybir
from concourse.alu_op_type import AluOpType as ALU
from contextlib import ExitStack

F32 = mybir.dt.float32
F32R = mybir.dt.float32r
BF16 = mybir.dt.bfloat16
U32 = mybir.dt.uint32
AF = mybir.ActivationFunctionType
AX = mybir.AxisListType

T = 512
D = 1024
KT = D // 128
NEG = -1e30
EPS = 1e-6
D_FF = 2816


class Step:

    def __init__(self, end, sem=None, value=None):
        self.end, self.sem, self.value, self.signals = end, sem, value, False


class Slot:

    def __init__(self, sem):
        self.sem, self.count = sem, 0


class Lane:
    dma_end = 0.0

    def __init__(self, sem, hop):
        self.sem, self.hop, self.items, self.clock, self.ready = sem, hop, [], 0.0, 0.0

    def __call__(self, fn, cost):
        self.clock = max(self.clock, self.ready) + cost
        self.ready = 0.0
        step = Step(self.clock)
        self.items.append((step, fn))
        return step

    def wait(self, *steps):
        for s in steps:
            if s is not None:
                s.signals = True
                self.ready = max(self.ready, s.end + self.hop)
                self.items.append((s, None))

    def dma(self, slot, fn, cost):
        slot.count += 16
        self.clock = max(self.clock, self.ready) + 0.65
        self.ready = 0.0
        Lane.dma_end = max(self.clock + 1.0, Lane.dma_end) + cost
        step = Step(Lane.dma_end + 0.5, slot.sem, slot.count)
        self.items.append((step, fn))
        return step

    def number(self):
        n = 0
        for step, fn in self.items:
            if fn is not None and step.sem is None and step.signals:
                n += 1
                step.sem, step.value = self.sem, n

    def play(self, eng):
        seen = {}
        for step, fn in self.items:
            if fn is None:
                if seen.get(step.sem.name, 0) < step.value:
                    eng.wait_ge(step.sem, step.value)
                    seen[step.sem.name] = step.value
                continue
            ins = fn(eng)
            if step.sem is not None:
                ins.then_inc(step.sem, 1 if step.sem is self.sem else 16)


class Hold:

    def __init__(self):
        self.free = []

    def give(self, *steps):
        self.free = list(steps)


class Late(list):
    pass


class Tasks:

    LOOK = 0.35
    MARGIN = 0.3
    PATIENCE = 2.0

    def __init__(self):
        self.now, self.queue, self.parked, self.count = 0.0, [], [], 0

    def push(self, time, task, lane=None, until=0.0):
        self.count += 1
        self.queue.append((max(time, self.now), self.count, task, lane, until))

    def start(self, task, *after):
        self.push(max([s.end for s in after if s is not None], default=0.0), task)

    def run(self):
        while self.queue:
            first = min(self.queue, key=lambda q: q[:2])
            self.queue.remove(first)
            self.now, _, task, lane, until = first
            if lane is not None and lane.clock - self.LOOK > self.now and self.now < until:
                self.push(min(until, lane.clock - self.LOOK), task, lane, until)
                continue
            try:
                got = next(task)
            except StopIteration:
                got = ()
                task = None
            if task is None:
                pass
            elif isinstance(got, Lane):
                self.push(got.clock - self.LOOK, task, got, max(self.now, got.clock - self.LOOK) + self.PATIENCE)
            elif callable(got):
                self.parked.append((got, task))
            else:
                late = self.MARGIN if isinstance(got, Late) else 0.0
                got = got if isinstance(got, (tuple, list)) else (got,)
                self.push(max([s.end for s in got if s is not None], default=0.0) + late, task)
            still = []
            for cond, t in self.parked:
                if cond():
                    self.push(self.now, t)
                else:
                    still.append((cond, t))
            self.parked = still
        assert not self.parked, "tasks wait for each other"


def take(*holds):
    while not all(h.free is not None for h in holds):
        yield lambda: all(h.free is not None for h in holds)
    got = [s for h in holds for s in h.free]
    for h in holds:
        h.free = None
    yield got
    return got


def take_one(holds):
    while not any(h.free is not None for h in holds):
        yield lambda: any(h.free is not None for h in holds)
    h = min((h for h in holds if h.free is not None), key=lambda h: max([s.end for s in h.free if s is not None], default=0.0))
    got, h.free = h.free, None
    yield got
    return h, got


def program(nc, A, out):
    ctx = ExitStack()
    with ctx:
        def semaphore(name):
            return ctx.enter_context(nc.semaphore(name))

        pe, act, dve, pool, sp = (Lane(semaphore(n), hop) for n, hop in (
            ("s_pe", 0.25), ("s_act", 0.18), ("s_dve", 0.18), ("s_pool", 0.18), ("s_sp", 0.1)))
        lanes = (pe, act, dve, pool, sp)
        Lane.dma_end = 0.0
        tasks = Tasks()
        start = tasks.start

        base = (nc.sbuf_base + 63) // 64 * 64
        room = nc.sbuf_usable_end - base

        def at(name, shape, dt, off):
            size = int(np.prod(shape[1:])) * mybir.dt.size(dt)
            assert off % 32 == 0 and off + size <= room, (name, off, size, room)
            return nc.alloc_sbuf_tensor_at(name, shape, dt, offset=base + off)

        KB = 1024
        NR, NS = 2, 4
        o_x = 0
        o_h = o_x + 16384
        o_raw = o_h + 32768
        o_ws = o_raw + NR * 8192
        o_u = o_ws + NS * 8192
        o_c = o_u + 32768
        XT = at("XT", [128, KT, T], F32, o_x)
        HH = at("HH", [128, KT, T], F32R, o_h)
        HL = at("HL", [128, KT, T], F32R, o_h + 16384)
        RAW = at("RAW", [128, NR, 2048], F32, o_raw)
        WH = at("WH", [128, NS, 1024], F32R, o_ws)
        WL = at("WL", [128, NS, 1024], F32R, o_ws + NS * 4096)
        UH = at("UH", [128, KT, T], F32R, o_u)
        UL = at("UL", [128, KT, T], F32R, o_u + 16384)
        P = ctx.enter_context(nc.psum_tensor("ps", [128, 8, 512], F32))

        off = [o_c]

        def const(name, shape, dt):
            t = at(name, shape, dt, off[0])
            off[0] += (int(np.prod(shape[1:])) * mybir.dt.size(dt) + 31) // 32 * 32
            return t

        BM = const("BM", [128, 384], F32)
        IDN, BLK, M01 = BM[:, 0:128], BM[:, 128:256], BM[:, 256:384]
        ONES = const("ONES", [128, 8], F32)
        MT = const("MT", [128, 2, T], BF16)
        GT = const("GT", [128, 128], F32)
        CS_off = off[0]
        CS = const("CS", [128, 2, T], F32)
        RB = const("RB", [128, T], F32)
        SM = const("SM", [128, 64], F32)
        RT = SM[:, 0:4]
        STD = SM[:, 4:8]
        EPSC = SM[:, 8:9]
        LB = SM[:, 12:16]
        LB1 = SM[:, 16:20]
        QFOLD = SM[:, 20:23]
        LAM = SM[:, 24:26]
        MS = SM[:, 28:32]
        NW = SM[:, 60:64]
        o_a = (off[0] + 63) // 64 * 64

        def cols(a):
            return int(np.prod(a.shape[1:]))

        def matmul(o, l, r, start, stop):
            n = cols(r)
            if r.dtype == F32:
                c = max(0.2, n * 1.65e-3)
            else:
                c = max(0.053 if r.dtype == BF16 else 0.103, n * 0.417e-3)
            return pe(lambda e: e.matmul(o, l, r, start=start, stop=stop), c)

        def transpose(o, i, ident):
            return pe(lambda e: e.transpose(o, i, ident), 0.107)

        def vcost(lane, n, fast=False):
            if lane is dve:
                return 0.06 + n * (0.52e-3 if fast else 1.04e-3)
            if lane is pool:
                return 0.2 + n * 2e-3
            return 0.17 + n * 0.7e-3

        def tt(lane, o, a, b, op):
            return lane(lambda e: e.tensor_tensor(o, a, b, op), vcost(lane, cols(o)))

        def ts(lane, o, a, s1, op0, s2=None, op1=None):
            c = vcost(lane, cols(o), True)
            if op1 is None:
                return lane(lambda e: e.tensor_scalar(o, a, s1, None, op0), c)
            return lane(lambda e: e.tensor_scalar(o, a, s1, s2, op0, op1), c)

        def stt(lane, o, a, s, b, op0, op1):
            return lane(lambda e: e.scalar_tensor_tensor(o, a, s, b, op0, op1), vcost(lane, cols(o)) + 0.06)

        def copy(lane, o, a):
            c = vcost(lane, cols(o), True)
            if lane is act:
                return lane(lambda e: e.copy(o, a), c)
            return lane(lambda e: e.tensor_copy(o, a), c)

        table = [None]

        def activ(o, a, func, scale=1.0, bias=None, accum=None):
            kw = {}
            if bias is not None:
                kw["bias"] = bias
            if accum is not None:
                kw["accum_out"] = accum
            c = 0.2 + cols(o) * 0.72e-3
            kind = AF.Exp if func == AF.Ln else func
            if kind not in (AF.Identity, AF.Square, table[0]):
                table[0] = kind
                act.clock += 1.3
            return act(lambda e: e.activation(o, a, func, scale=scale, **kw), c)

        def scale_rows(o, a, col):
            n = cols(o)
            if dve.clock + 3.0 + vcost(dve, n, True) <= pool.clock + vcost(pool, n):
                return dve, lambda: ts(dve, o, a, col, ALU.mult)
            return pool, lambda: tt(pool, o, a, col.to_broadcast([128, n]), ALU.mult)

        def recip(o, a):
            return dve(lambda e: e.reciprocal(o, a), 0.06 + cols(o) * 6.3e-3)

        def mask_min(o, a, mask, scale, least):
            return dve(lambda e: e.tensor_tensor_reduce(o, a, mask, scale, 3e38, ALU.add, ALU.min, least),
                       0.13 + cols(o) * 1.04e-3)

        def zero(lane, o):
            return lane(lambda e: e.memset(o, 0.0), 0.46)

        def diff(lane, o, a, b):
            return tt(lane, o, a, b, ALU.subtract)

        def dma(lane, slot, o, i):
            return lane.dma(slot, lambda e: e.dma_start(o, i), int(np.prod(o.shape)) * 4 / 350e3)

        bank = [Hold() for _ in range(8)]
        for b in range(8):
            bank[b].i = b

        class Unit:
            pass

        units = []

        def plan(src_cols, nk):
            u = Unit()
            u.src, u.nk, u.arrived = src_cols, nk, None
            u.width = sum(s.shape[-1] for s in src_cols)
            u.half = u.width // 2 if u.width > 128 else u.width
            u.slots, u.ready = [], [None] * (u.width // u.half)
            u.i = len(units)
            units.append(u)
            return u

        wslots = [Slot(semaphore(f"s_w{i}")) for i in range(NR)]
        raw = [Hold() for _ in range(NR)]
        wslot = [Hold() for _ in range(NS)]
        loads = [0]
        small_loads = {}

        def pump():
            while loads[0] < len(units) and raw[loads[0] % NR].free is not None:
                u = units[loads[0]]
                r = u.i % NR
                sp.wait(*raw[r].free)
                raw[r].free = None
                c = 0
                for s in u.src:
                    w = s.shape[-1]
                    dst = RAW[:, r, 0:u.nk * u.width].rearrange("p (k c) -> p k c", k=u.nk)[:, :, c:c + w]
                    u.arrived = dma(sp, wslots[r], dst, s.rearrange("(k p) c -> p k c", p=128))
                    c += w
                loads[0] += 1
                if u.i in small_loads:
                    small_loads[u.i]()

        def splitter():
            for u in units:
                r = u.i % NR
                while u.arrived is None:
                    yield lambda: u.arrived is not None
                rv = RAW[:, r, 0:u.nk * u.width].rearrange("p (k c) -> p k c", k=u.nk)
                for t in range(u.width // u.half):
                    s = (2 * u.i + t) % NS
                    u.slots.append(s)
                    hv = WH[:, s, 0:u.nk * u.half].rearrange("p (k c) -> p k c", k=u.nk)
                    lv = WL[:, s, 0:u.nk * u.half].rearrange("p (k c) -> p k c", k=u.nk)
                    src = rv[:, :, t * u.half:(t + 1) * u.half]
                    got = yield from take(wslot[s])
                    yield u.arrived
                    n = cols(hv)
                    yield act
                    act.wait(u.arrived, *got)
                    h = copy(act, hv, src)
                    yield h
                    lane = dve if dve.clock + vcost(dve, n) <= pool.clock + vcost(pool, n) else pool
                    yield lane
                    lane.wait(h)
                    u.ready[t] = diff(lane, lv, src, hv)
                raw[r].give(*u.ready)
                pump()

        def wtile(u, n):
            per = max(1, u.half // 128)
            return n // per, (n % per) * 128

        class Halves:

            def __init__(self, hi, lo):
                self.hi, self.lo, self.ev, self.used = hi, lo, {}, {}

        H, U = Halves(HH, HL), Halves(UH, UL)

        def unit(us, src, ring, evac, k0=0, kouter=False):
            us = us if isinstance(us, list) else [us]
            rows = [(u, k) for u in us for k in range(u.nk)]
            n = us[0].width // 128
            tiles = [(i, kt) for kt in range(len(rows)) for i in range(n)] if kouter else \
                    [(i, kt) for i in range(n) for kt in range(len(rows))]
            held = [None] * n
            for i, kt in tiles:
                u, k = rows[kt]
                t, c0 = wtile(u, i)
                if kt == 0:
                    held[i] = yield from take_one(ring)
                while u.ready[t] is None or k0 + kt not in src.ev:
                    yield lambda: u.ready[t] is not None and k0 + kt in src.ev
                yield u.ready[t], src.ev[k0 + kt]
                yield pe
                s, b = u.slots[t], held[i][0].i
                a = k * u.half + c0
                wh, wl = WH[:, s, a:a + 128], WL[:, s, a:a + 128]
                o = P[:, b, :]
                h, l = src.hi[:, k0 + kt, :], src.lo[:, k0 + kt, :]
                if kt == 0:
                    pe.wait(*held[i][1])
                pe.wait(u.ready[t], src.ev[k0 + kt])
                matmul(o, wh, h, kt == 0, False)
                matmul(o, wh, l, False, False)
                src.used[k0 + kt] = m = matmul(o, wl, h, False, kt == len(rows) - 1)
                if k == u.nk - 1 and (i == n - 1 or wtile(u, i + 1)[0] != t):
                    wslot[s].give(m)
                if kt == len(rows) - 1:
                    start(evac(i, held[i][0], m), m)

        def vunit(us, ring, evac, per=2):
            us = us if isinstance(us, list) else [us]
            rows = [(u, k) for u in us for k in range(u.nk)]
            for t in range(4):
                q = t % per
                if q == 0:
                    b, got = yield from take_one(ring)
                for kt, (u, k) in enumerate(rows):
                    while None in u.ready:
                        yield lambda: None not in u.ready
                    yield u.ready
                    yield pe
                    s, w = u.slots[0], slice(k * u.half, (k + 1) * u.half)
                    wh, wl = WH[:, s:s + 2, w], WL[:, s:s + 2, w]
                    h, l = HH[:, kt, 128 * t:128 * t + 128], HL[:, kt, 128 * t:128 * t + 128]
                    if q == 0 and kt == 0:
                        pe.wait(*got)
                    pe.wait(H.ev[kt], *u.ready)
                    o = P[:, b.i, q * u.width:(q + 1) * u.width]
                    matmul(o, h, wh, kt == 0, False)
                    matmul(o, h, wl, False, False)
                    H.used[kt] = m = matmul(o, l, wh, False, kt == KT - 1)
                    if t == 3 and k == u.nk - 1:
                        wslot[s].give(m)
                        wslot[s + 1].give(m)
                if q == per - 1:
                    start(evac(t // per, b, m), m)

        class Norm:

            def __init__(self):
                self.n, self.done, self.rt, self.rb, self.ring = 0, 0, None, None, []

        norms = []
        rt_read, rb_read = {}, {}
        SQA = at("SQA", [128, T], F32, o_a)
        SQ = [at("SQ0", [128, T], F32, o_a + 2048), at("SQ1", [128, T], F32, o_a + 4096)]
        DIAG = at("DIAG", [128, T], F32, o_a + 4096)
        sqa, sq = Hold(), [Hold(), Hold()]

        def has_rt(norm):
            while norm.rt is None:
                yield lambda: norm.rt is not None
            yield norm.rt

        def has_rb(norm):
            while norm.rb is None:
                yield lambda: norm.rb is not None
            yield norm.rb

        def new_norm():
            norms.append(Norm())
            H.ev = {}

        def prep_tile(kt, ev, g0):
            x = XT[:, kt, :]
            norm = norms[-1]
            g = GT[:, g0 + kt:g0 + kt + 1]
            act.wait(ev, H.used.get(kt))
            hi = activ(HH[:, kt, :], x, AF.Identity, scale=g)
            yield hi
            dve.wait(ev, hi)
            H.ev[kt] = stt(dve, HL[:, kt, :], x, g, HH[:, kt, :], ALU.mult, ALU.subtract)
            norm.n += 1
            if norm.n == 1:
                got = yield from take(sqa)
                yield act
                act.wait(ev, *got)
                s = activ(SQA[:], x, AF.Square)
                sqa.give(s)
                last = [s]
            else:
                i = norm.n % 2
                got = yield from take(sq[i])
                yield act
                act.wait(ev, *got)
                s = activ(SQ[i][:], x, AF.Square)
                last = [s]
                yield s
                got = yield from take(sqa)
                lane = dve if norm.done == KT - 1 else pool
                lane.wait(s, *got)
                a = tt(lane, SQA[:], SQA[:], SQ[i][:], ALU.add)
                sqa.give(a)
                sq[i].give(a)
            norm.done += 1
            if norm.done == KT:
                start(norm_sums(norm), *sqa.free)
            return last

        def norm_sums(norm):
            got = yield from take(sqa)
            m, a = yield from row_sums(MS, SQA, got, bank[6:8])
            sqa.give(m)
            dve.wait(a)
            m = ts(dve, MS, MS, 1.0 / D, ALU.mult, EPS, ALU.add)
            yield m
            act.wait(m, *rt_read.values())
            s = activ(STD, MS, AF.Sqrt)
            yield s
            dve.wait(s)
            dve.wait(*rt_read.values())
            rt = rsqrt_step(RT, STD, MS, NW, m)
            norm.rt = rt
            dve.wait(rt, got_in["idn"])
            d = along_rows(dve, DIAG, RT)
            yield d
            b, bgot = yield from take_one(bank[6:8])
            pe.wait(d, *bgot)
            m = spread(b, DIAG)
            yield m
            act.wait(m, *rb_read.values())
            norm.rb = copy(act, RB[:], P[:, b.i, :])
            b.give(norm.rb)
            norm.ring.append(bank[7])

        def row_sums(o, x, ready, banks):
            b, got = yield from take_one(banks)
            pe.wait(*ready, *got, got_in["idn"])
            m = spread(b, x)
            yield m
            dve.wait(m)
            i = P[:, b.i, :].rearrange("p (t d) -> p t d", t=4)
            if len(o.shape) == 3:
                i = i.rearrange("p t (g d) -> p t g d", g=o.shape[2])
            a = dve(lambda e: e.tensor_reduce(o, i, AX.X, ALU.add), vcost(dve, T))
            b.give(a)
            return m, a

        def along_rows(lane, tmp, r):
            n = 128 // (r.shape[2] if len(r.shape) == 3 else 1)
            o = tmp[:].rearrange("p (t n) -> p t n", t=4)
            if n < 128:
                o = o.rearrange("p t (g n) -> p t g n", n=n)
            return copy(lane, o, r.unsqueeze(len(r.shape)).to_broadcast(list(o.shape)))

        def spread(b, tmp):
            for t in range(4):
                m = transpose(P[:, b.i, 128 * t:128 * t + 128], tmp[:, 128 * t:128 * t + 128], IDN)
            return m

        def rsqrt_step(y, std, ms, w, ms_ev):
            a = recip(y, std)
            dve.wait(a, ms_ev)
            a = tt(dve, w, y, y, ALU.mult)
            dve.wait(a)
            a = tt(dve, w, w, ms, ALU.mult)
            dve.wait(a)
            a = ts(dve, w, w, -0.5, ALU.mult, 1.5, ALU.add)
            dve.wait(a)
            return tt(dve, y, y, w, ALU.mult)

        cslot, gslot, mslot = (Slot(semaphore(n)) for n in ("s_const", "s_vec", "s_mask"))
        xslots = [Slot(semaphore(f"s_x{i}")) for i in range(5)]
        xt_ev = [None] * KT
        MIN = at("MIN", [128, 2, 128], F32, o_a + 38 * KB)
        HM = at("HM", [128, 6, 128], F32, CS_off)
        CW1 = [at(f"CW1{i}", [128, 16, 128], F32, o_a + (22 + 8 * i) * KB) for i in range(2)]
        CWS = [at(f"CWS{i}", [128, 2, 64], F32, o_a + 68 * KB + 512 * i) for i in range(2)]
        LAMV = at("LAMV", [128, 4, 2, 64], F32, o_a + 40 * KB)
        got_in = {}

        def load_x(*parts):
            for i in parts:
                k0, k1 = ((0, 1), (1, 2), (2, 4), (4, 6), (6, 8))[i]
                step = dma(sp, xslots[i], XT[:, k0:k1, :], A["p_xt"][128 * k0:128 * k1, :].rearrange("(k p) t -> p k t", p=128))
                xt_ev[k0:k1] = [step] * (k1 - k0)

        def load_masks():
            got_in["idn"] = dma(sp, cslot, BM[:], A["c_idn"])
            got_in["mask"] = dma(sp, mslot, MIN[:], A["c_mask"])
            got_in["hm"] = dma(sp, Slot(semaphore("s_hm")), HM[:], A["c_hg"])

        wc_slot = [Slot(semaphore(f"s_cw{i}")) for i in range(2)]

        def load_cmp(i):
            src = A[("cmp_k_w1", "cmp_v_w1")[i]][0].rearrange("(a r d) n -> a d r n", a=2, r=16)
            for a in range(2):
                dma(sp, wc_slot[i], CW1[i][64 * a:64 * a + 64, :, :], src[a])
            for a in range(2):
                got_in[("cw", i)] = dma(sp, wc_slot[i], CWS[i][:, a, :], A[("cmp_k_w2", "cmp_v_w2")[i]][0])

        def load_lambdas():
            got_in["lam"] = dma(sp, Slot(semaphore("s_lam")), LAMV[:].rearrange("p a l d -> p (a l d)"),
                                A["p_lam"].partition_broadcast(128))

        small_loads.update({0: lambda: load_x(0, 1, 2), 1: lambda: load_x(3, 4), 2: load_masks, 4: lambda: load_cmp(0),
                            5: lambda: load_cmp(1), 6: load_lambdas})

        def opening():
            gt = got_in["gt"]
            none = zero(dve, MT[:])
            ones = pool(lambda e: e.memset(ONES[:], 1.0), 0.1)
            eps = pool(lambda e: e.memset(EPSC, EPS), 0.1)
            act.wait(eps)
            act.clock += 1.3
            activ(STD[:, 0:1], EPSC, AF.Square)
            act.wait(gt)
            dve.wait(gt)
            pool.wait(gt)
            pe.wait(none)
            for _ in range(14):
                m = matmul(P[:, 7, :], MT[:, 0, 0:128], MT[:, 0, :], True, True)
            bank[7].give(m)
            warm.append(m)
            pe.wait(ones)
            for kt in range(KT):
                while xt_ev[kt] is None:
                    yield lambda: xt_ev[kt] is not None
                yield xt_ev[kt]
                yield from prep_tile(kt, xt_ev[kt], 0)

        warm = []

        def small_things():
            while "mask" not in got_in:
                yield lambda: "mask" in got_in
            yield got_in["mask"]
            dve.wait(got_in["mask"], *warm)
            got_in["maskb"] = copy(dve, MT[:, :, 384:512], MIN[:])
            d = tt(dve, SM[:, 40:44], GT[:, 55:59], GT[:, 59:63], ALU.subtract)
            act.wait(d)
            l = activ(LB, SM[:, 40:44], AF.Sigmoid)
            dve.wait(l)
            ts(dve, LB1, LB, -1.0, ALU.mult, 1.0, ALU.add)
            q = ts(dve, QFOLD, GT[:, 49:52], GT[:, 48:49], ALU.mult)
            dve.wait(q)
            got_in["small"] = q

        def lambdas():
            while "lam" not in got_in:
                yield lambda: "lam" in got_in
            yield got_in["lam"]
            dve.wait(got_in["lam"])
            a = tt(dve, LAMV[:, 0], LAMV[:, 0], LAMV[:, 1], ALU.mult)
            b = tt(dve, LAMV[:, 2], LAMV[:, 2], LAMV[:, 3], ALU.mult)
            dve.wait(a, b)
            dve(lambda e: e.tensor_reduce(SM[:, 48:50], LAMV[:, 0], AX.X, ALU.add), 0.2)
            c = dve(lambda e: e.tensor_reduce(SM[:, 50:52], LAMV[:, 2], AX.X, ALU.add), 0.2)
            yield c
            act.wait(c)
            x = activ(SM[:, 52:56], SM[:, 48:52], AF.Exp)
            yield x
            dve.wait(x)
            a = tt(dve, LAM, SM[:, 52:54], SM[:, 54:56], ALU.subtract)
            dve.wait(a)
            for l in range(2):
                got_in["lambda"] = ts(dve, LAM[:, l:l + 1], LAM[:, l:l + 1], 0.8 - 0.6 * float(np.exp(-0.3 * l)), ALU.add)

        def add_x(o, b, m, then=None):
            dve.wait(m, xt_ev[o])
            xt_ev[o] = tt(dve, XT[:, o, :], P[:, b.i, :], XT[:, o, :], ALU.add)
            b.give(xt_ev[o])
            if then is not None:
                yield xt_ev[o]
                yield from prep_tile(o, xt_ev[o], then)

        def ffn(name, units, chunks, gated, g_next):
            TG = [at(f"TG{name}_{i}", [128, T], F32, o_a + 6144 + 2048 * i) for i in range(4)]
            TS = [at(f"TS{name}_{i}", [128, T], F32, o_a + 14336 + 2048 * i) for i in range(4)]
            TU = [at(f"TU{name}_{i}", [128, T], F32, o_a + 22528 + 2048 * i) for i in range(4)]
            tg, tsi, tu = ([Hold() for _ in range(4)] for _ in range(3))
            todo = list(units)
            norm = norms[-1]
            ring = norm.ring
            ring.extend(bank[0:7])
            gates = {}

            def hidden(j, n, u):
                yield u
                act.wait(u, U.used.get(j))
                h = copy(act, UH[:, j, :], TU[n][:])
                yield h
                dve.wait(u, h, U.used.get(j))
                U.ev[j] = diff(dve, UL[:, j, :], TU[n][:], UH[:, j, :])
                tu[n].give(U.ev[j])

            def ev_gate(j0):
                def evac(i, b, m):
                    j = j0 + i
                    n = j % 4
                    yield from has_rb(norm)
                    got = yield from take(tg[n])
                    dve.wait(m, norm.rb, *got)
                    g = tt(dve, TG[n][:], P[:, b.i, :], RB[:], ALU.mult)
                    rb_read["dve"] = g
                    b.give(g)
                    yield g
                    got = yield from take(tsi[n])
                    act.wait(g, *got)
                    s = activ(TS[n][:], TG[n][:], AF.Silu)
                    tg[n].give(s)
                    yield s
                    pool.wait(s, norm.rb)
                    gates[j] = tt(pool, TS[n][:], TS[n][:], RB[:], ALU.mult)
                    rb_read["pool"] = gates[j]
                return evac

            def ev_up(j0):
                def evac(i, b, m):
                    j = j0 + i
                    n = j % 4
                    while j not in gates:
                        yield lambda: j in gates
                    yield gates[j]
                    got = yield from take(tu[n])
                    dve.wait(m, gates[j], *got)
                    u = tt(dve, TU[n][:], P[:, b.i, :], TS[n][:], ALU.mult)
                    del gates[j]
                    b.give(u)
                    tsi[n].give(u)
                    yield from hidden(j, n, u)
                return evac

            def ev_relu2(j0):
                def evac(i, b, m):
                    j = j0 + i
                    n = j % 4
                    yield from has_rb(norm)
                    got = yield from take(tg[n])
                    dve.wait(m, norm.rb, *got)
                    a = tt(dve, TG[n][:], P[:, b.i, :], RB[:], ALU.mult)
                    rb_read["dve"] = a
                    b.give(a)
                    got = yield from take(tu[n])
                    dve.wait(a, *got)
                    u = stt(dve, TU[n][:], TG[n][:], 0.0, TG[n][:], ALU.max, ALU.mult)
                    tg[n].give(u)
                    yield from hidden(j, n, u)
                return evac

            for ci, n in enumerate(chunks):
                U.ev = {}
                for j in range(0, n, 2):
                    first = ci == 0 and j == 0
                    if gated:
                        yield from unit(todo.pop(0), H, ring, ev_gate(j), kouter=first)
                        yield from unit(todo.pop(0), H, ring, ev_up(j), kouter=first)
                    else:
                        yield from unit(todo.pop(0), H, ring, ev_relu2(j), kouter=first)
                final = ci == len(chunks) - 1
                if final:
                    new_norm()
                for o in range(0, KT, 2):
                    def evac(i, b, m, o=o):
                        return add_x(o + i, b, m, g_next if final else None)
                    yield from unit(todo.pop(0), U, ring, evac, kouter=o == 0)

        def ffn_last(units):
            TG = [at(f"TGz_{i}", [128, T], F32, o_a + 6144 + 2048 * i) for i in range(4)]
            TU = [at(f"TUz_{i}", [128, T], F32, o_a + 22528 + 2048 * i) for i in range(4)]
            tg, tu = ([Hold() for _ in range(4)] for _ in range(2))
            XK = at("XK", [128, 4, D], F32, o_a + 31 * KB)
            FG = at("FG", [128, D], F32, o_a + 47 * KB)
            OUT = at("OUT", [128, 4, D], F32, o_a + 51 * KB)
            SQK = at("SQK", [128, 256], F32, o_a + 67 * KB)
            SS = SM[:, 44:60].rearrange("p (t o) -> p t o", t=4)
            todo = list(units)
            norm = norms[-1]
            ring = norm.ring
            ring.extend(bank[0:7])
            fslot = Slot(semaphore("s_fg"))
            oslots = [Slot(semaphore(f"s_out{t}")) for t in range(4)]
            xk_ev = [[None] * 4 for _ in range(4)]
            fg = []
            sqk = Hold()

            def ev_relu2(j0):
                def evac(i, b, m):
                    j = j0 + i
                    n = j % 4
                    yield from has_rb(norm)
                    got = yield from take(tg[n])
                    dve.wait(m, norm.rb, *got)
                    a = tt(dve, TG[n][:], P[:, b.i, :], RB[:], ALU.mult)
                    b.give(a)
                    got = yield from take(tu[n])
                    dve.wait(a, *got)
                    u = stt(dve, TU[n][:], TG[n][:], 0.0, TG[n][:], ALU.max, ALU.mult)
                    tg[n].give(u)
                    yield u
                    act.wait(u, U.used.get(j))
                    h = copy(act, UH[:, j, :], TU[n][:])
                    yield h
                    dve.wait(u, h, U.used.get(j))
                    U.ev[j] = diff(dve, UL[:, j, :], TU[n][:], UH[:, j, :])
                    tu[n].give(U.ev[j])
                return evac

            def turn_x():
                for t in range(4):
                    for half in range(2):
                        b, got = yield from take_one(ring)
                        yield pe
                        pe.wait(*got)
                        for k in range(4):
                            kt = 4 * half + k
                            pe.wait(xt_ev[kt])
                            m = transpose(P[:, b.i, 128 * k:128 * k + 128], XT[:, kt, 128 * t:128 * t + 128], IDN)
                        yield m
                        act.wait(m)
                        c = copy(act, XK[:, t, 512 * half:512 * half + 512], P[:, b.i, :])
                        b.give(c)
                        for o in (2 * half, 2 * half + 1):
                            xk_ev[t][o] = c

            def down(u, o, final):
                held = [None] * 4
                order = [(t, kt) for t in range(4) for kt in range(u.nk)]
                if o == 0:
                    order = [(t, kt) for p in (0, 2) for kt in range(u.nk) for t in (p, p + 1)]
                for t, kt in order:
                    if held[t] is None:
                        held[t] = yield from take_one(ring)
                    while None in u.ready or kt not in U.ev:
                        yield lambda: None not in u.ready and kt in U.ev
                    yield u.ready + [U.ev[kt]]
                    yield pe
                    s, b = u.slots[0], held[t][0]
                    w = slice(128 * kt, 128 * kt + 128)
                    wh, wl = WH[:, s:s + 2, w], WL[:, s:s + 2, w]
                    tok = slice(128 * t, 128 * t + 128)
                    h, l = UH[:, kt, tok], UL[:, kt, tok]
                    p = P[:, b.i, 0:256]
                    if kt == 0:
                        pe.wait(*held[t][1])
                    pe.wait(U.ev[kt], *u.ready)
                    matmul(p, h, wh, kt == 0, False)
                    matmul(p, h, wl, False, False)
                    U.used[kt] = m = matmul(p, l, wh, False, kt == u.nk - 1)
                    if kt == u.nk - 1:
                        if t == 3:
                            wslot[s].give(m)
                            wslot[s + 1].give(m)
                        start(ev_down(t, o, b, m, final), m)

            def ev_down(t, o, b, m, final):
                x = XK[:, t, 256 * o:256 * o + 256]
                while xk_ev[t][o] is None:
                    yield lambda: xk_ev[t][o] is not None
                yield xk_ev[t][o]
                dve.wait(m, xk_ev[t][o])
                a = xk_ev[t][o] = tt(dve, x, P[:, b.i, 0:256], x, ALU.add)
                b.give(a)
                if not final:
                    return
                yield a
                got = yield from take(sqk)
                act.wait(a, *got)
                s = activ(SQK[:], x, AF.Square, accum=SS[:, t, o:o + 1])
                sqk.give(s)
                squares[t].append(s)
                if o < 3:
                    pool.wait(a, *fg)
                    gained[t].append(tt(pool, OUT[:, t, 256 * o:256 * o + 256], x, FG[:, 256 * o:256 * o + 256], ALU.mult))
                if len(squares[t]) < 4:
                    return
                yield squares[t]
                r = STD[:, t:t + 1]
                dve.wait(*squares[t])
                a = dve(lambda e: e.tensor_reduce(r, SS[:, t, :], AX.X, ALU.add), 0.07)
                yield a
                act.wait(a)
                a = activ(r, r, AF.Sqrt, scale=1.0 / D, bias=EPSC)
                yield a
                dve.wait(a)
                a = recip(RT[:, t:t + 1], r)
                dve.wait(a, *fg, *gained[t])
                c = slice(0, 768)
                y = ts(dve, OUT[:, t, c], OUT[:, t, c], RT[:, t:t + 1], ALU.mult)
                sp.wait(y)
                dma(sp, oslots[t], out[0, 128 * t:128 * t + 128, c], OUT[:, t, c])
                c = slice(768, 1024)
                y = stt(dve, OUT[:, t, c], XK[:, t, c], RT[:, t:t + 1], FG[:, c], ALU.mult, ALU.mult)
                sp.wait(y)
                stored.append(dma(sp, oslots[t], out[0, 128 * t:128 * t + 128, c], OUT[:, t, c]))

            stored, squares, gained = [], [[], [], [], []], [[], [], [], []]
            for ci in range(4):
                U.ev = {}
                for j in range(0, 8, 2):
                    yield from unit(todo.pop(0), H, ring, ev_relu2(j), kouter=ci == 0 and j == 0)
                    if ci == 0 and j == 2:
                        sp.wait(*xt_ev)
                        fg.append(dma(sp, fslot, FG[:], A["final_norm_2"].rearrange("(o d) -> o d", o=1).partition_broadcast(128)[:, 0]))
                        start(turn_x())
                for o in range(4):
                    yield from down(todo.pop(0), o, ci == 3)
            while len(stored) < 4:
                yield lambda: len(stored) == 4
            sp.wait(*stored)

        W1 = A["w_in"][0]
        C_Q, C_KC, _, C_KS, C_VS, C_KW, C_VW, _, C_HQ, C_HF, C_HI, C_HG = (
            0, 512, 640, 768, 896, 1024, 1152, 1280, 1304, 1816, 2328, 2840)

        def wcols(c, n=128):
            return W1[:, c:c + n]

        ORDER1 = "hqf0 hi0 hqf1 hg0 cmp hqf2 hi1 hqf3 vsw hg1 ksw q0 q1".split()

        def plan_mixer1():
            got = {}
            src = {"cmp": [wcols(C_KC, 256)], "ksw": [wcols(C_KS), wcols(C_KW)], "vsw": [wcols(C_VS), wcols(C_VW, 152)]}
            for i in range(4):
                src[f"hqf{i}"] = [wcols(C_HQ + 128 * i), wcols(C_HF + 128 * i)]
            for i in range(2):
                src[f"hi{i}"] = [wcols(C_HI + 256 * i, 256)]
                src[f"hg{i}"] = [wcols(C_HG + 256 * i, 256)]
                src[f"q{i}"] = [wcols(C_Q + 256 * i, 256)]
            for name in ORDER1:
                if name in ("hqf0", "hi0", "vsw"):
                    got[name] = [plan([w[r:r + 512, :] for w in src[name]], 4) for r in (0, 512)]
                else:
                    got[name] = plan(src[name], KT)
            for name, r, c in (("wh0", 512, 0), ("wh1", 512, 512)):
                got[name] = plan([A["w_out"][0][r:r + 512, c:c + 512]], 4)
            for i in range(2):
                got[f"wn{i}"] = plan([A["w_out"][0][0:256, 512 * i:512 * i + 512]], 2)
            for i in range(2, 4):
                got[f"wn{i}"] = plan([A["w_out"][0][128 * i:128 * i + 128, :]], 1)
            return got

        class Ring:

            def __init__(self, bufs):
                self.all = [Hold() for _ in bufs]
                for i, (h, b) in enumerate(zip(self.all, bufs)):
                    h.i, h.buf = i, b
                self.n = 0

            def next(self):
                self.n += 1
                h = self.all[(self.n - 1) % len(self.all)]
                got = yield from take(h)
                return h, got

            def pair(self):
                self.n += 2
                a, b = (self.all[(self.n - k) % len(self.all)] for k in (2, 1))
                got = yield from take(a, b)
                return a, b, got

        SPOT = {3: (2, 0, 512), 2: (3, 0, 384), 0: (3, 384, 128), 1: (4, 0, 256)}
        CHUNKS = (((2,), (3,)), ((3, 4), (2, 0, 1)))

        def spot(t):
            b, c, n = SPOT[t]
            return P[:, b, c:c + n]

        def scol(t):
            c = {3: 0, 2: 512, 0: 896, 1: 1024}[t]
            return c, c + 128 * (t + 1)

        def trow(j):
            c = {0: 0, 1: 512, 3: 896, 2: 1024}[j]
            return c, c + 512 - 128 * j

        class Order:

            def __init__(self):
                self.n = 0

            def turn(self, n):
                while self.n != n:
                    yield lambda: self.n == n

            def done(self):
                self.n += 1

        def row_softmax(bs, ts_, st, mask, scale, pf, m, got, free):
            yield m
            dve.wait(m, got_in["maskb"], *got, *free)
            for t in ts_:
                c = scol(t)
                a = mask_min(pf[:, c[0]:c[1]], spot(t), MT[:, mask, 384 - 128 * t:512],
                             scale if isinstance(scale, float) else scale[:, t:t + 1], st[:, t:t + 1])
            for b in bs:
                bank[b].give(a)
            yield a
            act.wait(a, *free)
            for t in ts_:
                p = pf[:, slice(*scol(t))]
                x = activ(p, p, AF.Exp, scale=-1.0, bias=st[:, t:t + 1], accum=st[:, 8 + t:9 + t])
            yield x
            r = slice(min(ts_), max(ts_) + 1)
            dve.wait(x)
            a = recip(st[:, 8:12][:, r], st[:, 8:12][:, r])
            return r, x, a

        def turn(pf, ready, pt, got, order):
            evs = []
            ph, pl = pt.buf

            def halves(b, c0, w, m):
                yield m
                act.wait(m, *got)
                hi = copy(act, ph[:, c0:c0 + w], P[:, b.i, 0:w])
                yield hi
                dve.wait(hi, *got)
                lo = diff(dve, pl[:, c0:c0 + w], P[:, b.i, 0:w], ph[:, c0:c0 + w])
                b.give(lo)
                evs.append(lo)

            for js in ((0,), (1, 3), (2,)):
                b, free = yield from take_one(bank[5:7])
                pe.wait(*ready, *free)
                c0, w = trow(js[0])[0], 0
                for j in js:
                    for t in range(j, 4):
                        c = scol(t)[0] + 128 * j
                        m = transpose(P[:, b.i, w:w + 128], pf.buf[:, c:c + 128], IDN)
                        w += 128
                start(halves(b, c0, w, m), m)
            pf.give(m)
            order.done()
            while len(evs) < 3:
                yield lambda: len(evs) == 3
            yield Late(evs)
            return evs

        def mix_halves(kt, src, ev):
            act.wait(ev)
            hi = copy(act, UH[:, kt, :], src)
            yield hi
            dve.wait(ev, hi)
            U.ev[kt] = diff(dve, UL[:, kt, :], src, UH[:, kt, :])

        def values(v, ph, pl, ready, first, stop):
            pe.wait(*ready)
            for j in range(4):
                c = trow(j)
                o = P[:, 7, 128 * j:512]
                matmul(o, v(j), ph[:, c[0]:c[1]], first and j == 0, False)
                m = matmul(o, v(j), pl[:, c[0]:c[1]], False, stop and j == 3)
            return m

        def fold(h, m, tmp, both, mix_free=None):
            if h % 2 == 0:
                both.got = yield from take(both)
            got = yield from take(tmp)
            act.wait(m, *got)
            c = copy(act, tmp.buf[0:64, :], P[64:128, 7, :])
            yield c
            dve.wait(c, *both.got)
            own = slice(64 * (h % 2), 64 * (h % 2) + 64)
            a = tt(dve, both.buf[own, :], P[0:64, 7, :], tmp.buf[0:64, :], ALU.add)
            bank[7].give(a)
            tmp.give(a)
            if h % 2:
                if mix_free is not None:
                    got = yield from mix_free(h // 2)
                    act.wait(*got)
                    dve.wait(*got)
                yield a
                yield from mix_halves(h // 2, both.buf[:], a)
                both.give(U.ev[h // 2])

        def out_tiles(u, k0, o0, ring, then):
            def evac(i, b, m):
                return add_x(o0 + i, b, m, then)
            return unit(u, U, ring, evac, k0=k0)

        def mixer1(m1):
            QS = [at(f"QS{h}", [128, T], F32R, o_a + (6 + 2 * h) * KB) for h in range(8)]
            HS = []
            for i in range(2):
                o = o_a + (6 + 8 * i) * KB
                HS.append((at(f"HQ{i}", [128, T], F32, o), at(f"HK{i}", [128, T], F32, o + 2 * KB),
                           at(f"HT{i}", [128, 1024], F32, o + 4 * KB)))
            KS = [[[at(f"KS{b}{g}{x}", [128, T], F32R, o_a + (22 + 8 * b + 4 * g + 2 * x) * KB) for x in range(2)]
                   for g in range(2)] for b in range(2)]
            VN = at("VN", [128, 4, 4, 128], F32R, o_a + 38 * KB)
            o = o_a + 46 * KB
            VCS = at("VCS", [128, 2, 128], F32R, o + 512)
            GATE = at("GATE", [128, 4, 24], F32, o + 1536)
            QSC = at("QSC", [128, 4, 8], F32, o + 1920)
            NQS = at("NQS", [128, 4, 8], F32, o)
            KW = at("KW", [128, 2, 4, 8], F32, o + 128)
            HN = at("HN", [128, 2, 4, 4], F32, o + 384)
            QW = at("QW", [128, 2, 4, 16], F32, o_a + 512)
            HV = [at(f"HV{i}", [128, 4, 256], F32, o_a + (48 + 4 * i) * KB) for i in range(2)]
            EV = Ring([at(f"EV{i}", [128, T], F32, o_a + (56 + 2 * i) * KB) for i in range(4)])
            TM = Ring([at(f"TM{i}", [128, T], F32, o_a + (64 + 2 * i) * KB) for i in range(2)])
            ATD = [at(f"ATD{i}", [128, 4, 128], F32, o_u + 16384 * i) for i in range(2)]
            ATO = [at(f"ATO{i}", [128, 768], F32, o_u + 16384 * i + 2048) for i in range(2)]
            CG = [at(f"CG{i}", [128, 5, 64], F32, o_u + 16384 * i + 5120) for i in range(2)]
            GR = at("GR", [128, 2, 128], F32, o_u + 6400)
            G = [at(f"G{h}", [128, T], F32, o_u + 16384 + 2048 * (4 + h)) for h in range(4)]
            KCX = at("KCX", [128, 2, T], F32, o_a + 2 * KB)
            KNB = [(at("KN0", [128, T], F32, o_a + 48 * KB), at("KN1", [128, T], F32, o_a + 50 * KB)),
                   (at("KN2", [128, T], F32, o_a + 2 * KB), at("KN3", [128, T], F32, o_a + 4 * KB))]
            U.ev = {}
            norm = norms[-1]

            def scaled(o, b, ev, free):
                dve.wait(ev, norm.rb, *free)
                a = tt(dve, o, P[:, b.i, :], RB[:], ALU.mult)
                rb_read["dve"] = a
                b.give(a)
                return a

            head_set, hv = [Hold(), Hold()], [Hold(), Hold()]
            head_in, v_in, g_in, set_got = {}, {}, {}, {}
            hgrn_at = [Hold(), Hold()]

            def ev_hqf(h):
                hq, hk, ht = HS[h % 2]

                def evac(i, b, m):
                    yield from has_rb(norm)
                    xb, yb, got = yield from EV.pair()
                    x, y = xb.buf[:], yb.buf[:]
                    a = scaled(x, b, m, got)
                    yield a
                    act.wait(a, *got)
                    s = activ(y, x, AF.Sigmoid)
                    if h not in set_got:
                        set_got[h] = None
                        set_got[h] = yield from take(head_set[h % 2])
                    while set_got[h] is None:
                        yield lambda: set_got[h] is not None
                    yield s
                    if i == 0:
                        pool.wait(s, *set_got[h])
                        q = tt(pool, hq[:], x, y, ALU.mult)
                        xb.give(q)
                        yb.give(q)
                        head_in[(h, 0)] = q
                    else:
                        while "small" not in got_in:
                            yield lambda: "small" in got_in
                        dve.wait(s, got_in["small"], *set_got[h])
                        f = ts(dve, ht[:, 0:T], y, LB1[:, h:h + 1], ALU.mult, LB[:, h:h + 1], ALU.add)
                        dve.wait(f)
                        k = ts(dve, hk[:], ht[:, 0:T], -1.0, ALU.mult, 1.0, ALU.add)
                        xb.give(s)
                        yb.give(f)
                        head_in[(h, 1)] = k
                return evac

            def ev_hi(p):
                def evac(tp, b, m):
                    yield from has_rt(norm)
                    if tp == 0:
                        set_got[("v", p)] = yield from take(hv[p])
                    while ("v", p) not in set_got:
                        yield lambda: ("v", p) in set_got
                    act.wait(m, norm.rt, *set_got[("v", p)])
                    for q in range(2):
                        t = 2 * tp + q
                        c = activ(HV[p][:, t, :], P[:, b.i, 256 * q:256 * q + 256], AF.Identity, scale=RT[:, t:t + 1])
                    rt_read["act"] = c
                    b.give(c)
                    v_in[(p, tp)] = c
                return evac

            def ev_hg(p):
                def evac(i, b, m):
                    h = 2 * p + i
                    yield from has_rb(norm)
                    xb, yb, got = yield from EV.pair()
                    x, y = xb.buf[:], yb.buf[:]
                    a = scaled(x, b, m, got)
                    yield a
                    act.wait(a, *got)
                    s = activ(y, x, AF.Sigmoid)
                    yield s
                    pool.wait(s)
                    g_in[h] = tt(pool, G[h][:], x, y, ALU.mult)
                    xb.give(g_in[h])
                    yb.give(g_in[h])
                return evac

            heads_done, v_read = [], {}

            def hgrn(h):
                par, p = h % 2, h // 2
                hq, hk, ht = HS[par]
                atd, ato = ATD[par], ATO[par]
                ring = [bank[2 + par], bank[4 + par]]
                v = HV[p]
                while (h, 0) not in head_in or (h, 1) not in head_in or "hm" not in got_in:
                    yield lambda: (h, 0) in head_in and (h, 1) in head_in and "hm" in got_in
                q_ev, k_ev, t_ev = head_in[(h, 0)], head_in[(h, 1)], head_in[(h, 1)]
                got = yield from take(hgrn_at[par])
                pool.wait(*got)
                wrote = [zero(pool, atd[:])]
                yield q_ev, k_ev
                for n, lev in enumerate((0, 1, 2, 4, 8, 16, 32, 64)):
                    b, got = yield from take_one(ring)
                    pe.wait(q_ev, k_ev, *got)
                    w = 64 if lev else 128
                    rows = 128 - lev if lev >= 32 else 128
                    pb = P[0:rows, b.i, 0:4 * w].rearrange("p (j t) -> p j t", j=4)
                    for j in range(4):
                        qj, o = hq[:, 128 * j:128 * j + 128], pb[:, j, :]
                        if lev:
                            qj = qj.rearrange("p (n s l) -> p n s l", s=2, l=lev)[:, :, 1, :]
                            o = o.rearrange("p (n l) -> p n l", l=lev)
                        m = matmul(o, hk[:, 128 * j:128 * j + rows], qj, True, True)
                    yield m
                    if lev == 0:
                        dve.wait(m, q_ev)
                        q_ev = tt(dve, hq[:], hq[:], ht[:, 0:T], ALU.mult)
                    else:
                        q_ev, k_ev, t_ev = double(hq, hk, ht, lev, m, q_ev, k_ev, t_ev)
                    if lev <= 16:
                        mk, to, src = HM[:, n, :].bitcast(U32), atd[:], pb
                        if lev:
                            mk = mk.rearrange("p (n s l) -> p n s l", s=2, l=lev)[:, :, 1, :]
                            mk = mk.unsqueeze(1).to_broadcast([128, 4, 64 // lev, lev])
                            to = to.rearrange("p j (n s l) -> p j n s l", s=2, l=lev)[:, :, :, 1, :]
                            src = src.rearrange("p j (n l) -> p j n l", l=lev)
                        else:
                            mk = mk.unsqueeze(1).to_broadcast([128, 4, 128])
                        dve.wait(m, got_in["hm"], *wrote)
                        c = dve(lambda e, mk=mk, to=to, src=src: e.copy_predicated(to, mk, src), vcost(dve, 4 * w))
                        hm_last[0] = c
                    else:
                        act.wait(m, *wrote)
                        for r in range(0, 128, 2 * lev):
                            c = copy(act, atd[r:r + lev, :, r + lev:r + 2 * lev], pb[r:r + lev, :, r // 2:r // 2 + lev])
                    wrote = [c]
                    b.give(c)
                    yield q_ev, k_ev
                b, got = yield from take_one(ring)
                pe.wait(q_ev, k_ev, *got)
                matmul(P[:, b.i, 0:128], hk[:, 0:128], hq[:, 128:256], True, True)
                m = matmul(P[:, b.i, 128:256], hk[:, 256:384], hq[:, 384:512], True, True)
                yield m
                q_ev, k_ev, t_ev = double(hq, hk, ht, 128, m, q_ev, k_ev, t_ev)
                act.wait(m)
                copy(act, ato[:, 0:128], P[:, b.i, 0:128])
                c = copy(act, ato[:, 640:768], P[:, b.i, 128:256])
                b.give(c)
                wrote.append(c)
                yield q_ev, k_ev
                b, got = yield from take_one(ring)
                pe.wait(q_ev, k_ev, *got)
                matmul(P[:, b.i, 0:256], hk[:, 0:128], hq[:, 256:512], True, True)
                m = matmul(P[:, b.i, 256:512], hk[:, 128:256], hq[:, 256:512], True, True)
                head_set[par].give(m)
                yield m
                act.wait(m)
                c = copy(act, ato[:, 128:640], P[:, b.i, :])
                b.give(c)
                wrote.append(c)
                while (p, 0) not in v_in or (p, 1) not in v_in:
                    yield lambda: (p, 0) in v_in and (p, 1) in v_in
                yield c
                ob, got = yield from take_one(ring)
                pe.wait(v_in[(p, 0)], v_in[(p, 1)], *wrote, *got)
                for t in range(4):
                    for j in range(t + 1):
                        w = atd[:, t, :]
                        if j < t:
                            c = (0, 384, 640)[j] + 128 * (t - j - 1)
                            w = ato[:, c:c + 128]
                        m = matmul(P[:, ob.i, 128 * t:128 * t + 128], w, v[:, j, 128 * par:128 * par + 128], t == 0, j == t == 3)
                hgrn_at[par].give(m)
                heads_done.append(m)
                v_read.setdefault(p, []).append(m)
                if len(v_read[p]) == 2:
                    hv[p].give(*v_read[p])
                yield m
                tb, got = yield from TM.next()
                tm = tb.buf
                ms, std, r, tmp = (HN[:, par, k, :] for k in range(4))
                act.wait(m, *got)
                for t in range(4):
                    c = slice(128 * t, 128 * t + 128)
                    s = activ(tm[:, c], P[:, ob.i, c], AF.Square, accum=ms[:, t:t + 1])
                yield s
                dve.wait(s)
                ms_ev = ts(dve, ms, ms, 1.0 / 128, ALU.mult, EPS, ALU.add)
                yield ms_ev
                act.wait(ms_ev)
                s = activ(std, ms, AF.Sqrt)
                yield s
                dve.wait(s)
                r_ev = rsqrt_step(r, std, ms, tmp, ms_ev)
                yield r_ev
                act.wait(r_ev)
                for t in range(4):
                    c = slice(128 * t, 128 * t + 128)
                    y = activ(tm[:, c], P[:, ob.i, c], AF.Identity, scale=r[:, t:t + 1])
                ob.give(y)
                yield y
                b, got = yield from take_one(ring)
                pe.wait(y, *got)
                for t in range(4):
                    m = transpose(P[:, b.i, 128 * t:128 * t + 128], tm[:, 128 * t:128 * t + 128], IDN)
                while h not in g_in:
                    yield lambda: h in g_in
                yield m, g_in[h]
                dve.wait(m, g_in[h])
                y = stt(dve, tm[:], P[:, b.i, :], GT[:, 52:53], G[h][:], ALU.mult, ALU.mult)
                b.give(y)
                yield y
                yield from mix_halves(4 + h, tm[:], y)
                tb.give(U.ev[4 + h])

            def double(hq, hk, ht, lev, m, q_ev, k_ev, t_ev):
                nb = T // (2 * lev)
                base = {1: 0, 2: 512, 4: 768, 8: 896, 16: 960, 32: 992, 64: 1008, 128: 1016}[lev]
                nxt = base + 2 * nb
                tv = ht[:, base:base + 2 * nb].rearrange("p (n s) -> p n s", s=2)
                qv = hq[:].rearrange("p (n s l) -> p n s l", s=2, l=lev)
                kv = hk[:].rearrange("p (n s l) -> p n s l", s=2, l=lev)
                pool.wait(m, k_ev, t_ev)
                k2 = tt(pool, kv[:, :, 0, :], kv[:, :, 0, :], tv[:, :, 1:2].to_broadcast([128, nb, lev]), ALU.mult)
                t2 = t_ev
                if lev < 128:
                    t2 = tt(pool, ht[:, nxt:nxt + nb], tv[:, :, 0], tv[:, :, 1], ALU.mult)
                dve.wait(m, q_ev, t_ev)
                q2 = tt(dve, qv[:, :, 1, :], qv[:, :, 1, :], tv[:, :, 0:1].to_broadcast([128, nb, lev]), ALU.mult)
                return q2, k2, t2

            cmp_src = {}
            kc_ev, kcx_done = [None, None], [None]

            def ev_cmp(i, b, m):
                yield from has_rb(norm)
                xb, xg = yield from EV.next()
                cmp_src[i] = (xb, scaled(xb.buf[:], b, m, xg))

            def compress():
                for i in range(2):
                    while i not in cmp_src or ("cw", i) not in got_in:
                        yield lambda: i in cmp_src and ("cw", i) in got_in
                    xb, ev = cmp_src[i]
                    yield ev
                    x = xb.buf
                    free = [norm.rb] if i == 0 else [m]
                    dve.wait(ev, *free)
                    for g in range(2):
                        r = slice(64 * g, 64 * g + 64)
                        pos = GT[r, 64 + 32 * i:96 + 32 * i]
                        xa = x[r, :].rearrange("p (n s) -> p n s", s=16)
                        ka = KCX[0:64, g, :].rearrange("p (n s) -> p n s", s=16)
                        kb = KCX[64:128, g, :].rearrange("p (n s) -> p n s", s=16)
                        tt(dve, ka, xa, pos[:, 0:16].unsqueeze(1).to_broadcast([64, 32, 16]), ALU.add)
                        c = tt(dve, kb[:, 0:31, :], xa[:, 1:32, :],
                               pos[:, 16:32].unsqueeze(1).to_broadcast([64, 31, 16]), ALU.add)
                    xb.give(c)
                    yield c
                    b6, got = yield from take_one(bank[6:8])
                    kv = KCX[:].rearrange("p g (n s) -> p g n s", s=16)
                    o = P[:, b6.i, 0:64].rearrange("p (g n) -> p g n", g=2)[:, :, 0:31]
                    for r in range(16):
                        if r == 0:
                            pe.wait(c, got_in[("cw", i)], *got)
                        m = matmul(o, CW1[i][:, r, :], kv[:, :, 0:31, r], r == 0, r == 15)
                        if r % 4 == 3:
                            yield pe
                    kcx_done[0] = m
                    hs, u, w, th, gl = (CG[i][:, k, :].rearrange("p (g n) -> p g n", g=2) for k in range(5))
                    z = zero(pool, gl)
                    v = slice(0, 31)
                    yield m
                    dve.wait(m)
                    a = copy(dve, hs[:, :, v], o)
                    b6.give(a)
                    dve.wait(a)
                    a = tt(dve, u[:, :, v], hs[:, :, v], hs[:, :, v], ALU.mult)
                    dve.wait(a)
                    a = ts(dve, w[:, :, v], u[:, :, v], 0.044715, ALU.mult, 1.0, ALU.add)
                    dve.wait(a)
                    a = tt(dve, u[:, :, v], w[:, :, v], hs[:, :, v], ALU.mult)
                    yield a
                    act.wait(a)
                    a = activ(th[:, :, v], u[:, :, v], AF.Tanh, scale=float(np.sqrt(2 / np.pi)))
                    yield a
                    dve.wait(a)
                    a = ts(dve, w[:, :, v], th[:, :, v], 1.0, ALU.add, 0.5, ALU.mult)
                    dve.wait(a, z)
                    a = tt(dve, gl[:, :, v], w[:, :, v], hs[:, :, v], ALU.mult)
                    yield a
                    b6, got = yield from take_one(bank[6:8])
                    if i == 0:
                        pe.wait(a, *got)
                        m = matmul(P[:, b6.i, 0:64], CWS[0][:].rearrange("p a d -> p (a d)"), CG[0][:, 4, :], True, True)
                        yield m
                        act.wait(m)
                        s = activ(CG[0][:, 1, :], P[:, b6.i, 0:64], AF.Square)
                        yield s
                        b7, got = yield from take_one(bank[6:8])
                        pe.wait(got_in["idn"], s, *got)
                        m = matmul(P[:, b7.i, 0:64], BLK, CG[0][:, 1, :], True, True)
                        yield m
                        act.wait(m)
                        s = activ(CG[0][:, 2, :], P[:, b7.i, 0:64], AF.Sqrt, scale=1.0 / 64, bias=EPSC)
                        b7.give(s)
                        yield s
                        dve.wait(s)
                        r_ = recip(CG[0][:, 3, :], CG[0][:, 2, :])
                        dve.wait(r_)
                        y = stt(dve, CG[0][:, 0, :], P[:, b6.i, 0:64], QFOLD[:, 0:1], CG[0][:, 3, :], ALU.mult, ALU.mult)
                        b6.give(y)
                        yield y
                        kc_ev[0] = y
                    else:
                        dve.wait(a)
                        a = copy(dve, GR[:].rearrange("p g (r n) -> p g r n", r=4),
                                 gl.unsqueeze(2).to_broadcast([128, 2, 4, 32]))
                        yield a
                        pe.wait(a, *got)
                        for g in range(2):
                            m = matmul(P[:, b6.i, 64 * g:64 * g + 64], GR[:, g, :], CWS[1][:, 0, :], True, True)
                        pv = P[:, b6.i, 0:128].rearrange("p (g d) -> p g d", g=2)
                        yield m
                        act.wait(m)
                        hi = copy(act, VCS[:, :, 0:64], pv)
                        yield hi
                        dve.wait(hi)
                        kc_ev[1] = diff(dve, VCS[:, :, 64:128], pv, VCS[:, :, 0:64])
                        b6.give(kc_ev[1])

            ks_ev = {}

            def ev_ksw(i, b, m):
                kn, sq_ = KNB[i]
                if i == 0:
                    got = yield from take(hv[0])
                else:
                    while kc_ev[1] is None:
                        yield lambda: kc_ev[1] is not None
                    got = [kcx_done[0]]
                a = scaled(kn[:], b, m, got)
                yield a
                act.wait(a, *got)
                s = activ(sq_[:], kn[:], AF.Square)
                yield s
                ms, std, r, tmp = (KW[:, i, k, :] for k in range(4))
                m, a = yield from row_sums(ms.rearrange("p (t g) -> p t g", t=4), sq_, [s], bank[6:8])
                dve.wait(a)
                ms_ev = ts(dve, ms, ms, 1.0 / 64, ALU.mult, EPS, ALU.add)
                yield ms_ev
                act.wait(ms_ev)
                s = activ(std, ms, AF.Sqrt)
                yield s
                dve.wait(s)
                r_ev = rsqrt_step(r, std, ms, tmp, ms_ev)
                yield r_ev
                act.wait(r_ev)
                d = along_rows(act, sq_, r.rearrange("p (t g) -> p t g", t=4))
                yield d
                b, got = yield from take_one(bank[6:8])
                pe.wait(d, *got)
                m = spread(b, sq_)
                yield m
                dve.wait(m)
                y = stt(dve, kn[:], kn[:], QFOLD[:, 1 + i:2 + i], P[:, b.i, :], ALU.mult, ALU.mult)
                b.give(y)
                while kc_ev[1] is None:
                    yield lambda: kc_ev[1] is not None
                yield y
                for g in range(2):
                    own = slice(64 * g, 64 * g + 64)
                    other = slice(64 - 64 * g, 128 - 64 * g)
                    hh, ll = KS[i][g]
                    act.wait(y)
                    c = copy(act, hh[own, :], kn[own, :])
                    c2 = copy(act, hh[other, :], kn[own, :])
                    yield c
                    dve.wait(y, c)
                    diff(dve, ll[own, :], kn[own, :], hh[own, :])
                    dve.wait(c2)
                    ks_ev[(i, g)] = [c2, diff(dve, ll[other, :], kn[own, :], hh[own, :])]

            vn_ev = [None] * 4

            gate_ev = [None]

            def ev_vsw(t, b, m):
                yield from has_rt(norm)
                src = P[:, b.i, 0:256].rearrange("p (n d) -> p n d", n=4)
                r = RT[:, t:t + 1]
                act.wait(m, norm.rt, got_in["maskb"])
                hi = activ(VN[:, t, :, 0:64], src, AF.Identity, scale=r)
                g = activ(GATE[:, t, :], P[:, b.i, 256:280], AF.Identity, scale=r)
                rt_read["act"] = g
                yield hi
                dve.wait(g, norm.rt)
                vn_ev[t] = stt(dve, VN[:, t, :, 64:128], src, r, VN[:, t, :, 0:64], ALU.mult, ALU.subtract)
                rt_read["dve"] = vn_ev[t]
                b.give(vn_ev[t])
                if t == 3:
                    act.wait(g)
                    gate_ev[0] = activ(GATE[:], GATE[:], AF.Sigmoid)

            q_ev, qsc_ev, q_sums = {}, [None, None], [[], []]
            q_bank = [None, None]

            def ev_q(u):
                def evac(i, b, m):
                    j = 2 * u + i
                    xb, xg = yield from EV.next()
                    x = xb.buf[:]
                    act.wait(m, *xg)
                    s = activ(x, P[:, b.i, :], AF.Square)
                    while len(heads_done) < 4:
                        yield lambda: len(heads_done) == 4
                    free = heads_done
                    yield [s] + free
                    act.wait(*free)
                    copy(act, QS[2 * j][0:64, :], P[0:64, b.i, :])
                    c = copy(act, QS[2 * j + 1][64:128, :], P[64:128, b.i, :])
                    if i == 0:
                        q_bank[u], got = yield from take_one(bank[5:7])
                        pe.wait(*got)
                    while q_bank[u] is None:
                        yield lambda: q_bank[u] is not None
                    pe.wait(s, got_in["idn"])
                    for t in range(4):
                        cc = 2 * (4 * i + t)
                        mm = matmul(P[:, q_bank[u].i, cc:cc + 2], x[:, 128 * t:128 * t + 128], BLK[:, 0:128:64], True, True)
                    xb.give(mm)
                    q_sums[u].append(mm)
                    if len(q_sums[u]) == 2:
                        start(q_scale(u), mm)
                    yield c
                    dve.wait(c, *free)
                    d = diff(dve, QS[2 * j][64:128, :], P[0:64, b.i, :], QS[2 * j][0:64, :])
                    q_ev[2 * j] = d
                    d = diff(dve, QS[2 * j + 1][0:64, :], P[64:128, b.i, :], QS[2 * j + 1][64:128, :])
                    q_ev[2 * j + 1] = d
                    b.give(d)
                return evac

            def q_scale(u):
                pq = P[:, q_bank[u].i, 0:16].rearrange("p (j t c) -> p t j c", j=2, t=4)
                w, r8 = SM[:, 32:36], SM[:, 36:40]
                ms, std, y, tmp = (QW[:, u, k, :] for k in range(4))
                dve.wait(*q_sums[u], norm.rt)
                a = [tt(dve, w, RT, RT, ALU.mult), ts(dve, r8, RT, 0.125, ALU.mult)] if u == 0 else []
                rt_read["dve"] = a[1] if a else rt_read["dve"]
                dve.wait(*a)
                qv = ms.rearrange("p (t j c) -> p t j c", t=4, c=2)
                a = tt(dve, qv, pq, w.unsqueeze(2).unsqueeze(3).to_broadcast([128, 4, 2, 2]), ALU.mult)
                q_bank[u].give(a)
                dve.wait(a)
                a = ts(dve, ms, ms, 1.0 / 64, ALU.mult, EPS, ALU.add)
                yield a
                act.wait(a)
                b = activ(std, ms, AF.Sqrt)
                yield b
                dve.wait(b)
                a = rsqrt_step(y, std, ms, tmp, a)
                dve.wait(a)
                h = slice(4 * u, 4 * u + 4)
                a = tt(dve, QSC[:, :, h], y.rearrange("p (t h) -> p t h", t=4),
                       r8.unsqueeze(2).to_broadcast([128, 4, 4]), ALU.mult)
                dve.wait(a)
                qsc_ev[u] = ts(dve, NQS[:, :, h], QSC[:, :, h], -1.0, ALU.mult)

            SC = [at(f"SC{g}", [128, T], F32, o_u + 16384 * g + 6144) for g in range(2)]
            KZ = at("KZ", [128, 608], F32R, o_a + 53 * KB)
            PCH = [at(f"PCH{g}", [128, T], F32R, o) for g, o in enumerate((CS_off, o_a + 56 * KB))]
            PCL = [at(f"PCL{g}", [128, T], F32R, o) for g, o in enumerate((CS_off + 2048, o_a + 58 * KB))]
            STC = at("STC", [128, 3, 32], F32, o_a)
            pct_ev, kz_ev, sc_read = [None, None], [None], [None, None]
            maskt_slot, maskt = Slot(semaphore("s_maskt")), [None]

            def cmp_keys():
                while kc_ev[0] is None or len(heads_done) < 4:
                    yield lambda: kc_ev[0] is not None and len(heads_done) == 4
                yield heads_done + kc_ev[0:1]
                pool.wait(*heads_done)
                one = ONES[:, 0:1].to_broadcast([128, 608])
                z = diff(pool, KZ[:], one, one)
                src = CG[0][:, 0, :].rearrange("p (g n) -> p g n", g=2)
                yield z
                act.wait(kc_ev[0], z)
                kv = KZ[:, 96:608].rearrange("p (g x n) -> p g x n", g=2, x=2)[:, :, :, 0:32]
                hi = copy(act, kv[:, :, 0, :], src)
                yield hi
                dve.wait(hi)
                kz_ev[0] = diff(dve, kv[:, :, 1, :], src, kv[:, :, 0, :])
                while (1, 0) not in ks_ev or (1, 1) not in ks_ev:
                    yield lambda: (1, 0) in ks_ev and (1, 1) in ks_ev
                got = yield from take(sq[0])
                got = got + ks_ev[(1, 0)] + ks_ev[(1, 1)]
                yield got
                sp.wait(*got)
                maskt[0] = dma(sp, maskt_slot, SQ[0][:], A["c_maskt"])

            def cmp_group(g):
                def ready():
                    return (len(q_ev) >= 4 * g + 4 and qsc_ev[g] is not None and gate_ev[0] is not None and None not in kc_ev
                            and kz_ev[0] is not None and maskt[0] is not None and s_order.n >= 1)
                while not ready():
                    yield ready
                heads = [q_ev[4 * g + i] for i in range(4)]
                yield heads + kz_ev
                b, got = yield from take_one([bank[5], bank[6]])
                yield pe
                pe.wait(*kz_ev, *heads, *got)
                for i in range(4):
                    for x in range(2):
                        c = 128 * (2 * g + x) + 96 - 32 * i
                        m = matmul(P[:, b.i, :], KZ[:, c:c + 128], QS[4 * g + i][:], i == 0 and x == 0, i == 3 and x == 1)
                yield m, maskt[0]
                dve.wait(m, maskt[0], *kc_ev)
                a = tt(dve, SC[g][:], P[:, b.i, :], SQ[0][:], ALU.add)
                b.give(a)
                if g == 1:
                    sq[0].give(a)
                yield a
                b, got = yield from take_one([bank[5], bank[6]])
                pe.wait(a, *got)
                for t in range(4):
                    m = transpose(P[:, b.i, 128 * t:128 * t + 128], SC[g][:, 128 * t:128 * t + 128], IDN)
                yield m
                pv = P[:, b.i, :].rearrange("p (t h n) -> p t h n", t=4, n=32)
                ec = SC[g][:].rearrange("p (t h n) -> p t h n", t=4, n=32)
                mx, sm, rc = (STC[:, i, 16 * g:16 * g + 16].rearrange("p (t h) -> p t h", t=4) for i in range(3))

                def over(v):
                    return v.unsqueeze(3).to_broadcast([128, 4, 4, 32])

                dve.wait(m)
                a = dve(lambda e: e.tensor_reduce(mx, pv, AX.X, ALU.max), 0.6)
                dve.wait(a)
                a = tt(dve, ec, pv, over(mx), ALU.subtract)
                b.give(a)
                yield a
                pool.wait(a, qsc_ev[g])
                a = tt(pool, ec, ec, over(QSC[:, :, 4 * g:4 * g + 4]), ALU.mult)
                yield a
                act.wait(a)
                x = activ(SC[g][:], SC[g][:], AF.Exp)
                yield x
                dve.wait(x)
                a = dve(lambda e: e.tensor_reduce(sm, ec, AX.X, ALU.add), 0.6)
                dve.wait(a)
                a = recip(rc, sm)
                dve.wait(a, gate_ev[0])
                a = tt(dve, rc, rc, GATE[:, :, 12 * g:12 * g + 12:3], ALU.mult)
                yield a
                pool.wait(a, x)
                a = tt(pool, ec, ec, over(rc), ALU.mult)
                pool.wait(a, got_in["idn"])
                a = tt(pool, ec, ec, M01.rearrange("p (t n) -> p t n", t=4).unsqueeze(2).to_broadcast([128, 4, 4, 32]), ALU.mult)
                yield a
                b, got = yield from take_one([bank[5], bank[6]])
                pe.wait(a, *got)
                for t in range(4):
                    m = transpose(P[:, b.i, 128 * t:128 * t + 128], SC[g][:, 128 * t:128 * t + 128], IDN)
                sc_read[g] = m
                yield m
                if g == 0:
                    free = hm_last
                else:
                    free = yield from take(*EV.all)
                    for e in EV.all[2:]:
                        e.give(*free)
                act.wait(m, *free)
                hi = copy(act, PCH[g][:], P[:, b.i, :])
                yield hi
                dve.wait(hi, *free)
                pct_ev[g] = diff(dve, PCL[g][:], P[:, b.i, :], PCH[g][:])
                b.give(pct_ev[g])

            EARLY = 2
            PFS = [Ring([at(f"PF{e}{i}", [128, 1280], F32, o) for i, o in enumerate(os)])
                   for e, os in enumerate(((o_u,), (o_h, o_h + 5 * KB, o_a + 48 * KB)))]
            PFS[1].all[2].free = None
            PTS = [Ring([(at(f"PH{e}{i}", [128, 1280], F32R, a), at(f"PL{e}{i}", [128, 1280], F32R, b))
                         for i, (a, b) in enumerate(os)])
                   for e, os in enumerate((((o_u + 16384, o_a + 48 * KB),),
                                           ((o_h + 10 * KB, o_h + 20 * KB), (o_h + 15 * KB, o_h + 25 * KB))))]
            ST = at("ST", [128, 4, 16], F32, o_a + 69 * KB)
            STR = Ring([ST[:, i, :] for i in range(4)])
            s_order, t_order, v_order = Order(), Order(), Order()

            def mix_free(kt):
                got = []
                if kt == 0:
                    got = yield from take(*PFS[0].all, *PTS[0].all)
                if kt == 3:
                    got = sc_read
                return got

            def item(n):
                h, br = n // 2, n % 2
                g = h // 4
                hh, ll = KS[br][g]
                q = QS[h]
                yield from s_order.turn(n)
                late = int(n >= EARLY)

                def ready():
                    return (h in q_ev and len(ks_ev) == 4 and qsc_ev[g] is not None and gate_ev[0] is not None
                            and (h_over or not late))
                while not ready():
                    yield ready
                free = h_over if late else heads_done + [s for k in ks_ev.values() for s in k]
                pf, pf_got = yield from PFS[late].next()
                st, st_got = yield from STR.next()
                pf_got = pf_got + free
                scaled_ev = []
                yield Late([q_ev[h]] + ks_ev[(br, g)])

                def soft(bs, ts_, m):
                    dve.wait(qsc_ev[g])
                    r, x, a = yield from row_softmax(bs, ts_, st.buf, 0, NQS[:, :, h], pf.buf, m,
                                                     pf_got, st_got)
                    yield a
                    pool.wait(a, gate_ev[0])
                    a = tt(pool, st.buf[:, 8:12][:, r], st.buf[:, 8:12][:, r], GATE[:, r, 3 * h + 1 + br], ALU.mult)
                    yield a
                    for t in ts_:
                        c = scol(t)
                        p = pf.buf[:, c[0]:c[1]]
                        lane, scale = scale_rows(p, p, st.buf[:, 8 + t:9 + t])
                        lane.wait(a, x)
                        scaled_ev.append(scale())

                for bs, ts_ in CHUNKS:
                    got = yield from take(*(bank[b] for b in bs))
                    pe.wait(q_ev[h], *ks_ev[(br, g)], *got)
                    for t in ts_:
                        o = spot(t)
                        k = slice(0, 128 * (t + 1))
                        qt = q[:, 128 * t:128 * t + 128]
                        matmul(o, qt, hh[:, k], True, False)
                        m = matmul(o, qt, ll[:, k], False, True)
                    start(soft(bs, ts_, m), m)
                s_order.done()
                while len(scaled_ev) < 4:
                    yield lambda: len(scaled_ev) == 4
                yield Late(scaled_ev)
                st.give(*scaled_ev)
                yield from t_order.turn(n)
                pt, pt_got = yield from PTS[late].next()
                turned = yield from turn(pf, scaled_ev, pt, pt_got + free, t_order)
                ph, pl = pt.buf
                yield from v_order.turn(n)
                o_got = []
                if br == 0:
                    while None in vn_ev:
                        yield lambda: None not in vn_ev
                    yield Late(vn_ev)
                    o_got = yield from take(bank[7])
                elif pct_ev[g] is None:
                    while pct_ev[g] is None:
                        yield lambda: pct_ev[g] is not None
                    yield pct_ev[g]
                m = values(lambda j: VN[:, j, 2 * br + g, :], ph, pl, turned + vn_ev + o_got, br == 0, False)
                pt.give(m)
                if n == EARLY - 1:
                    PFS[1].all[2].give(m)
                if br == 1:
                    pe.wait(pct_ev[g], kc_ev[1])
                    r = slice(32 * (h % 4), 32 * (h % 4) + 32)
                    matmul(P[:, 7, :], VCS[r, g, :], PCH[g][r, :], False, False)
                    m = matmul(P[:, 7, :], VCS[r, g, :], PCL[g][r, :], False, True)
                    yield m
                    c_read[0] = m
                    yield from fold(h, m, TM.all[0], TM.all[1], mix_free)
                v_order.done()
                if n == 15:
                    ring.extend(bank[2:8])

            h_over, c_read = [], [None]

            def add_early(i, b, m):
                xb, got = yield from take_one(EV.all[2:])
                act.wait(m, *got)
                c = copy(act, xb.buf[:], P[:, b.i, :])
                b.give(c)
                yield c
                pool.wait(c, xt_ev[i])
                xt_ev[i] = tt(pool, XT[:, i, :], XT[:, i, :], xb.buf[:], ALU.add)
                xb.give(xt_ev[i])

            ring = [bank[0], bank[1]]

            def early(u, k0, o0):
                return unit(u, U, ring, lambda i, b, m: add_early(o0 + i, b, m), k0=k0)

            def main(name, evac):
                return unit(m1[name], H, ring, evac)

            products = {"cmp": lambda: main("cmp", ev_cmp), "ksw": lambda: main("ksw", ev_ksw),
                        "vsw": lambda: vunit(m1["vsw"], ring, ev_vsw, 1)}
            for i in range(4):
                products[f"hqf{i}"] = lambda i=i: main(f"hqf{i}", ev_hqf(i))
            for i in range(2):
                products[f"hi{i}"] = lambda i=i: vunit(m1[f"hi{i}"], ring, ev_hi(i))
                products[f"hg{i}"] = lambda i=i: main(f"hg{i}", ev_hg(i))
                products[f"q{i}"] = lambda i=i: main(f"q{i}", ev_q(i))
            yield from unit(m1["hqf0"], H, bank[2:6], ev_hqf(0), kouter=True)
            pe.wait(got_in["idn"])
            for task in [small_things(), lambdas(), compress(), cmp_keys()] + [hgrn(h) for h in range(4)] + \
                    [cmp_group(g) for g in range(2)] + [item(n) for n in range(16)]:
                start(task)
            for name in ORDER1[1:]:
                yield from products[name]()
            h_over.extend([H.used[kt] for kt in range(KT)])
            for i in range(2):
                yield from early(m1[f"wh{i}"], 4, 4 * i)
            start(rotary_tables(lambda: v_order.n >= 8 and c_read))
            for i in range(2):
                yield from out_tiles(m1[f"wn{i}"], 0, 4 * i, ring, None)
            yield from out_tiles(m1["wn2"], 2, 0, ring, None)
            new_norm()
            yield from out_tiles(m1["wn3"], 3, 0, ring, 8)
        csslot, cs_in, hm_last = Slot(semaphore("s_cs")), [None], [None]

        def rotary_tables(free):
            while not free():
                yield free
            yield free()
            sp.wait(*free())
            for i in range(2):
                cs_in[0] = dma(sp, csslot, CS[:, i, :], A["c_rope"][i])

        def plan_mixer2(l):
            got = {}
            w, wo = A["w_in_2"][l], A["w_o_2"][l]
            for part, c in (("d", 1536), ("s", 0)):
                for name in ("qk0", "v0", "qk1", "qk2", "qk3", "v1"):
                    i = int(name[-1])
                    if name[0] == "q":
                        src = [w[:, c + 128 * i:c + 128 * i + 128], w[:, c + 512 + 128 * i:c + 512 + 128 * i + 128]]
                    else:
                        src = [w[:, c + 1024 + 256 * i:c + 1280 + 256 * i]]
                    got[part + name] = plan(src, KT)
            for i in range(2):
                got[f"od{i}"] = plan([wo[512:1024, 512 * i:512 * i + 512]], 4)
            for i in range(2):
                got[f"os{i}"] = plan([wo[0:384, 512 * i:512 * i + 512]], 3)
            got["os2"] = plan([wo[384:512, :]], 1)
            return got

        def mixer2(l, M):
            init = 0.8 - 0.6 * float(np.exp(-0.3 * l))

            def nm(x):
                return f"{x}_{l}"

            o = o_a + 6 * KB
            u_at = [o_u + 2048 * i for i in range(8)] + [o_u + 16384 + 2048 * i for i in range(8)]
            sets = [[o + 2 * KB * i for i in range(5)], [o + (10 + 2 * i) * KB for i in range(5)],
                    [u_at[k] for k in (12, 13, 14, 15, 8)]]
            QSET = [[at(nm(f"QT{i}{x}"), [128, T], F32R, s[x]) for x in range(2)] for i, s in enumerate(sets)]
            KSET = [[at(nm(f"KT{i}{x}"), [128, T], F32R, s[2 + x]) for x in range(2)] for i, s in enumerate(sets)]
            KLO = [at(nm(f"KL{i}"), [128, T], F32R, s[4]) for i, s in enumerate(sets)]
            SET = {"d": (0, 1, 2, 0), "s": (1, 0, 1, 0)}
            o = o_a + 26 * KB
            VSET = [at(nm(f"VS{i}"), [128, 4, 512], F32R, o + 8 * KB * i) for i in range(2)]
            o = o_a + 42 * KB
            E0 = Ring([at(nm(f"E0{i}"), [128, 1280], F32, o + 5 * KB * i) for i in range(2)])
            E1 = Ring([at(nm("E1"), [128, 1288], F32, o + 10 * KB)])
            o += 32
            PT = Ring([(at(nm("PH"), [128, 1280], F32R, o + 15 * KB), at(nm("PL"), [128, 1280], F32R, o + 20 * KB))])
            TMD = Ring([at(nm("TMD"), [128, T], F32, o + 25 * KB)])
            ST = at(nm("ST"), [128, 4, 16], F32, o + 27 * KB)
            STR = Ring([ST[:, i, :] for i in range(4)])
            EV = Ring([at(nm(f"EV{i}"), [128, T], F32, u_at[k]) for i, k in enumerate((2, 10, 3, 11))])
            XO = [at(nm(f"XO{h}"), [128, T], F32, u_at[4 + h]) for h in range(4)]
            DN = at(nm("DN"), [128, 4, 16], F32, u_at[9])
            dn = Hold()
            dn.free = None
            RO = Ring([at(nm(f"RO{i}"), [128, T], F32, o_a + 2 * KB * i) for i in range(3)] + [at(nm("RO3"), [128, T], F32, u_at[1])])

            qk_set, v_set = [Hold() for _ in sets], [Hold(), Hold()]
            set_got, qk_ready, v_ready = {}, {}, {}
            U.ev = {}
            norm = norms[-1]

            def q_halves(dst, src, ev, got):
                yield ev
                act.wait(ev, *got)
                for x in range(2):
                    own = slice(64 * x, 64 * x + 64)
                    c = copy(act, dst[x][own, :], src[own, :])
                yield c
                dve.wait(ev, c, *got)
                for x in range(2):
                    own, other = slice(64 * x, 64 * x + 64), slice(64 - 64 * x, 128 - 64 * x)
                    d = diff(dve, dst[x][other, :], src[own, :], dst[x][own, :])
                return d

            def k_halves(dst, lo, src, ev, got):
                yield ev
                act.wait(ev, *got)
                for x in range(2):
                    own = slice(64 * x, 64 * x + 64)
                    c = copy(act, dst[x][own, :], src[own, :])
                yield c
                dve.wait(ev, c, *got)
                for x in range(2):
                    own, other = slice(64 * x, 64 * x + 64), slice(64 - 64 * x, 128 - 64 * x)
                    diff(dve, lo[own, :], src[own, :], dst[x][own, :])
                    d = copy(dve, dst[x][other, :], dst[x][own, :])
                return d

            def set_taken(key, hold):
                if key not in set_got:
                    set_got[key] = None
                    set_got[key] = yield from take(hold)
                while set_got[key] is None:
                    yield lambda: set_got[key] is not None
                return set_got[key]

            def halves(i, key, n, x, a, got):
                if i == 0:
                    d = yield from q_halves(QSET[n], x, a, got)
                else:
                    d = yield from k_halves(KSET[n], KLO[n], x, a, got)
                qk_ready.setdefault(key, []).append(d)
                return d

            def ev_sqk(p):
                def evac(i, b, m):
                    yield from has_rb(norm)
                    n = SET["s"][p]
                    got = yield from set_taken(("s", p), qk_set[n])
                    xb, xg = yield from EV.next()
                    x = xb.buf[:]
                    dve.wait(m, norm.rb, *xg)
                    a = stt(dve, x, P[:, b.i, :], 0.125 if i == 0 else 1.0, RB[:], ALU.mult, ALU.mult)
                    rb_read["dve"] = a
                    b.give(a)
                    d = yield from halves(i, ("s", p), n, x, a, got)
                    xb.give(d)
                return evac

            def ev_v(part, p):
                def evac(tp, b, m):
                    yield from has_rt(norm)
                    got = yield from set_taken((part + "v", p), v_set[p])
                    vs = VSET[p]
                    act.wait(m, norm.rt, *got)
                    dv = []
                    for q in range(2):
                        t = 2 * tp + q
                        src = P[:, b.i, 256 * q:256 * q + 256]
                        if part == "s":
                            src = src.rearrange("p (n d) -> p n d", n=4)
                            dst = vs[:, t, :].rearrange("p (n x d) -> p n x d", n=4, x=2)
                            hi, lo = dst[:, :, 0, :], dst[:, :, 1, :]
                        else:
                            hi, lo = vs[:, t, 0:256], vs[:, t, 256:512]
                        c = activ(hi, src, AF.Identity, scale=RT[:, t:t + 1])
                        dv.append((lo, src, RT[:, t:t + 1], hi))
                    rt_read["act"] = c
                    yield c
                    dve.wait(m, c, norm.rt, *got)
                    for lo, src, r, hi in dv:
                        d = stt(dve, lo, src, r, hi, ALU.mult, ALU.subtract)
                    rt_read["dve"] = d
                    b.give(d)
                    v_ready.setdefault((part, p), []).append(d)
                return evac

            ro = RO.all
            rslot = [Slot(semaphore(nm(f"s_ro{i}"))) for i in range(4)]

            def ev_dqk(h):
                def evac(i, b, m):
                    yield from has_rb(norm)
                    n = SET["d"][h]
                    got = yield from set_taken(("d", h), qk_set[n])
                    rb, rrb, rg = yield from RO.pair()
                    r, rr = rb.buf, rrb.buf
                    dve.wait(m, norm.rb, *rg)
                    a = stt(dve, r[:], P[:, b.i, :], 0.125 if i == 0 else 1.0, RB[:], ALU.mult, ALU.mult)
                    rb_read["dve"] = a
                    b.give(a)
                    yield a
                    sp.wait(a, *rg)
                    for k in range(4):
                        src = 32 * (k ^ 1)
                        s = dma(sp, rslot[rb.i], rr[32 * k:32 * k + 32, :], r[src:src + 32, :])
                    yield s
                    pool.wait(s, cs_in[0])
                    w = tt(pool, rr[:], rr[:], CS[:, 1, :], ALU.mult)
                    dve.wait(s, cs_in[0])
                    c = tt(dve, r[:], r[:], CS[:, 0, :], ALU.mult)
                    yield w
                    dve.wait(c, w)
                    a = tt(dve, r[:], r[:], rr[:], ALU.add)
                    rrb.give(a)
                    d = yield from halves(i, ("d", h), n, r, a, got)
                    rb.give(d)
                return evac

            s_order, t_order, v_order = Order(), Order(), Order()

            def scores2(ts_, n, x, ready, got):
                own = slice(64 * x, 64 * x + 64)
                q, hh, lo = QSET[n][x], KSET[n][x], KLO[n]
                pe.wait(*ready, *got)
                for t in ts_:
                    o = spot(t)
                    k = slice(0, 128 * (t + 1))
                    matmul(o, q[:, 128 * t:128 * t + 128], hh[:, k], True, False)
                    m = matmul(o, q[own, 128 * t:128 * t + 128], lo[own, k], False, True)
                return m

            flat = P[:, 2:5, :].rearrange("p b c -> p (b c)")[:, 0:1280]

            def sb_head(h):
                p, x, n = h // 2, h % 2, SET["s"][h // 2]
                yield from s_order.turn(4 + h)
                while len(qk_ready.get(("s", p), [])) < 2:
                    yield lambda: len(qk_ready.get(("s", p), [])) == 2
                yield Late(qk_ready[("s", p)])
                e0, got0 = yield from E0.next()
                for bs, ts_ in CHUNKS:
                    got = yield from take(*(bank[b] for b in bs))
                    m = scores2(ts_, n, x, qk_ready[("s", p)], got)
                if x == 1:
                    qk_set[n].give(m)
                s_order.done()
                yield m
                act.wait(m, *got0)
                bt = activ(e0.buf[:], flat, AF.Sigmoid)
                e1, got1 = yield from E1.next()
                act.wait(*got1)
                kp = activ(e1.buf[:, 0:1280], flat, AF.Sigmoid, scale=-1.0)
                for b in (2, 3, 4):
                    bank[b].give(kp)
                yield kp
                pool.wait(kp)
                zero(pool, e1.buf[:, 512:1025:512])
                z = zero(pool, e1.buf[:, 896:1281:384])

                def scan(c0, c1, at_, op, first):
                    v = e1.buf[:, slice(c1 - 1, c0 - 1 if c0 else None, -1)]
                    return dve(lambda e: e.tensor_tensor_scan(v, v, at_, first, ALU.mult, op), vcost(dve, c1 - c0))

                dve.wait(kp, got_in["idn"])
                for t in range(4):
                    c1 = scol(t)[1]
                    n = 127 if t == 0 else 128
                    s = scan(c1 - n, c1, IDN[:, 127:127 - n if n < 128 else None:-1], ALU.max, 0.0)
                dve.wait(s)
                for t in range(1, 4):
                    c0, c1 = scol(t)
                    c0, c1 = c0 + 1, c1 - 128
                    s = scan(c0, c1, ONES[:, 0:1].to_broadcast([128, c1 - c0]), ALU.mult, e1.buf[:, c1:c1 + 1])
                yield s
                pool.wait(s, bt, z)
                w = tt(pool, e0.buf[:], e0.buf[:], e1.buf[:, 1:1281], ALU.mult)
                e1.give(w)
                yield w
                yield from t_order.turn(4 + h)
                pt, pt_got = yield from PT.next()
                turned = yield from turn(e0, [w], pt, pt_got, t_order)
                ph, pl = pt.buf
                yield from v_order.turn(4 + h)
                g = h // 4
                while len(v_ready.get(("s", g), [])) < 2:
                    yield lambda: len(v_ready.get(("s", g), [])) == 2
                yield Late(v_ready[("s", g)])
                got = yield from take(bank[7])
                c = 128 * (h % 4)
                m = values(lambda j: VSET[g][:, j, c:c + 128], ph, pl, turned + v_ready[("s", g)] + got, True, True)
                pt.give(m)
                v_order.done()
                yield m
                yield from fold(h, m, ro[0], ro[1], mix_free)
                if h == 7:
                    ring.extend(bank[2:8])

            def mix_free(kt):
                if kt >= 2:
                    while len(qk_ready.get(("s", 3), [])) < 2:
                        yield lambda: len(qk_ready.get(("s", 3), [])) == 2
                got = []
                for h in {0: [], 1: [ro[3], dn], 2: EV.all[0:2], 3: EV.all[2:4]}[kt]:
                    got += yield from take(h)
                return got

            sln = SM[:, 44 + l:45 + l]

            def df_head(h):
                n, g = SET["d"][h], h // 2
                o_ = h
                yield from s_order.turn(o_)
                while len(qk_ready.get(("d", h), [])) < 2:
                    yield lambda: len(qk_ready.get(("d", h), [])) == 2
                yield Late(qk_ready[("d", h)])
                es, sts, done = [], [], [[], []]

                def soft(mp, bs, ts_, m, got, st_got):
                    r, x, a = yield from row_softmax(bs, ts_, sts[mp].buf, 1, -1.0, es[mp].buf, m, got, st_got)
                    if mp == 1:
                        st = sts[1].buf
                        dve.wait(a, got_in["lambda"])
                        a = ts(dve, st[:, 8:12][:, r], st[:, 8:12][:, r], LAM[:, l:l + 1], ALU.mult)
                        yield a
                        for t in ts_:
                            c = scol(t)
                            p = es[1].buf[:, c[0]:c[1]]
                            lane, scale = scale_rows(p, p, st[:, 8 + t:9 + t])
                            lane.wait(a, x)
                            done[1].append(scale())
                    else:
                        done[0].append(a)

                for mp in range(2):
                    e, got = yield from (E0, E1)[mp].next()
                    st, st_got = yield from STR.next()
                    es.append(e)
                    sts.append(st)
                    for bs, ts_ in CHUNKS:
                        bg = yield from take(*(bank[b] for b in bs))
                        m = scores2(ts_, n, mp, qk_ready[("d", h)], bg)
                        start(soft(mp, bs, ts_, m, got, st_got), m)
                qk_set[n].give(m)
                s_order.done()
                while len(done[0]) < 2 or len(done[1]) < 4:
                    yield lambda: len(done[0]) == 2 and len(done[1]) == 4
                yield done[0] + done[1]
                dve.wait(*done[0], *done[1])
                for t in (3, 2, 0, 1):
                    c = scol(t)
                    p = es[0].buf[:, c[0]:c[1]]
                    a = stt(dve, p, p, sts[0].buf[:, 8 + t:9 + t], es[1].buf[:, c[0]:c[1]], ALU.mult, ALU.subtract)
                es[1].give(a)
                sts[0].give(a)
                sts[1].give(a)
                yield a
                yield from t_order.turn(o_)
                pt, pt_got = yield from PT.next()
                turned = yield from turn(es[0], [a], pt, pt_got, t_order)
                ph, pl = pt.buf
                yield from v_order.turn(o_)
                while len(v_ready.get(("d", g), [])) < 2:
                    yield lambda: len(v_ready.get(("d", g), [])) == 2
                yield Late(v_ready[("d", g)])
                v = VSET[g][:].rearrange("p j (x c) -> p j x c", x=2)[:, :, :, 128 * (h % 2):128 * (h % 2) + 128]
                xo = XO[h][:].rearrange("p (t d) -> p t d", t=4)
                for t0, t1 in ((0, 3), (1, 2)):
                    got = yield from take(bank[7])
                    pe.wait(*got, *turned, *v_ready[("d", g)])
                    o = P[:, 7, :].rearrange("p (q x d) -> p q x d", q=2, x=2)
                    for q, t in enumerate((t0, t1)):
                        for j in range(t + 1):
                            k = slice(trow(j)[0] + 128 * (t - j), trow(j)[0] + 128 * (t - j) + 128)
                            matmul(o[:, q], ph[:, k], v[:, j], q == j == 0, False)
                            m = matmul(o[:, q, 0, :], pl[:, k], v[:, j, 0, :], False, q == 1 and j == t)
                    if t0 == 1:
                        pt.give(m)
                        if h % 2 == 1:
                            v_set[g].give(m)
                        v_order.done()
                    yield m
                    dve.wait(m)
                    x = o_ev[h] = dve(lambda e, q=xo[:, t0:t1 + 1:t1 - t0, :], o=o: e.tensor_reduce(
                        q, o.rearrange("p q x d -> p q d x"), AX.X, ALU.add), vcost(dve, 512))
                    bank[7].give(x)
                yield x
                tb, got = yield from TMD.next()
                act.wait(x, *got)
                for t in range(4):
                    s = activ(tb.buf[:, 128 * t:128 * t + 128], xo[:, t, :], AF.Square, accum=DN[:, 0, 4 * h + t:4 * h + t + 1])
                tb.give(s)
                sums.append(s)
                if len(sums) == 4:
                    start(df_norm(), s)

            o_ev, sums = {}, []

            def df_norm():
                dve.wait(*sums)
                ms = ts(dve, DN[:, 0, :], DN[:, 0, :], 1.0 / 128, ALU.mult, EPS, ALU.add)
                act.wait(ms)
                s = activ(DN[:, 1, :], DN[:, 0, :], AF.Sqrt)
                yield s
                dve.wait(s)
                r = rsqrt_step(DN[:, 2, :], DN[:, 1, :], DN[:, 0, :], DN[:, 3, :], ms)
                for h in range(4):
                    tb, got = yield from TMD.next()
                    pool.wait(r, o_ev[h], *got)
                    d = tt(pool, tb.buf[:].rearrange("p (t d) -> p t d", t=4), XO[h][:].rearrange("p (t d) -> p t d", t=4),
                           DN[:, 2, 4 * h:4 * h + 4].unsqueeze(2).to_broadcast([128, 4, 128]), ALU.mult)
                    yield d
                    b, got = yield from take_one(bank[5:7])
                    pe.wait(d, *got)
                    for t in range(4):
                        m = transpose(P[:, b.i, 128 * t:128 * t + 128], tb.buf[:, 128 * t:128 * t + 128], IDN)
                    yield m
                    tb.give(m)
                    act.wait(m, sln_ev[0])
                    hi = activ(UH[:, 4 + h, :], P[:, b.i, :], AF.Identity, scale=sln)
                    yield hi
                    dve.wait(hi, sln_ev[0])
                    U.ev[4 + h] = stt(dve, UL[:, 4 + h, :], P[:, b.i, :], sln, UH[:, 4 + h, :], ALU.mult, ALU.subtract)
                    b.give(U.ev[4 + h])
                dn.give(d)

            sln_ev = [None]

            def scales():
                yield None
                sln_ev[0] = ts(dve, sln, GT[:, 53 + l:54 + l], 1.0 - init, ALU.mult)

            ring = [bank[0], bank[1]]
            start(scales())
            for h in range(4):
                start(df_head(h))
            for h in range(8):
                start(sb_head(h))
            for part, ev in (("d", ev_dqk), ("s", ev_sqk)):
                if part == "d":
                    yield from unit(M["dqk0"], H, bank[2:5], ev_dqk(0), kouter=True)
                else:
                    yield from unit(M["sqk0"], H, ring, ev_sqk(0))
                yield from vunit(M[part + "v0"], ring, ev_v(part, 0))
                for i in (1, 2, 3):
                    yield from unit(M[f"{part}qk{i}"], H, ring, ev(i))
                yield from vunit(M[part + "v1"], ring, ev_v(part, 1))
            for i in range(2):
                yield from out_tiles(M[f"od{i}"], 4, 4 * i, ring, None)
            for i in range(2):
                yield from out_tiles(M[f"os{i}"], 0, 4 * i, ring, None)
            new_norm()
            yield from out_tiles(M["os2"], 3, 0, ring, 32 + 8 * l)

        def plan_ffn1():
            w, wd = A["w_gate_up"][0], A["w_down"][0]
            got = []
            for n, j0 in ((8, 0), (8, 8), (6, 16)):
                for j in range(j0, j0 + n, 2):
                    got.append(plan([w[:, 128 * j:128 * j + 256]], KT))
                    got.append(plan([w[:, D_FF + 128 * j:D_FF + 128 * j + 256]], KT))
                for o in range(0, D, 256):
                    got.append(plan([wd[128 * j0:128 * (j0 + n), o:o + 256]], n))
            return got

        def plan_ffn2(l):
            w, wd = A["w_ff1_2"][l], A["w_ff2_2"][l]
            got = []
            for j0 in range(0, 32, 8):
                for j in range(j0, j0 + 8, 2):
                    got.append(plan([w[:, 128 * j:128 * j + 256]], KT))
                for o in range(0, D, 256):
                    got.append(plan([wd[128 * j0:128 * (j0 + 8), o:o + 256]], 8))
            return got

        m1, f1 = plan_mixer1(), plan_ffn1()
        m20, f20 = plan_mixer2(0), plan_ffn2(0)
        m21, f21 = plan_mixer2(1), plan_ffn2(1)

        def whole():
            new_norm()
            got_in["gt"] = dma(sp, gslot, GT[:], A["p_vec"])
            pump()
            start(opening())
            start(splitter())
            yield from mixer1(m1)
            yield from ffn("1", f1, (8, 8, 6), True, 16)
            yield from mixer2(0, m20)
            yield from ffn("2", f20, (8, 8, 8, 8), False, 24)
            yield from mixer2(1, m21)
            yield from ffn_last(f21)

        start(whole())
        tasks.run()

        for lane in lanes:
            lane.number()
        block = ctx.enter_context(nc.Block())

        @block.tensor
        def _(e):
            pe.play(e)

        @block.scalar
        def _(e):
            act.play(e)

        @block.vector
        def _(e):
            dve.play(e)

        @block.gpsimd
        def _(e):
            pool.play(e)

        @block.sync
        def _(e):
            sp.play(e)


def constants(inputs):
    i = np.arange(128)
    t, s = i[:, None], i[None, :]
    tok = 128 * (np.arange(128) // 32)[None, :] + t
    n = (np.arange(128) % 32)[None, :]
    seen = (16 * n + 31 <= tok) & (n < 31)
    eye = np.eye(128, dtype=np.float32)
    idn = np.concatenate([eye, (t // 64 == s // 64).astype(np.float32), seen.astype(np.float32)], axis=1)
    mask = np.stack([np.where(s <= t, 0, NEG), np.where(s // 64 <= t // 64, 0, NEG)], axis=1).astype(np.float32)
    blk, tok = (i % 32)[:, None], np.arange(T)[None, :]
    maskt = np.where((16 * blk + 31 <= tok) & (blk < 31), 0, NEG).astype(np.float32)
    d = np.arange(0, 64, 2, dtype=np.float32)
    inv = (np.float32(1.0) / (np.float32(10000.0) ** (d / np.float32(64)))).astype(np.float32)
    ang = np.arange(T, dtype=np.float32)[None, :] * inv[i % 32][:, None]
    rope = np.stack([np.cos(ang), np.where(t % 64 < 32, -1, 1) * np.sin(ang)]).astype(np.float32)
    hg = np.zeros((128, 6, 128), np.float32)
    hg[:, 0, :] = eye
    for n, h in enumerate((1, 2, 4, 8, 16)):
        hg[:, n + 1, :] = (t // (2 * h) == s // (2 * h)) & (t // h % 2 == 0) & (s // h % 2 == 1)

    def vec(name):
        return np.asarray(inputs[name])

    rows = [vec(n).reshape(-1, 128) for n in ("norm_mix", "norm_ffn", "attn_norm_2", "mlp_norm_2")]
    rows += [np.concatenate([r, r], axis=1) for r in (vec("q_norm"), vec("k_norm")[0])]
    rows += [vec("hgrn_o_norm"), vec("subln_norm_2"), vec("hgrn_lb_logits").reshape(8, 128)]
    rows += [np.zeros((1, 128), np.float32)]
    rows += [np.concatenate([r, r], axis=1) for r in (vec("cmp_pos_k")[0], vec("cmp_pos_v")[0])]
    vecs = np.ascontiguousarray(np.concatenate(rows, axis=0).T)
    lam = np.concatenate([vec(n).reshape(1, 128) for n in ("lam_q1_2", "lam_k1_2", "lam_q2_2", "lam_k2_2")], axis=1)[0]
    return {"c_rope": rope, "c_hg": hg, "c_idn": idn, "c_mask": mask, "c_maskt": maskt, "p_vec": vecs, "p_lam": lam,
            "p_xt": np.ascontiguousarray(np.asarray(inputs["x"])[0].T)}


_INS = ["x", "norm_mix", "w_in", "q_norm", "k_norm", "cmp_pos_k", "cmp_pos_v", "cmp_k_w1", "cmp_k_w2", "cmp_v_w1",
        "cmp_v_w2", "hgrn_lb_logits", "hgrn_o_norm", "w_out", "norm_ffn", "w_gate_up", "w_down", "w_in_2", "w_o_2",
        "attn_norm_2", "subln_norm_2", "lam_q1_2", "lam_k1_2", "lam_q2_2", "lam_k2_2", "mlp_norm_2", "w_ff1_2",
        "w_ff2_2", "final_norm_2"]
_OUTS = [((1, 512, 1024), "float32")]


def kernel(**inputs):
    import numpy as _np
    import concourse.bacc as _bacc
    from concourse import mybir as _mybir
    from concourse.bass_utils import run_bass_kernel_spmd as _run

    nc = _bacc.Bacc("TRN2", target_bir_lowering=False, num_devices=1)
    given = {name: inputs[name] for name in _INS}
    given.update(constants(inputs))
    arrays, aps = {}, {}
    for name, value in given.items():
        a = _np.ascontiguousarray(value)
        arrays[f"in_{name}_dram"] = a
        aps[name] = nc.dram_tensor(f"in_{name}_dram", a.shape, _mybir.dt.from_np(a.dtype), kind="ExternalInput").ap()
    shape, dtype = _OUTS[0]
    out = nc.dram_tensor("out_0_dram", shape, _mybir.dt.from_np(_np.dtype(dtype)), kind="ExternalOutput").ap()
    program(nc, aps, out)
    r = _run(nc, [arrays], core_ids=[0])
    return r.results[0]["out_0_dram"]
```
